# Optimizing a Trainium2 kernel written in Bass

```python
import math
import jax, jax.numpy as jnp
from jax import lax
import numpy as np

D_MODEL = 1024
BATCH = 1
SEQ = 512
DEPTH = 1

CHUNK = 64
BAND_PREV = 8
BAND = (BAND_PREV + 1) * CHUNK
REL_CLIP = 256
N_REL = REL_CLIP + CHUNK

W_A = D_MODEL // 2
HEAD_A = 64
H_A = W_A // HEAD_A
W_B = D_MODEL // 2
HEAD_B = 64
H_B = W_B // HEAD_B
DECAY_LORA = 64
A_LORA = 64
GATE_LORA = 128
D_FF = 4 * D_MODEL

ATT_COLS = 3 * W_A
RWKV_COLS = 3 * W_B + DECAY_LORA + A_LORA + GATE_LORA
GATE_COLS = 2 * D_MODEL
IN_COLS = ATT_COLS + RWKV_COLS + GATE_COLS

RMS_EPS = 1e-6
GN_EPS = HEAD_B * 1e-5
NEG_INF = -1e30


def rms_norm(x, g):
    xf = x.astype(jnp.float32)
    y = xf * lax.rsqrt(jnp.mean(xf * xf, axis=-1, keepdims=True) + RMS_EPS)
    return (y * g.astype(jnp.float32)).astype(x.dtype)

def chunk_band_attention(q, k, v, rel_bias):
    b, s, h, d = q.shape
    nc = s // CHUNK
    qc = q.reshape(b, nc, CHUNK, h, d)
    pad = ((0, 0), (BAND_PREV * CHUNK, 0), (0, 0), (0, 0))
    kp = jnp.pad(k, pad).reshape(b, nc + BAND_PREV, CHUNK, h, d)
    vp = jnp.pad(v, pad).reshape(b, nc + BAND_PREV, CHUNK, h, d)
    kb = jnp.concatenate([kp[:, o:o + nc] for o in range(BAND_PREV + 1)], axis=2)
    vb = jnp.concatenate([vp[:, o:o + nc] for o in range(BAND_PREV + 1)], axis=2)
    scores = jnp.einsum('bnqhd,bnkhd->bnhqk', qc, kb).astype(jnp.float32) * (d ** -0.5)
    qi = jnp.arange(CHUNK)[:, None]
    kj = jnp.arange(BAND)[None, :]
    dist = qi + BAND_PREV * CHUNK - kj
    idx = jnp.clip(dist, -(CHUNK - 1), REL_CLIP) + (CHUNK - 1)
    bias = rel_bias.astype(jnp.float32)[:, idx]
    valid = (jnp.arange(nc)[:, None] - BAND_PREV + kj // CHUNK) >= 0
    scores = jnp.where(valid[None, :, None, None, :], scores + bias[None, None], NEG_INF)
    p = jax.nn.softmax(scores, axis=-1)
    out = jnp.einsum('bnhqk,bnkhd->bnqhd', p.astype(vb.dtype), vb)
    return out.reshape(b, s, h * d)

def rwkv7_time_mix(p, shift_mu, w0, w2, a0, a2, g2, k_k, k_a, r_k, ln_x_w, ln_x_b):
    b, s, _ = p.shape
    prev = jnp.pad(p, ((0, 0), (1, 0), (0, 0)))[:, :-1]
    p = p + (prev - p) * shift_mu
    splits = [W_B, 2 * W_B, 3 * W_B, 3 * W_B + DECAY_LORA, 3 * W_B + DECAY_LORA + A_LORA]
    r, k, v, cw, ca, cg = jnp.split(p, splits, axis=-1)
    w_log = -jax.nn.softplus(-(w0 + jnp.tanh(cw) @ w2)) - 0.5
    decay = jnp.exp(-jnp.exp(w_log.astype(jnp.float32)))
    a = jax.nn.sigmoid(a0 + ca @ a2)
    g = jax.nn.sigmoid(cg) @ g2

    def heads(t):
        return t.reshape(b, s, H_B, HEAD_B).astype(jnp.float32)

    kk = heads(k * k_k)
    kk = kk / jnp.maximum(jnp.sqrt(jnp.sum(kk * kk, axis=-1, keepdims=True)), 1e-12)
    k = k * (1.0 + (a - 1.0) * k_a)
    r_h, k_h, v_h, a_h, w_h = heads(r), heads(k), heads(v), heads(a), heads(decay)

    def step(state, inp):
        r_t, w_t, k_t, v_t, aa_t, bb_t = inp
        sa = jnp.einsum('bhij,bhj->bhi', state, aa_t)
        state = (state * w_t[:, :, None, :] + sa[..., None] * bb_t[:, :, None, :]
                 + v_t[..., None] * k_t[:, :, None, :])
        y = jnp.einsum('bhij,bhj->bhi', state, r_t)
        return state, y

    xs = tuple(jnp.moveaxis(t, 1, 0) for t in (r_h, w_h, k_h, v_h, -kk, kk * a_h))
    init = jnp.zeros((b, H_B, HEAD_B, HEAD_B), jnp.float32)
    _, ys = lax.scan(step, init, xs)
    y = jnp.moveaxis(ys, 0, 1)
    mu = jnp.mean(y, axis=-1, keepdims=True)
    var = jnp.mean(jnp.square(y - mu), axis=-1, keepdims=True)
    yn = (y - mu) * lax.rsqrt(var + GN_EPS)
    gn_w = ln_x_w.reshape(H_B, HEAD_B).astype(jnp.float32)
    gn_b = ln_x_b.reshape(H_B, HEAD_B).astype(jnp.float32)
    yn = yn * gn_w + gn_b
    bonus = jnp.sum(r_h * k_h * r_k.astype(jnp.float32), axis=-1, keepdims=True) * v_h
    out = (yn + bonus) * heads(g)
    return out.reshape(b, s, W_B).astype(p.dtype)

def first_inputs(seed: int = 0) -> dict:
    key = jax.random.key(seed)
    ks = jax.random.split(key, 24)
    L = DEPTH

    def nrm(k, shape, scale):
        return jax.random.normal(k, shape, jnp.float32) * scale

    return {
        "x": nrm(ks[0], (BATCH, SEQ, D_MODEL), 1.0),
        "pre_mix_g": 1.0 + nrm(ks[1], (L, D_MODEL), 0.05),
        "w_in": nrm(ks[2], (L, D_MODEL, IN_COLS), D_MODEL ** -0.5),
        "gate_bias": nrm(ks[3], (L, GATE_COLS), 0.1),
        "rel_bias": nrm(ks[4], (L, H_A, N_REL), 0.5),
        "shift_mu": jax.random.uniform(ks[5], (L, RWKV_COLS), jnp.float32),
        "w0": jax.random.uniform(ks[6], (L, W_B), jnp.float32, -5.0, 0.5),
        "w2": nrm(ks[7], (L, DECAY_LORA, W_B), 0.1),
        "a0": nrm(ks[8], (L, W_B), 0.1),
        "a2": nrm(ks[9], (L, A_LORA, W_B), A_LORA ** -0.5),
        "g2": nrm(ks[10], (L, GATE_LORA, W_B), GATE_LORA ** -0.5),
        "k_k": 0.85 + nrm(ks[11], (L, W_B), 0.05),
        "k_a": 1.0 + nrm(ks[12], (L, W_B), 0.05),
        "r_k": nrm(ks[13], (L, H_B, HEAD_B), 0.1),
        "ln_x_w": 1.0 + nrm(ks[14], (L, W_B), 0.05),
        "ln_x_b": nrm(ks[15], (L, W_B), 0.05),
        "proj_a": nrm(ks[16], (L, W_A, D_MODEL), W_A ** -0.5),
        "proj_b": nrm(ks[17], (L, W_B, D_MODEL), W_B ** -0.5),
        "w_out": nrm(ks[18], (L, D_MODEL, D_MODEL), D_MODEL ** -0.5),
        "post_mix_g": 1.0 + nrm(ks[19], (L, D_MODEL), 0.05),
        "pre_ffn_g": 1.0 + nrm(ks[20], (L, D_MODEL), 0.05),
        "w_up": nrm(ks[21], (L, D_MODEL, D_FF), D_MODEL ** -0.5),
        "w_down": nrm(ks[22], (L, D_FF, D_MODEL), D_FF ** -0.5),
        "post_ffn_g": 1.0 + nrm(ks[23], (L, D_MODEL), 0.05),
    }

def first_block(x, pre_mix_g, w_in, gate_bias, rel_bias, shift_mu, w0, w2, a0, a2, g2,
              k_k, k_a, r_k, ln_x_w, ln_x_b, proj_a, proj_b, w_out, post_mix_g,
              pre_ffn_g, w_up, w_down, post_ffn_g):
    b, s, _ = x.shape
    for l in range(DEPTH):
        h = rms_norm(x, pre_mix_g[l])
        proj = h @ w_in[l]
        p_att = proj[..., :ATT_COLS]
        p_rwkv = proj[..., ATT_COLS:ATT_COLS + RWKV_COLS]
        p_gate = proj[..., ATT_COLS + RWKV_COLS:] + gate_bias[l]

        q, k, v = jnp.split(p_att, 3, axis=-1)
        shp = (b, s, H_A, HEAD_A)
        y_a = chunk_band_attention(q.reshape(shp), k.reshape(shp), v.reshape(shp), rel_bias[l])
        y_b = rwkv7_time_mix(p_rwkv, shift_mu[l], w0[l], w2[l], a0[l], a2[l], g2[l],
                             k_k[l], k_a[l], r_k[l], ln_x_w[l], ln_x_b[l])

        gate_a = jax.nn.sigmoid(p_gate[..., :D_MODEL])
        gate_b = jax.nn.sigmoid(p_gate[..., D_MODEL:])
        merged = gate_a * (y_a @ proj_a[l]) + gate_b * (y_b @ proj_b[l])
        x = x + rms_norm(merged @ w_out[l], post_mix_g[l])

        hf = rms_norm(x, pre_ffn_g[l])
        u = jnp.square(jax.nn.relu(hf @ w_up[l])) @ w_down[l]
        x = x + rms_norm(u, post_ffn_g[l])
    return x


DEPTH_2 = 2

N_EVEN = (DEPTH_2 + 1) // 2
N_ODD = DEPTH_2 // 2
MIX_WIDTH = D_MODEL
HALF = MIX_WIDTH // 2

ML_HEADS = 4
ML_HD = HALF // ML_HEADS
ML_CHUNK = 64
FOX_HEADS = 8
FOX_HD = HALF // FOX_HEADS
FOX_QBLOCK = 128
SSM_HEADDIM = 64
SSM_HEADS = HALF // SSM_HEADDIM
SSM_GROUPS = 2
SSM_HPG = SSM_HEADS // SSM_GROUPS
SSM_STATE = 128
SSM_CONV = 4
SSM_CHUNK = 128
SSM_CONV_CH = HALF + 2 * SSM_GROUPS * SSM_STATE
POOL_WINDOWS = (2, 4, 8, 16)
POOL_GROUPS = 4
POOL_GW = HALF // POOL_GROUPS
D_FF_2 = 256 * ((8 * D_MODEL // 3 + 255) // 256)
FFN_CONV = 3

EVEN_IN = 4 * HALF + 2 * ML_HEADS + 3 * HALF + FOX_HEADS
ODD_IN = HALF + SSM_CONV_CH + SSM_HEADS + HALF
LN_EPS = 1e-5
ALPHA = (2.0 * DEPTH_2) ** 0.25
BETA = (8.0 * DEPTH_2) ** -0.25


def split_sizes(x, sizes):
    offs = []
    acc = 0
    for s in sizes[:-1]:
        acc += s
        offs.append(acc)
    return jnp.split(x, offs, axis=-1)

def layer_norm(x, g, b):
    xf = x.astype(jnp.float32)
    mu = xf.mean(-1, keepdims=True)
    var = jnp.square(xf - mu).mean(-1, keepdims=True)
    return ((xf - mu) * lax.rsqrt(var + LN_EPS) * g.astype(jnp.float32) + b.astype(jnp.float32)).astype(x.dtype)

def rms_norm_2(x, g):
    xf = x.astype(jnp.float32)
    return xf * lax.rsqrt(jnp.square(xf).mean(-1, keepdims=True) + LN_EPS) * g.astype(jnp.float32)

def causal_dwconv(x, w, b):
    k, c = w.shape
    y = lax.conv_general_dilated(x, w[:, None, :].astype(x.dtype), window_strides=(1,), padding=[(k - 1, 0)], dimension_numbers=('NWC', 'WIO', 'NWC'), feature_group_count=c)
    return y + b.astype(x.dtype)

def mlstm_chunkwise(q, k, v, i_pre, f_pre):
    b, h, s, d = q.shape
    L = ML_CHUNK
    nc = s // L
    q = q.astype(jnp.float32) * (d ** -0.5)
    k = k.astype(jnp.float32)
    v = v.astype(jnp.float32)
    ig = i_pre.astype(jnp.float32)
    logf = jax.nn.log_sigmoid(f_pre.astype(jnp.float32))

    def to_chunks(t):
        return jnp.moveaxis(t.reshape(b, h, nc, L, *t.shape[3:]), 2, 0)

    causal = jnp.tril(jnp.ones((L, L), dtype=bool))

    def step(carry, inp):
        c_st, n_st, m_st = carry
        qq, kk, vv, ii, ff = inp
        bcum = jnp.cumsum(ff, axis=-1)
        a = bcum + m_st[..., None]
        dmat = jnp.where(causal, bcum[..., :, None] - bcum[..., None, :] + ii[..., None, :], -jnp.inf)
        mt = jnp.maximum(a, dmat.max(-1))
        w_intra = jnp.exp(dmat - mt[..., None])
        w_inter = jnp.exp(a - mt)
        qk = jnp.einsum('bhld,bhsd->bhls', qq, kk) * w_intra
        num = jnp.einsum('bhls,bhsd->bhld', qk, vv) + w_inter[..., None] * jnp.einsum('bhvk,bhlk->bhlv', c_st, qq)
        den = qk.sum(-1) + w_inter * jnp.einsum('bhk,bhlk->bhl', n_st, qq)
        h_out = num / jnp.maximum(jnp.abs(den), jnp.exp(-mt))[..., None]
        btot = bcum[..., -1]
        g_log = btot[..., None] - bcum + ii
        m_new = jnp.maximum(btot + m_st, g_log.max(-1))
        ws = jnp.exp(g_log - m_new[..., None])
        decay = jnp.exp(btot + m_st - m_new)
        c_new = decay[..., None, None] * c_st + jnp.einsum('bhl,bhlv,bhlk->bhvk', ws, vv, kk)
        n_new = decay[..., None] * n_st + jnp.einsum('bhl,bhlk->bhk', ws, kk)
        return (c_new, n_new, m_new), h_out

    init = (jnp.zeros((b, h, d, d), jnp.float32), jnp.zeros((b, h, d), jnp.float32), jnp.zeros((b, h), jnp.float32))
    _, hs = lax.scan(step, init, (to_chunks(q), to_chunks(k), to_chunks(v), to_chunks(ig), to_chunks(logf)))
    return jnp.moveaxis(hs, 0, 2).reshape(b, h, s, d)

def forgetting_attention(q, k, v, f_pre):
    b, h, s, d = q.shape
    F = jnp.cumsum(jax.nn.log_sigmoid(f_pre.astype(jnp.float32)), axis=-1)
    nb = s // FOX_QBLOCK
    kpos = jnp.arange(s)
    scale = d ** -0.5

    def block(i):
        start = i * FOX_QBLOCK
        qb = lax.dynamic_slice_in_dim(q, start, FOX_QBLOCK, axis=2)
        fq = lax.dynamic_slice_in_dim(F, start, FOX_QBLOCK, axis=2)
        qpos = start + jnp.arange(FOX_QBLOCK)
        logits = jnp.einsum('bhqd,bhkd->bhqk', qb, k).astype(jnp.float32) * scale + fq[..., :, None] - F[..., None, :]
        logits = jnp.where(kpos[None, :] <= qpos[:, None], logits, -jnp.inf)
        p = jax.nn.softmax(logits, axis=-1)
        return jnp.einsum('bhqk,bhkd->bhqd', p.astype(v.dtype), v)

    out = lax.map(block, jnp.arange(nb))
    return jnp.moveaxis(out, 0, 2).reshape(b, h, s, d)

def segsum(a):
    L = a.shape[-1]
    cs = jnp.cumsum(a, axis=-1)
    mask = jnp.tril(jnp.ones((L, L), dtype=bool))
    return jnp.where(mask, cs[..., :, None] - cs[..., None, :], -jnp.inf)

def ssd_chunked(x, dt_a, bm, cm):
    b, s, g, e, p = x.shape
    L = SSM_CHUNK
    nc = s // L
    x = x.reshape(b, nc, L, g, e, p)
    bm = bm.reshape(b, nc, L, g, -1)
    cm = cm.reshape(b, nc, L, g, -1)
    a = jnp.moveaxis(dt_a.reshape(b, nc, L, g, e), (1, 2), (3, 4))
    a_cs = jnp.cumsum(a, axis=-1)
    lmat = jnp.exp(segsum(a))
    cb = jnp.einsum('bclgn,bcsgn->bgcls', cm, bm)
    y_diag = jnp.einsum('bgcls,bgecls,bcsgep->bclgep', cb, lmat, x)
    decay_states = jnp.exp(a_cs[..., -1:] - a_cs)
    states = jnp.einsum('bclgn,bgecl,bclgep->bcgepn', bm, decay_states, x)
    chunk_decay = jnp.exp(a_cs[..., -1])

    def step(hst, inp):
        st, dec = inp
        return dec[..., None, None] * hst + st, hst

    h0 = jnp.zeros((b, g, e, p, states.shape[-1]), jnp.float32)
    _, prev = lax.scan(step, h0, (jnp.moveaxis(states, 1, 0), jnp.moveaxis(chunk_decay, 3, 0)))
    y_off = jnp.einsum('bclgn,cbgepn,bgecl->bclgep', cm, prev, jnp.exp(a_cs))
    return (y_diag + y_off).reshape(b, s, g, e, p)

def multiscale_pool(u, w_grp, b_grp, scale):
    b, s, c = u.shape
    uf = u.astype(jnp.float32)
    csz = jnp.concatenate([jnp.zeros((b, 1, c), jnp.float32), jnp.cumsum(uf, axis=1)], axis=1)
    t = jnp.arange(s)
    outs = []
    for gi, w in enumerate(POOL_WINDOWS):
        lo_c, hi_c = gi * POOL_GW, (gi + 1) * POOL_GW
        cg = csz[:, :, lo_c:hi_c]
        lo = jnp.maximum(t + 1 - w, 0)
        wsum = cg[:, 1:] - jnp.take(cg, lo, axis=1)
        cnt = jnp.minimum(t + 1, w).astype(jnp.float32)
        outs.append(wsum / cnt[None, :, None] - uf[:, :, lo_c:hi_c])
    pooled = jnp.stack(outs, axis=2)
    y = jnp.einsum('bsgc,gcd->bsgd', pooled, w_grp.astype(jnp.float32)).reshape(b, s, c) + b_grp.astype(jnp.float32)
    return y * scale.astype(jnp.float32)

def head_norm(h, g):
    nh, d = h.shape[1], h.shape[3]
    mu = h.mean(-1, keepdims=True)
    var = jnp.square(h - mu).mean(-1, keepdims=True)
    return (h - mu) * lax.rsqrt(var + LN_EPS) * g.astype(jnp.float32).reshape(nh, 1, d)

def even_mixer(x, w_in, b_in, ml_norm, w_out):
    b, s, _ = x.shape
    u = x @ w_in + b_in
    mq, mk, mv, mo, mi, mf, fq, fk, fv, ff = split_sizes(u, [HALF, HALF, HALF, HALF, ML_HEADS, ML_HEADS, HALF, HALF, HALF, FOX_HEADS])

    def heads(t, nh):
        return t.reshape(b, s, nh, -1).transpose(0, 2, 1, 3)

    h_ml = mlstm_chunkwise(heads(mq, ML_HEADS), heads(mk, ML_HEADS), heads(mv, ML_HEADS), mi.transpose(0, 2, 1), mf.transpose(0, 2, 1))
    h_ml = head_norm(h_ml, ml_norm).transpose(0, 2, 1, 3).reshape(b, s, HALF)
    h_ml = (jax.nn.sigmoid(mo.astype(jnp.float32)) * h_ml).astype(x.dtype)
    h_fx = forgetting_attention(heads(fq, FOX_HEADS), heads(fk, FOX_HEADS), heads(fv, FOX_HEADS), ff.transpose(0, 2, 1))
    h_fx = h_fx.transpose(0, 2, 1, 3).reshape(b, s, HALF).astype(x.dtype)
    return jnp.concatenate([h_ml, h_fx], axis=-1) @ w_out

def odd_mixer(x, w_in, conv_w, conv_b, dt_bias, a_log, d_skip, ssm_norm, pool_w, pool_b, pool_scale, w_out):
    b, s, _ = x.shape
    u = x @ w_in
    z, xbc, dt_raw, pool_in = split_sizes(u, [HALF, SSM_CONV_CH, SSM_HEADS, HALF])
    xbc = jax.nn.silu(causal_dwconv(xbc, conv_w, conv_b)).astype(jnp.float32)
    xs, bm, cm = split_sizes(xbc, [HALF, SSM_GROUPS * SSM_STATE, SSM_GROUPS * SSM_STATE])
    dt = jax.nn.softplus(dt_raw.astype(jnp.float32) + dt_bias.astype(jnp.float32))
    a = -jnp.exp(a_log.astype(jnp.float32)).reshape(SSM_GROUPS, SSM_HPG)
    xh = xs.reshape(b, s, SSM_GROUPS, SSM_HPG, SSM_HEADDIM)
    dth = dt.reshape(b, s, SSM_GROUPS, SSM_HPG)
    y = ssd_chunked(xh * dth[..., None], dth * a, bm.reshape(b, s, SSM_GROUPS, SSM_STATE), cm.reshape(b, s, SSM_GROUPS, SSM_STATE))
    y = y + d_skip.astype(jnp.float32).reshape(SSM_GROUPS, SSM_HPG, 1) * xh
    y = rms_norm_2(y.reshape(b, s, HALF) * jax.nn.silu(z.astype(jnp.float32)), ssm_norm).astype(x.dtype)
    p = multiscale_pool(pool_in, pool_w, pool_b, pool_scale).astype(x.dtype)
    return jnp.concatenate([y, p], axis=-1) @ w_out

def conv_ffn(x, w_up, conv_w, conv_b, w_down):
    h = causal_dwconv(x @ w_up, conv_w, conv_b)
    val, gate = jnp.split(h, 2, axis=-1)
    return (jax.nn.silu(gate) * val) @ w_down

def second_inputs(seed: int = 0) -> dict:
    key = jax.random.key(seed)
    ks = jax.random.split(key, 40)
    E, O, L = N_EVEN, N_ODD, DEPTH_2
    nrm = lambda k, shape, sc: jax.random.normal(k, shape, jnp.float32) * sc
    x = nrm(ks[0], (BATCH, SEQ, D_MODEL), 1.0)
    ev_w_in = nrm(ks[1], (E, D_MODEL, EVEN_IN), D_MODEL ** -0.5)
    ev_b_in = jnp.concatenate([
        nrm(ks[2], (E, 4 * HALF), 0.02),
        nrm(ks[3], (E, ML_HEADS), 0.1),
        3.0 + 3.0 * jax.random.uniform(ks[4], (E, ML_HEADS), jnp.float32),
        nrm(ks[5], (E, 3 * HALF), 0.02),
        1.0 + 3.0 * jax.random.uniform(ks[6], (E, FOX_HEADS), jnp.float32)], axis=-1)
    ev_ml_norm = 1.0 + nrm(ks[7], (E, HALF), 0.02)
    ev_w_out = nrm(ks[8], (E, MIX_WIDTH, D_MODEL), MIX_WIDTH ** -0.5 * BETA)
    od_w_in = nrm(ks[9], (O, D_MODEL, ODD_IN), D_MODEL ** -0.5)
    od_conv_w = nrm(ks[10], (O, SSM_CONV, SSM_CONV_CH), SSM_CONV ** -0.5)
    od_conv_b = nrm(ks[11], (O, SSM_CONV_CH), 0.02)
    dt0 = jnp.exp(jax.random.uniform(ks[12], (O, SSM_HEADS), jnp.float32, math.log(1e-3), math.log(1e-1)))
    od_dt_bias = dt0 + jnp.log(-jnp.expm1(-dt0))
    od_a_log = jnp.log(jax.random.uniform(ks[13], (O, SSM_HEADS), jnp.float32, 1.0, 16.0))
    od_d_skip = 1.0 + nrm(ks[14], (O, SSM_HEADS), 0.02)
    od_ssm_norm = 1.0 + nrm(ks[15], (O, HALF), 0.02)
    od_pool_w = nrm(ks[16], (O, POOL_GROUPS, POOL_GW, POOL_GW), POOL_GW ** -0.5)
    od_pool_b = nrm(ks[17], (O, HALF), 0.02)
    od_pool_scale = 1.0 + nrm(ks[18], (O, HALF), 0.1)
    od_w_out = nrm(ks[19], (O, MIX_WIDTH, D_MODEL), MIX_WIDTH ** -0.5 * BETA)
    ffn_w_up = nrm(ks[20], (L, D_MODEL, 2 * D_FF_2), D_MODEL ** -0.5)
    ffn_conv_w = nrm(ks[21], (L, FFN_CONV, 2 * D_FF_2), FFN_CONV ** -0.5)
    ffn_conv_b = nrm(ks[22], (L, 2 * D_FF_2), 0.02)
    ffn_w_down = nrm(ks[23], (L, D_FF_2, D_MODEL), D_FF_2 ** -0.5 * BETA)
    ln1_g = 1.0 + nrm(ks[24], (L, D_MODEL), 0.02)
    ln1_b = nrm(ks[25], (L, D_MODEL), 0.02)
    ln2_g = 1.0 + nrm(ks[26], (L, D_MODEL), 0.02)
    ln2_b = nrm(ks[27], (L, D_MODEL), 0.02)
    return {'x': x, 'ev_w_in': ev_w_in, 'ev_b_in': ev_b_in, 'ev_ml_norm': ev_ml_norm, 'ev_w_out': ev_w_out,
            'od_w_in': od_w_in, 'od_conv_w': od_conv_w, 'od_conv_b': od_conv_b, 'od_dt_bias': od_dt_bias,
            'od_a_log': od_a_log, 'od_d_skip': od_d_skip, 'od_ssm_norm': od_ssm_norm, 'od_pool_w': od_pool_w,
            'od_pool_b': od_pool_b, 'od_pool_scale': od_pool_scale, 'od_w_out': od_w_out,
            'ffn_w_up': ffn_w_up, 'ffn_conv_w': ffn_conv_w, 'ffn_conv_b': ffn_conv_b, 'ffn_w_down': ffn_w_down,
            'ln1_g': ln1_g, 'ln1_b': ln1_b, 'ln2_g': ln2_g, 'ln2_b': ln2_b}

def second_block(x, ev_w_in, ev_b_in, ev_ml_norm, ev_w_out, od_w_in, od_conv_w, od_conv_b, od_dt_bias, od_a_log, od_d_skip, od_ssm_norm, od_pool_w, od_pool_b, od_pool_scale, od_w_out, ffn_w_up, ffn_conv_w, ffn_conv_b, ffn_w_down, ln1_g, ln1_b, ln2_g, ln2_b):
    for layer in range(DEPTH_2):
        j = layer // 2
        if layer % 2 == 0:
            y = even_mixer(x, ev_w_in[j], ev_b_in[j], ev_ml_norm[j], ev_w_out[j])
        else:
            y = odd_mixer(x, od_w_in[j], od_conv_w[j], od_conv_b[j], od_dt_bias[j], od_a_log[j], od_d_skip[j], od_ssm_norm[j], od_pool_w[j], od_pool_b[j], od_pool_scale[j], od_w_out[j])
        x = layer_norm(ALPHA * x + y, ln1_g[layer], ln1_b[layer])
        f = conv_ffn(x, ffn_w_up[layer], ffn_conv_w[layer], ffn_conv_b[layer], ffn_w_down[layer])
        x = layer_norm(ALPHA * x + f, ln2_g[layer], ln2_b[layer])
    return x


def setup_inputs(seed=0):
    out = dict(first_inputs(seed))
    for name, value in second_inputs(seed + 1).items():
        if name != "x":
            out[name + "_2"] = value
    return out


def reference(
    x, pre_mix_g, w_in, gate_bias, rel_bias, shift_mu, w0, w2, a0, a2, g2, k_k, k_a, r_k,
    ln_x_w, ln_x_b, proj_a, proj_b, w_out, post_mix_g, pre_ffn_g, w_up, w_down, post_ffn_g,
    ev_w_in_2, ev_b_in_2, ev_ml_norm_2, ev_w_out_2, od_w_in_2, od_conv_w_2, od_conv_b_2,
    od_dt_bias_2, od_a_log_2, od_d_skip_2, od_ssm_norm_2, od_pool_w_2, od_pool_b_2,
    od_pool_scale_2, od_w_out_2, ffn_w_up_2, ffn_conv_w_2, ffn_conv_b_2, ffn_w_down_2, ln1_g_2,
    ln1_b_2, ln2_g_2, ln2_b_2,
):
    x = first_block(
        x, pre_mix_g, w_in, gate_bias, rel_bias, shift_mu, w0, w2, a0, a2, g2, k_k, k_a, r_k,
        ln_x_w, ln_x_b, proj_a, proj_b, w_out, post_mix_g, pre_ffn_g, w_up, w_down, post_ffn_g,
    )
    return second_block(
        x, ev_w_in_2, ev_b_in_2, ev_ml_norm_2, ev_w_out_2, od_w_in_2, od_conv_w_2, od_conv_b_2,
        od_dt_bias_2, od_a_log_2, od_d_skip_2, od_ssm_norm_2, od_pool_w_2, od_pool_b_2,
        od_pool_scale_2, od_w_out_2, ffn_w_up_2, ffn_conv_w_2, ffn_conv_b_2, ffn_w_down_2,
        ln1_g_2, ln1_b_2, ln2_g_2, ln2_b_2,
    )


_drawn_inputs = setup_inputs


def setup_inputs(seed=0):
    import zlib

    import numpy as np

    out = dict(_drawn_inputs(seed))
    spreads = {}
    factors = {'ev_ml_norm_2': 8.0,
     'od_conv_b_2': 8.0,
     'od_d_skip_2': 8.0,
     'od_ssm_norm_2': 8.0,
     'od_pool_b_2': 8.0,
     'od_pool_scale_2': 2.824,
     'ffn_conv_b_2': 6.562}
    for name, (base, spread) in spreads.items():
        noise = np.random.default_rng([zlib.crc32(name.encode()), seed]).standard_normal(out[name].shape)
        drawn = base * np.exp(spread * noise) if base else spread * noise
        out[name] = __import__('jax').numpy.asarray(drawn.astype(out[name].dtype))
    for name, factor in factors.items():
        out[name] = (out[name] * factor).astype(out[name].dtype)
    return out
```

```python
from contextlib import ExitStack

import numpy as np

import concourse.bass as bass
from concourse import mybir


F32 = mybir.dt.float32
I32 = mybir.dt.int32
ALU = mybir.AluOpType
ACT = mybir.ActivationFunctionType
AX_X = mybir.AxisListType.X

P = 128
T = 512
NT = T // P
D = 1024
KD = D // P
HALF = D // 2
KH = HALF // P
HEADS = 8
HD = 64
ML_HEADS = 4
BAND_BIAS = 320
REL_CLIP = 256
DIAG_PAD = 704
FF1 = 4096 // P
FF2 = 2816 // P
NEG = -1e30
RMS_EPS = 1e-6
LN_EPS = 1e-5
GN_EPS = HD * 1e-5
ALPHA = 4.0 ** 0.25
WINDOWS = (2, 4, 8, 16)
LEVELS = 7

UNIT = 8
RING = 8
WORK = 58

VECTORS = [("pre_mix_g", 8), ("gate_bias", 16), ("shift_mu", 14), ("w0", 4), ("a0", 4), ("k_k", 4),
           ("k_a", 4), ("r_k", 4), ("ln_x_w", 4), ("ln_x_b", 4), ("post_mix_g", 8), ("pre_ffn_g", 8),
           ("post_ffn_g", 8), ("ev_b", 28), ("ev_bi", 1), ("ev_bf", 1), ("ev_bff", 1), ("ml_norm", 4),
           ("conv_w", 32), ("conv_b", 8), ("dt_bias", 1), ("a_log", 1), ("d_skip", 4), ("ssm_norm", 4),
           ("pool_b", 4), ("pool_scale", 4), ("ffn_w", 264), ("ffn_b", 88), ("ln1_g", 16), ("ln1_b", 16),
           ("ln2_g", 16), ("ln2_b", 16), ("w2a2", 512), ("g2", 512), ("ev_gates", 128), ("od_dt", 64),
           ("pool_w", 512)]
CONSTANTS = [("ident", 128), ("flip", 128), ("same_head", 128), ("levels", 128 * LEVELS), ("level0_t", 128),
             ("mask4", 512), ("diag_qk", 128), ("diag_st", 128), ("inv_count", 64), ("eps", 3)]


def columns(spec):
    at, out = 0, {}
    for name, n in spec:
        out[name] = (at, n)
        at += n
    return out, at


class Signal:

    def __init__(self, sem):
        self.sem, self.base = sem, 0

    def at(self, n):
        return self.base + n

    def close(self, n):
        self.base += n


class Chain:

    def __init__(self, sem):
        self.sem, self.n = sem, 0

    def link(self, eng, ins):
        self.n += 1
        ins.then_inc(self.sem, 1)
        eng.wait_ge(self.sem, self.n)


class Weights:

    def __init__(self, ring, landed, unit_used, source, n_units):
        self.ring, self.landed, self.unit_used, self.source = ring, landed, unit_used, source
        self.n_units, self.block, self.loaded, self.used = n_units, 0, 0, 0
        self.release = []

    def take(self, pe):
        unit, i = divmod(self.block, UNIT)
        if i == 0:
            pe.wait_ge(self.landed[unit % RING], 16 * (unit // RING + 1))
        self.block += 1
        return self.ring[:, unit % RING, i * P:(i + 1) * P]

    def free(self, ins, signal=None, n=0):
        if self.block % UNIT == 0:
            if signal is None:
                self.used += 1
                ins.then_inc(self.unit_used, 1)
                self.release.append((self.unit_used, self.used))
            else:
                self.release.append((signal.sem, signal.at(n)))

    def load(self, sp):
        while self.loaded < min(self.n_units, len(self.release) + RING):
            u = self.loaded
            if u >= RING:
                sp.wait_ge(*self.release[u - RING])
            sp.dma_start(self.ring[:, u % RING, :], self.source[u]).then_inc(self.landed[u % RING], 16)
            self.loaded += 1


def network(nc, x_t, vectors, constants, rel_rev, stream, bias_line, out_t, upto=None):
    n_units = stream.shape[0]
    ctx = ExitStack()
    with ctx:
        def sb(name, shape, dt=F32):
            return ctx.enter_context(nc.sbuf_tensor(name, shape, dt))

        def sem(name):
            return ctx.enter_context(nc.semaphore(name))

        x = sb("x", [P, KD, T])
        h = sb("h", [P, KD, T])
        ring = sb("ring", [P, RING, UNIT * P])
        w = sb("work", [P, WORK, T])
        vec_cols, n_vec = columns(VECTORS)
        con_cols, n_con = columns(CONSTANTS)
        vec = sb("vec", [P, n_vec])
        con = sb("con", [P, n_con])
        ones = sb("ones", [P, T])
        col = sb("col", [P, 64])
        ps = ctx.enter_context(nc.psum_tensor("ps", [P, 8, T], F32))

        def v(name, i=0, n=1, rows=P):
            a = vec_cols[name][0] + i
            return vec[0:rows, a:a + n]

        def c(name, i=0, n=None, rows=P):
            a, m = con_cols[name]
            return con[0:rows, a + i:a + i + (m if n is None else n)]

        ident = c("ident")
        eps_of = {RMS_EPS: c("eps", 0, 1), LN_EPS: c("eps", 1, 1), GN_EPS: c("eps", 2, 1)}
        one = ones[:, 0:1]

        dve_chain = Chain(sem("dve_chain"))
        act_chain = Chain(sem("act_chain"))
        pool_chain = Chain(sem("pool_chain"))
        inputs_landed = sem("inputs_landed")
        wts = Weights(ring, [sem(f"unit_landed_{i}") for i in range(RING)], sem("unit_used"), stream, n_units)

        tile_ready = Signal(sem("tile_ready"))
        tile_read = Signal(sem("tile_read"))
        act_out = Signal(sem("act_out"))
        act_out2 = Signal(sem("act_out2"))
        dve_out = Signal(sem("dve_out"))
        dve_out2 = Signal(sem("dve_out2"))
        dve_out3 = Signal(sem("dve_out3"))
        pe_out = Signal(sem("pe_out"))
        pe_out2 = Signal(sem("pe_out2"))
        dma_out = Signal(sem("dma_out"))

        V, S, TE, G = nc.vector, nc.scalar, nc.tensor, nc.gpsimd

        def bank(b, a=0, n=T, rows=slice(0, P)):
            return ps[rows, b, a:a + n]

        def tok(k, c0, n=P):
            return slice(c0 * P, c0 * P + n)

        def half(hh):
            return slice(HD * (hh % 2), HD * (hh % 2) + HD)

        def product(pe, n_tiles, n_k, rhs, banks=4, first=0, width=T):
            for m in range(first, first + n_tiles):
                if m >= banks:
                    pe.wait_ge(tile_read.sem, tile_read.at(m - banks + 1))
                for k in range(n_k):
                    ins = TE.matmul(bank(m % banks), wts.take(pe), rhs(k), start=(k == 0), stop=(k == n_k - 1))
                    last = k == n_k - 1
                    wts.free(ins, tile_ready if last else None, m + 1)
                ins.then_inc(tile_ready.sem, 1)

        def norm(src, groups, mean_of, eps, gain, out, sums, centre=False, bias=None, add_to=None, sq0=0):
            n_g = len(groups)
            order = [(g, t) for g, ts in enumerate(groups) for t in ts]
            size = len(groups[0])
            with nc.Block() as block:
                @block.tensor
                def _(pe):
                    if centre:
                        for g, ts in enumerate(groups):
                            for i, t in enumerate(ts):
                                ins = TE.matmul(bank(g % 4), sums, src(t), start=(i == 0), stop=(i == size - 1))
                            ins.then_inc(pe_out.sem, 1)
                    for g, ts in enumerate(groups):
                        for i, t in enumerate(ts):
                            pe.wait_ge(act_out.sem, act_out.at(g * size + i + 1))
                            ins = TE.matmul(bank(4 + g % 4), sums, w[:, sq0 + g * size + i, :],
                                            start=(i == 0), stop=(i == size - 1))
                        ins.then_inc(tile_ready.sem, 1)

                @block.scalar
                def _(act):
                    for n, (g, t) in enumerate(order):
                        if centre:
                            act.wait_ge(dve_out.sem, dve_out.at(n + 1))
                        S.activation(w[:, sq0 + n, :], src(t), ACT.Square).then_inc(act_out.sem, 1)
                    for g in range(n_g):
                        act.wait_ge(tile_ready.sem, tile_ready.at(g + 1))
                        S.activation(w[:, sq0 + 8 + g, :], bank(4 + g % 4), ACT.Sqrt, scale=1.0 / mean_of,
                                     bias=eps_of[eps]).then_inc(act_out2.sem, 1)
                    if bias is not None:
                        for n, (g, t) in enumerate(order):
                            act.wait_ge(dve_out2.sem, dve_out2.at(n + 1))
                            S.activation(out(t), out(t), ACT.Identity, bias=bias(t)).then_inc(act_out2.sem, 1)

                @block.vector
                def _(dve):
                    if centre:
                        for g, ts in enumerate(groups):
                            dve.wait_ge(pe_out.sem, pe_out.at(g + 1))
                            for t in ts:
                                V.scalar_tensor_tensor(src(t), bank(g % 4), -1.0 / mean_of, src(t), ALU.mult,
                                                       ALU.add).then_inc(dve_out.sem, 1)
                        dve.wait_ge(dve_out.sem, dve_out.at(len(order)))
                    for g, ts in enumerate(groups):
                        dve.wait_ge(act_out2.sem, act_out2.at(g + 1))
                        r = w[:, sq0 + 8 + g, :]
                        dve_chain.link(dve, V.reciprocal(r, r))
                        for t in ts:
                            dst = w[:, sq0 + t, :] if add_to is not None else out(t)
                            V.scalar_tensor_tensor(dst, src(t), gain(t), r, ALU.mult,
                                                   ALU.mult).then_inc(dve_out2.sem, 1)

                if add_to is not None:
                    @block.gpsimd
                    def _(pool):
                        for n, (g, t) in enumerate(order):
                            pool.wait_ge(dve_out2.sem, dve_out2.at(n + 1))
                            G.tensor_tensor(add_to(t), add_to(t), w[:, sq0 + t, :],
                                            ALU.add).then_inc(pool_chain.sem, 1)
                        pool_chain.n += len(order)
                        pool.wait_ge(pool_chain.sem, pool_chain.n)
            if centre:
                pe_out.close(n_g)
                dve_out.close(len(order))
            act_out.close(len(order))
            tile_ready.close(n_g)
            act_out2.close(n_g + (len(order) if bias is not None else 0))
            dve_out2.close(len(order))

        def xt(t):
            return x[:, t, :]

        def ht(t):
            return h[:, t, :]

        def wt(a):
            return lambda t: w[:, a + t, :]

        def to_token_major(jobs, scaled=None):
            n_banks = 4 * len(jobs)
            with nc.Block() as block:
                @block.tensor
                def _(pe):
                    for n in range(n_banks):
                        src = jobs[n // 4][0]
                        if n >= 4:
                            pe.wait_ge(tile_read.sem, tile_read.at(n - 3))
                        for t in range(4):
                            ins = TE.transpose(bank(n % 4, t * P, P), w[:, src + t, tok(0, n % 4)], ident)
                        ins.then_inc(tile_ready.sem, 1)

                @block.vector
                def _(dve):
                    for n in range(n_banks):
                        dst = jobs[n // 4][1] + n % 4
                        dve.wait_ge(tile_ready.sem, tile_ready.at(n + 1))
                        if scaled is None:
                            V.tensor_copy(w[:, dst, :], bank(n % 4)).then_inc(tile_read.sem, 1)
                        else:
                            V.tensor_tensor(w[:, dst, :].rearrange("p (h d) -> p h d", d=HD),
                                            bank(n % 4).rearrange("p (h d) -> p h d", d=HD),
                                            scaled(n % 4).unsqueeze(2).to_broadcast([P, HEADS, HD]),
                                            ALU.mult).then_inc(tile_read.sem, 1)
            tile_ready.close(n_banks)
            tile_read.close(n_banks)

        def attention(kind, q0, k0, vt0, out0, tmp, f_rows=None, g_rows=None, f_cols=None, bias0=None):
            heads = ML_HEADS if kind == "mlstm" else HEADS
            dim = HALF // heads
            items = [(hd, i) for hd in range(heads) for i in range(NT)]
            n_items = len(items)
            e = [w[:, tmp, :], w[:, tmp + 1, :]]
            pt = [w[:, tmp + 2, :], w[:, tmp + 3, :]]
            ml = kind == "mlstm"
            heads_a_tile = P // dim

            def rows(hd):
                return half(hd) if dim == HD else slice(0, P)

            with nc.Block() as block:
                @block.tensor
                def _(pe):
                    def scores(n):
                        hd, i = items[n]
                        wd = (i + 1) * P
                        t, r = hd // heads_a_tile, rows(hd)
                        if n >= 2:
                            last = dve_out2 if ml else act_out
                            pe.wait_ge(last.sem, last.at(n - 1))
                        d = bank(n % 2, 0, wd)
                        qk = bank(6 + n % 2, 0, wd) if ml else d
                        ins = TE.matmul(qk, w[r, q0 + t, i * P:(i + 1) * P], w[r, k0 + t, 0:wd],
                                        start=True, stop=ml)
                        if kind == "band":
                            ins = TE.matmul(d, c("flip"), w[:, bias0 + hd, (3 - i) * P:T], start=False, stop=True)
                        else:
                            sel = c("ident", hd, 1, rows=heads)
                            TE.matmul(d, f_rows[:, i * P:(i + 1) * P], sel.to_broadcast([heads, wd]),
                                      start=ml, stop=False)
                            TE.matmul(d, sel.to_broadcast([heads, P]), g_rows[:, 0:wd], start=False, stop=False)
                            ins = TE.matmul(bank(n % 2, i * P, P), ident, c("diag_qk"), start=False, stop=True)
                        ins.then_inc(tile_ready.sem, 1)

                    def turn(n):
                        hd, i = items[n]
                        pe.wait_ge(dve_out2.sem, dve_out2.at(n + 1))
                        if n >= 2:
                            pe.wait_ge(act_out2.sem, act_out2.at(n - 1))
                        for j in range(i + 1):
                            ins = TE.transpose(bank(2 + n % 2, j * P, P), e[n % 2][:, j * P:(j + 1) * P], ident)
                        ins.then_inc(pe_out.sem, 1)

                    def values(n):
                        hd, i = items[n]
                        t = hd // heads_a_tile
                        if i == 0 and hd % heads_a_tile == 0 and t >= 2:
                            pe.wait_ge(dve_out3.sem, dve_out3.at(t - 1))
                        pe.wait_ge(act_out2.sem, act_out2.at(n + 1))
                        for j in range(i + 1):
                            ins = TE.matmul(bank(4 + t % 2, i * P, P, rows(hd)),
                                            w[:, vt0 + j, hd * dim:(hd + 1) * dim],
                                            pt[n % 2][:, j * P:(j + 1) * P], start=(j == 0), stop=(j == i))
                        ins.then_inc(pe_out2.sem, 1)

                    scores(0)
                    for n in range(n_items):
                        if n + 1 < n_items:
                            scores(n + 1)
                        if n >= 1:
                            values(n - 1)
                        turn(n)
                    values(n_items - 1)

                @block.vector
                def _(dve):
                    def peak(n):
                        hd, i = items[n]
                        dve.wait_ge(tile_ready.sem, tile_ready.at(n + 1))
                        mx, neg = col[:, n % 2:n % 2 + 1], col[:, 2 + n % 2:3 + n % 2]
                        dve_chain.link(dve, V.reduce_max(mx, bank(n % 2, 0, (i + 1) * P), AX_X))
                        if ml:
                            dve_chain.link(dve, V.tensor_tensor(mx, mx, f_cols(i, hd), ALU.max))
                        if n >= 2:
                            dve.wait_ge(act_out.sem, act_out.at(n - 1))
                        V.tensor_scalar(neg, mx, -1.0, None, ALU.mult).then_inc(dve_out.sem, 1)

                    def scale(n):
                        hd, i = items[n]
                        wd = (i + 1) * P
                        s = col[:, 4 + n % 2:5 + n % 2]
                        a = e[n % 2][:, 0:wd]
                        dve.wait_ge(act_out.sem, act_out.at(n + 1))
                        if ml:
                            low, neg = col[:, 6 + n % 2:7 + n % 2], col[:, 8 + n % 2:9 + n % 2]
                            dve_chain.link(dve, V.tensor_tensor(a, bank(6 + n % 2, 0, wd), a, ALU.mult))
                            dve_chain.link(dve, V.reduce_sum(s, a, AX_X))
                            dve_chain.link(dve, V.tensor_scalar(neg, s, -1.0, None, ALU.mult))
                            dve_chain.link(dve, V.tensor_tensor(s, s, neg, ALU.max))
                            dve_chain.link(dve, V.tensor_tensor(s, s, low, ALU.max))
                        dve_chain.link(dve, V.reciprocal(s, s))
                        V.tensor_scalar(a, a, s, None, ALU.mult).then_inc(dve_out2.sem, 1)

                    def empty(t):
                        dve.wait_ge(pe_out2.sem, pe_out2.at((t + 1) * NT * heads_a_tile))
                        V.tensor_copy(w[:, out0 + t, :], bank(4 + t % 2)).then_inc(dve_out3.sem, 1)

                    peak(0)
                    per = NT * heads_a_tile
                    for n in range(n_items):
                        if n + 1 < n_items:
                            peak(n + 1)
                        scale(n)
                        if n >= per and n % per == 1:
                            empty(n // per - 1)
                    empty(heads // heads_a_tile - 1)

                @block.scalar
                def _(act):
                    def exps(n):
                        hd, i = items[n]
                        wd = (i + 1) * P
                        neg = col[:, 2 + n % 2:3 + n % 2]
                        act.wait_ge(dve_out.sem, dve_out.at(n + 1))
                        if n >= 2:
                            act.wait_ge(pe_out.sem, pe_out.at(n - 1))
                        if ml:
                            S.activation(e[n % 2][:, 0:wd], bank(n % 2, 0, wd), ACT.Exp, bias=neg)
                            S.activation(col[:, 6 + n % 2:7 + n % 2], neg, ACT.Exp).then_inc(act_out.sem, 1)
                        else:
                            S.activation(e[n % 2][:, 0:wd], bank(n % 2, 0, wd), ACT.Exp, bias=neg,
                                         accum_out=col[:, 4 + n % 2:5 + n % 2]).then_inc(act_out.sem, 1)

                    def copy(n):
                        hd, i = items[n]
                        wd = (i + 1) * P
                        act.wait_ge(pe_out.sem, pe_out.at(n + 1))
                        if n >= 2:
                            act.wait_ge(pe_out2.sem, pe_out2.at(n - 1))
                        S.activation(pt[n % 2][:, 0:wd], bank(2 + n % 2, 0, wd), ACT.Copy).then_inc(act_out2.sem, 1)

                    exps(0)
                    for n in range(n_items):
                        if n + 1 < n_items:
                            exps(n + 1)
                        copy(n)
            tile_ready.close(n_items)
            pe_out.close(n_items)
            pe_out2.close(n_items)
            dve_out.close(n_items)
            dve_out2.close(n_items)
            dve_out3.close(heads // heads_a_tile)
            act_out.close(n_items)
            act_out2.close(n_items)

        def stage_inputs():
            with nc.Block() as block:
                @block.sync
                def _(sp):
                    sp.dma_start(x[:, :, :], x_t.rearrange("(k p) t -> p k t", p=P)).then_inc(inputs_landed, 16)
                    sp.dma_start(vec[:, :], vectors).then_inc(inputs_landed, 16)
                    sp.dma_start(con[:, :], constants).then_inc(inputs_landed, 16)
                    sp.dma_start(w[0:HEADS, 0, 0:BAND_BIAS], rel_rev).then_inc(inputs_landed, 16)
                    wts.load(sp)
                    sp.wait_ge(inputs_landed, 64)
                    sp.wait_ge(dve_out.sem, dve_out.at(1))
                    sp.dma_start(bias_line, w[0:HEADS, 1:3, :].rearrange("p a t -> p (a t)")[:, 0:DIAG_PAD]
                                 ).then_inc(dma_out.sem, 16)
                    sp.wait_ge(dma_out.sem, dma_out.at(16))
                    diagonals = bass.AP(bias_line.tensor, bias_line.offset + 1, [[1, P], [DIAG_PAD, HEADS], [1, T]])
                    sp.dma_start(w[:, 20:28, :], diagonals).then_inc(dma_out.sem, 16)
                    sp.wait_ge(dma_out.sem, dma_out.at(32))

                @block.vector
                def _(dve):
                    line = w[0:HEADS, 1:3, :].rearrange("p a t -> p (a t)")
                    V.memset(ones[:, :], 1.0)
                    dve_chain.link(dve, V.memset(line, 0.0))
                    dve.wait_ge(inputs_landed, 64)
                    V.tensor_copy(line[:, REL_CLIP:REL_CLIP + BAND_BIAS], w[0:HEADS, 0, 0:BAND_BIAS])
                    V.tensor_copy(line[:, 0:REL_CLIP],
                                  w[0:HEADS, 0, 0:1].to_broadcast([HEADS, REL_CLIP])).then_inc(dve_out.sem, 1)
            dve_out.close(1)
            dma_out.close(32)
            with nc.Block() as block:
                @block.vector
                def _(dve):
                    dve_chain.link(dve, V.memset(w[HD:P, 20:28, T - HD:T], NEG))

        YA, YB = 14, 50

        def stage_qkv():
            with nc.Block() as block:
                @block.tensor
                def _(pe):
                    product(pe, 12, KD, ht)

                @block.sync
                def _(sp):
                    wts.load(sp)

                @block.scalar
                def _(act):
                    for m in range(12):
                        act.wait_ge(tile_ready.sem, tile_ready.at(m + 1))
                        S.activation(w[:, m, :], bank(m % 4), ACT.Copy,
                                     scale=HD ** -0.5 if m < 4 else 1.0).then_inc(tile_read.sem, 1)
            tile_ready.close(12)
            tile_read.close(12)

        def stage_rwkv_in():
            raw0 = 54
            raw = w[:, raw0:raw0 + 3, :].rearrange("p a t -> p (a t)")
            pads = [raw[:, 0:T + 1], raw[:, T + 8:2 * T + 9]]
            with nc.Block() as block:
                @block.tensor
                def _(pe):
                    product(pe, 14, KD, ht)

                @block.sync
                def _(sp):
                    wts.load(sp)

                @block.scalar
                def _(act):
                    act.wait_ge(dve_out2.sem, dve_out2.at(1))
                    for m in range(14):
                        act.wait_ge(tile_ready.sem, tile_ready.at(m + 1))
                        if m >= 2:
                            act.wait_ge(dve_out.sem, dve_out.at(m - 1))
                        S.activation(pads[m % 2][:, 1:T + 1], bank(m % 4), ACT.Copy).then_inc(tile_read.sem, 1)

                @block.vector
                def _(dve):
                    V.memset(pads[0][:, 0:1], 0.0)
                    V.memset(pads[1][:, 0:1], 0.0).then_inc(dve_out2.sem, 1)
                    dve.wait_ge(dve_out2.sem, dve_out2.at(1))
                    for m in range(14):
                        p = pads[m % 2]
                        dve.wait_ge(tile_read.sem, tile_read.at(m + 1))
                        dve_chain.link(dve, V.tensor_tensor(w[:, m, :], p[:, 0:T], p[:, 1:T + 1], ALU.subtract))
                        V.scalar_tensor_tensor(w[:, m, :], w[:, m, :], v("shift_mu", m), p[:, 1:T + 1], ALU.mult,
                                               ALU.add).then_inc(dve_out.sem, 1)
            tile_ready.close(14)
            tile_read.close(14)
            dve_out.close(14)
            dve_out2.close(1)

        R, K, VV, CW, CG = 0, 4, 8, 12, 13
        LW, CM, AA, KK, GG, EE, AT, BO = 18, 22, 26, 30, 34, 38, 42, 46

        def stage_rwkv_prepare():
            with nc.Block() as block:
                @block.scalar
                def _(act):
                    act_chain.link(act, S.activation(w[0:HD, CW, :], w[0:HD, CW, :], ACT.Tanh))
                    S.activation(w[:, CG, :], w[:, CG, :], ACT.Sigmoid).then_inc(act_out.sem, 1)
                    for t in range(4):
                        act.wait_ge(tile_ready.sem, tile_ready.at(3 * t + 1))
                        S.activation(w[:, LW + t, :], bank(0), ACT.Sigmoid, bias=v("w0", t)).then_inc(tile_read.sem, 1)
                        act.wait_ge(tile_ready.sem, tile_ready.at(3 * t + 2))
                        S.activation(w[:, AA + t, :], bank(1), ACT.Sigmoid, bias=v("a0", t)).then_inc(tile_read.sem, 1)
                        act.wait_ge(tile_ready.sem, tile_ready.at(3 * t + 3))
                        S.activation(w[:, GG + t, :], bank(2), ACT.Copy).then_inc(tile_read.sem, 1)
                    for t in range(4):
                        act.wait_ge(pe_out.sem, pe_out.at(t + 1))
                        S.activation(w[:, EE + t, :], bank(4 + t), ACT.Sqrt).then_inc(act_out2.sem, 1)

                @block.tensor
                def _(pe):
                    pe.wait_ge(act_out.sem, act_out.at(1))
                    for t in range(4):
                        if t >= 1:
                            pe.wait_ge(tile_read.sem, tile_read.at(3 * t - 2))
                        TE.matmul(bank(0), v("w2a2", t * P, P)[0:HD], w[0:HD, CW, :], start=True,
                                  stop=True).then_inc(tile_ready.sem, 1)
                        if t >= 1:
                            pe.wait_ge(tile_read.sem, tile_read.at(3 * t - 1))
                        TE.matmul(bank(1), v("w2a2", t * P, P)[HD:P], w[HD:P, CW, :], start=True,
                                  stop=True).then_inc(tile_ready.sem, 1)
                        if t >= 1:
                            pe.wait_ge(tile_read.sem, tile_read.at(3 * t))
                        TE.matmul(bank(2), v("g2", t * P, P), w[:, CG, :], start=True,
                                  stop=True).then_inc(tile_ready.sem, 1)
                    for t in range(4):
                        pe.wait_ge(dve_out.sem, dve_out.at(t + 1))
                        TE.matmul(bank(4 + t), c("same_head"), w[:, AT + t, :], start=True,
                                  stop=True).then_inc(pe_out.sem, 1)
                    for t in range(4):
                        pe.wait_ge(act_out2.sem, act_out2.at(t + 1))
                        pe.wait_ge(dve_out2.sem, dve_out2.at(t + 1))
                        TE.matmul(bank(4 + t), c("same_head"), w[:, BO + t, :], start=True,
                                  stop=True).then_inc(pe_out.sem, 1)

                @block.vector
                def _(dve):
                    for t in range(4):
                        kk, sq = w[:, KK + t, :], w[:, AT + t, :]
                        dve_chain.link(dve, V.tensor_scalar(kk, w[:, K + t, :], v("k_k", t), None, ALU.mult))
                        V.tensor_tensor(sq, kk, kk, ALU.mult).then_inc(dve_out.sem, 1)
                    for t in range(4):
                        kt, lw, a = w[:, K + t, :], w[:, LW + t, :], w[:, AA + t, :]
                        cm = w[:, CM + t, :]
                        dve.wait_ge(tile_read.sem, tile_read.at(3 * t + 2))
                        tmp = w[:, BO + t, :]
                        dve_chain.link(dve, V.tensor_scalar(tmp, a, -1.0, v("k_a", t), ALU.add, ALU.mult))
                        dve_chain.link(dve, V.scalar_tensor_tensor(kt, tmp, 1.0, kt, ALU.add, ALU.mult))
                        V.scalar_tensor_tensor(tmp, w[:, R + t, :], v("r_k", t), kt, ALU.mult,
                                               ALU.mult).then_inc(dve_out2.sem, 1)
                        dve_chain.link(dve, V.tensor_scalar(lw, lw, -float(np.exp(-0.5)), None, ALU.mult))
                        for ch in range(NT):
                            s = slice(ch * P, (ch + 1) * P)
                            dve_chain.link(dve, V.tensor_tensor_scan(cm[:, s], ones[:, 0:P], lw[:, s], 0.0,
                                                                     ALU.mult, ALU.add))
                            mid = col[:, 0:1]
                            dve_chain.link(dve, V.tensor_copy(mid, cm[:, ch * P + HD - 1:ch * P + HD]))
                            dve_chain.link(dve, V.tensor_scalar(cm[:, s], cm[:, s], mid, None, ALU.subtract))
                    dve.wait_ge(dve_out2.sem, dve_out2.at(4))
                    for t in range(4):
                        kk, rn = w[:, KK + t, :], w[:, EE + t, :]
                        dve.wait_ge(act_out2.sem, act_out2.at(t + 1))
                        dve_chain.link(dve, V.tensor_scalar(rn, rn, 1e-12, None, ALU.max))
                        dve_chain.link(dve, V.reciprocal(rn, rn))
                        dve_chain.link(dve, V.tensor_tensor(kk, kk, rn, ALU.mult))
                    for t in range(4):
                        dve.wait_ge(pe_out.sem, pe_out.at(5 + t))
                        dve_chain.link(dve, V.tensor_tensor(w[:, BO + t, :], bank(4 + t), w[:, VV + t, :], ALU.mult))
            tile_ready.close(12)
            tile_read.close(12)
            pe_out.close(8)
            act_out.close(1)
            act_out2.close(4)
            dve_out.close(4)
            dve_out2.close(4)
            with nc.Block() as block:
                @block.scalar
                def _(act):
                    for t in range(4):
                        act.wait_ge(dve_out.sem, dve_out.at(t + 1))
                        e = w[:, EE + t, :]
                        S.activation(e, e, ACT.Exp).then_inc(act_out.sem, 1)
                    for t in range(4):
                        act.wait_ge(dve_out2.sem, dve_out2.at(t + 1))
                        e, cm = w[:, EE + t, :], w[:, CM + t, :]
                        S.activation(e, cm, ACT.Exp, scale=-1.0).then_inc(act_out.sem, 1)
                        act_chain.link(act, S.activation(cm, cm, ACT.Exp))
                        S.activation(col[:, 32 + 4 * t:36 + 4 * t], cm[:, P - 1::P], ACT.Copy).then_inc(act_out2.sem, 1)
                    act.wait_ge(dve_out2.sem, dve_out2.at(4))
                    S.activation(col[:, 16:32], col[:, 16:32], ACT.Exp).then_inc(act_out2.sem, 1)

                @block.vector
                def _(dve):
                    for t in range(4):
                        e = w[:, EE + t, :]
                        dve_chain.link(dve, V.tensor_tensor(e, w[:, CM + t, :], w[:, LW + t, :], ALU.subtract))
                        V.tensor_scalar(col[:, 16 + 4 * t:20 + 4 * t], e[:, 0::P], -1.0, None,
                                        ALU.mult).then_inc(dve_out.sem, 1)
                    for t in range(4):
                        kk = w[:, KK + t, :]
                        dve.wait_ge(act_out.sem, act_out.at(t + 1))
                        dve_chain.link(dve, V.scalar_tensor_tensor(w[:, AT + t, :], kk, -1.0, w[:, EE + t, :],
                                                                   ALU.mult, ALU.mult))
                        V.tensor_tensor(kk, kk, w[:, AA + t, :], ALU.mult).then_inc(dve_out2.sem, 1)
                    dve.wait_ge(dve_out2.sem, dve_out2.at(4))
                    for t in range(4):
                        e = w[:, EE + t, :]
                        dve.wait_ge(act_out.sem, act_out.at(5 + t))
                        V.tensor_tensor(w[:, KK + t, :], w[:, KK + t, :], e, ALU.mult)
                        V.tensor_tensor(w[:, K + t, :], w[:, K + t, :], e, ALU.mult)
                        dve.wait_ge(act_out2.sem, act_out2.at(t + 1))
                        dve_chain.link(dve, V.tensor_tensor(w[:, R + t, :], w[:, R + t, :], w[:, CM + t, :], ALU.mult))
            act_out.close(8)
            act_out2.close(5)
            dve_out.close(4)
            dve_out2.close(4)

        BT, KT, VT = LW, CM, AA
        N4 = VV
        UU, TT, XX, GS = EE, EE + 1, EE + 2, EE + 3
        ZS = CW

        def stage_rwkv_chunks():
            batches = [(hg, ch) for hg in range(2) for ch in range(NT)]
            n_b = len(batches)

            def n4(i, j):
                return w[:, N4 + i, j * P:(j + 1) * P]

            def part(tile, i):
                return w[:, tile, i * P:(i + 1) * P]

            def quad(ap):
                return ap.rearrange("p (a t) -> p a t", a=4)

            def wide(m):
                return m.unsqueeze(1).to_broadcast([P, 4, P])

            z = w[:, ZS, :]
            with nc.Block() as block:
                @block.vector
                def _(dve):
                    for i in range(4):
                        V.memset(w[:, N4 + i, :], 0.0)
                    dve_chain.link(dve, V.memset(z, 0.0))
            per_t = 1 + 2 * (LEVELS - 1) + 3

            with nc.Block() as block:
                @block.tensor
                def _(pe):
                    for b, (hg, ch) in enumerate(batches):
                        s = slice(ch * P, (ch + 1) * P)
                        d0 = b * per_d
                        if b >= 1:
                            pe.wait_ge(dve_out.sem, dve_out.at(d0))
                        for i in range(4):
                            hd = 4 * hg + i
                            t, r = hd // 2, half(hd)
                            a, rr = w[r, AT + t, s], w[r, R + t, s]
                            bt, kt = w[r, KK + t, s], w[r, K + t, s]
                            for j, (lhs, rhs) in enumerate(((bt, a), (bt, rr), (kt, a), (kt, rr))):
                                ins = TE.matmul(bank(i, j * P, P), lhs, rhs, start=True, stop=True)
                            ins.then_inc(pe_out.sem, 1)
                        pe.wait_ge(dve_out.sem, dve_out.at(d0 + 1))
                        for i in range(4):
                            ins = TE.transpose(bank(4, i * P, P), part(UU, i), ident)
                        ins.then_inc(tile_ready.sem, 1)
                        for l in range(1, LEVELS):
                            pe.wait_ge(dve_out.sem, dve_out.at(d0 + 2 * l))
                            for i in range(4):
                                ins = TE.matmul(bank(5, i * P, P), n4(i, 0), part(TT, i), start=True, stop=True)
                            ins.then_inc(tile_ready.sem, 1)
                            pe.wait_ge(dve_out.sem, dve_out.at(d0 + 2 * l + 1))
                            if l < LEVELS - 1:
                                for i in range(4):
                                    TE.matmul(bank(4, i * P, P), part(UU, i), part(XX, i), start=True, stop=True)
                            for i in range(4):
                                ins = TE.matmul(bank(6, i * P, P), part(XX, i), part(UU, i), start=True, stop=True)
                            ins.then_inc(tile_ready.sem, 1)
                        pe.wait_ge(dve_out.sem, dve_out.at(d0 + 2 * LEVELS))
                        for i in range(4):
                            hd = 4 * hg + i
                            t, r = hd // 2, half(hd)
                            g = bank(7 - i % 2, (i // 2) * HD, HD)
                            vh = w[:, VT + ch, hd * HD:(hd + 1) * HD]
                            TE.matmul(g, w[r, AT + t, s], z[r, t * HD:(t + 1) * HD], start=True, stop=False)
                            ins = TE.matmul(g, n4(i, 2), vh, start=False, stop=True)
                        ins.then_inc(tile_ready.sem, 1)
                        pe.wait_ge(dve_out.sem, dve_out.at(d0 + 2 * LEVELS + 1))
                        for i in range(4):
                            ins = TE.matmul(bank(5, i * HD, HD), part(UU, i), w[:, GS, i * HD:(i + 1) * HD],
                                            start=True, stop=True)
                        ins.then_inc(tile_ready.sem, 1)
                        pe.wait_ge(dve_out.sem, dve_out.at(d0 + 2 * LEVELS + 2))
                        for i in range(4):
                            hd = 4 * hg + i
                            t, r = hd // 2, half(hd)
                            vh = w[:, VT + ch, hd * HD:(hd + 1) * HD]
                            sa = w[:, GS, 256 + i * HD:256 + (i + 1) * HD]
                            y = bank(4, (i // 2) * P, P, r)
                            TE.matmul(y, z[r, t * HD:(t + 1) * HD], w[r, R + t, s], start=True, stop=False)
                            TE.matmul(y, sa, n4(i, 1), start=False, stop=False)
                            TE.matmul(y, vh, n4(i, 3), start=False, stop=True)
                            zz = bank(6, (i // 2) * HD, HD, r)
                            TE.matmul(zz, w[:, BT + ch, hd * HD:(hd + 1) * HD], sa, start=True, stop=False)
                            ins = TE.matmul(zz, w[:, KT + ch, hd * HD:(hd + 1) * HD], vh, start=False, stop=True)
                        ins.then_inc(tile_ready.sem, 1)

                @block.vector
                def _(dve):
                    for b, (hg, ch) in enumerate(batches):
                        s = slice(ch * P, (ch + 1) * P)
                        r0 = b * per_t
                        for i in range(4):
                            dve.wait_ge(pe_out.sem, pe_out.at(4 * b + i + 1))
                            dve_chain.link(dve, V.copy_predicated(w[:, N4 + i, :], c("mask4").bitcast(I32), bank(i)))
                        uu, tt, xx = quad(w[:, UU, :]), quad(w[:, TT, :]), quad(w[:, XX, :])
                        first = w[:, N4:N4 + 4, 0:P]
                        dve_chain.link(dve, V.tensor_tensor(uu, first, wide(c("level0_t")), ALU.mult))
                        zt = z[:, 2 * hg * HD:2 * (hg + 1) * HD].rearrange("p (a d) -> p a d", d=HD)
                        before = col[:, 16 + 8 * hg + ch:16 + 8 * hg + ch + 5:4].unsqueeze(2).to_broadcast([P, 2, HD])
                        after = col[:, 32 + 8 * hg + ch:32 + 8 * hg + ch + 5:4].unsqueeze(2).to_broadcast([P, 2, HD])
                        dve_chain.link(dve, V.tensor_tensor(zt, zt, before, ALU.mult))
                        V.tensor_tensor(uu, uu, wide(ident), ALU.add).then_inc(dve_out.sem, 1)
                        dve.wait_ge(tile_ready.sem, tile_ready.at(r0 + 1))
                        V.tensor_copy(w[:, TT, :], bank(4)).then_inc(dve_out.sem, 1)
                        for l in range(1, LEVELS):
                            dve.wait_ge(tile_ready.sem, tile_ready.at(r0 + 2 * l))
                            V.tensor_tensor(xx, quad(bank(5)), wide(c("levels", l * P, P)),
                                            ALU.mult).then_inc(dve_out.sem, 1)
                            dve.wait_ge(tile_ready.sem, tile_ready.at(r0 + 2 * l + 1))
                            if l < LEVELS - 1:
                                V.tensor_tensor(w[:, TT, :], w[:, TT, :], bank(4), ALU.add)
                            V.tensor_tensor(w[:, UU, :], w[:, UU, :], bank(6), ALU.add).then_inc(dve_out.sem, 1)
                        dve.wait_ge(tile_ready.sem, tile_ready.at(r0 + 2 * LEVELS))
                        g = w[:, GS, 0:256].rearrange("p (a b d) -> p a b d", a=2, b=2)
                        V.tensor_copy(g[:, :, 0, :], bank(7, 0, P).rearrange("p (a d) -> p a d", d=HD))
                        V.tensor_copy(g[:, :, 1, :], bank(6, 0, P).rearrange("p (a d) -> p a d", d=HD)
                                      ).then_inc(dve_out.sem, 1)
                        dve.wait_ge(tile_ready.sem, tile_ready.at(r0 + 2 * LEVELS + 1))
                        V.tensor_copy(w[:, GS, 256:512], bank(5, 0, 256)).then_inc(dve_out.sem, 1)
                        dve.wait_ge(tile_ready.sem, tile_ready.at(r0 + 2 * LEVELS + 2))
                        for j in range(2):
                            V.tensor_copy(w[:, YB + 2 * hg + j, s], bank(4, j * P, P))
                        dve_chain.link(dve, V.tensor_tensor(
                            zt, zt, bank(6, 0, P).rearrange("p (a d) -> p a d", d=HD), ALU.add))
                        V.tensor_tensor(zt, zt, after, ALU.mult).then_inc(dve_out.sem, 1)
                        dve.wait_ge(dve_out.sem, dve_out.at((b + 1) * per_d))
            pe_out.close(4 * n_b)
            tile_ready.close(per_t * n_b)
            dve_out.close(per_d * n_b)

        per_d = 2 + 2 * (LEVELS - 1) + 3

        def stage_rwkv_out():
            norm(wt(YB), [[0], [1], [2], [3]], HD, GN_EPS, lambda t: v("ln_x_w", t), wt(YB), c("same_head"),
                 centre=True, bias=lambda t: v("ln_x_b", t), sq0=0)
            with nc.Block() as block:
                @block.vector
                def _(dve):
                    for t in range(4):
                        y = w[:, YB + t, :]
                        dve_chain.link(dve, V.tensor_tensor(y, y, w[:, BO + t, :], ALU.add))
                        dve_chain.link(dve, V.tensor_tensor(y, y, w[:, GG + t, :], ALU.mult))

        MG = 0

        def stage_merge():
            with nc.Block() as block:
                @block.tensor
                def _(pe):
                    for m in range(KD):
                        for j, (n_k, src) in enumerate(((KD, ht), (KD, ht), (KH, wt(YA)), (KH, wt(YB)))):
                            n = 4 * m + j
                            b = n % 8
                            if n >= 8:
                                if j < 2:
                                    pe.wait_ge(tile_read.sem, tile_read.at(2 * (m - 2) + j + 1))
                                else:
                                    pe.wait_ge(dve_out.sem, dve_out.at(2 * (m - 2) + j - 1))
                            for k in range(n_k):
                                ins = TE.matmul(bank(b), wts.take(pe), src(k), start=(k == 0), stop=(k == n_k - 1))
                                wts.free(ins, tile_ready if k == n_k - 1 else None, n + 1)
                            ins.then_inc(tile_ready.sem, 1)

                @block.sync
                def _(sp):
                    wts.load(sp)

                @block.scalar
                def _(act):
                    for m in range(KD):
                        for j in range(2):
                            n = 4 * m + j
                            act.wait_ge(tile_ready.sem, tile_ready.at(n + 1))
                            if m >= 2:
                                act.wait_ge(dve_out.sem, dve_out.at(2 * (m - 2) + j + 1))
                            S.activation(w[:, 8 + 2 * (m % 2) + j if m % 2 == 0 else 18 + j, :], bank(n % 8),
                                         ACT.Sigmoid, bias=v("gate_bias", 8 * j + m)).then_inc(tile_read.sem, 1)

                @block.vector
                def _(dve):
                    for m in range(KD):
                        ga = w[:, 8 if m % 2 == 0 else 18, :]
                        gb = w[:, 9 if m % 2 == 0 else 19, :]
                        dve.wait_ge(tile_ready.sem, tile_ready.at(4 * m + 3))
                        dve.wait_ge(tile_read.sem, tile_read.at(2 * m + 1))
                        V.tensor_tensor(w[:, MG + m, :], bank((4 * m + 2) % 8), ga, ALU.mult).then_inc(dve_out.sem, 1)
                        dve.wait_ge(tile_ready.sem, tile_ready.at(4 * m + 4))
                        dve.wait_ge(tile_read.sem, tile_read.at(2 * m + 2))
                        dve_chain.link(dve, V.tensor_tensor(gb, bank((4 * m + 3) % 8), gb, ALU.mult))
                        dve.wait_ge(dve_out.sem, dve_out.at(2 * m + 1))
                        V.tensor_tensor(w[:, MG + m, :], w[:, MG + m, :], gb, ALU.add).then_inc(dve_out.sem, 1)
            tile_ready.close(4 * KD)
            tile_read.close(2 * KD)
            dve_out.close(2 * KD)

        def stage_linear(n_k, src, out, residual=False):
            with nc.Block() as block:
                @block.tensor
                def _(pe):
                    product(pe, KD, n_k, src)

                @block.sync
                def _(sp):
                    wts.load(sp)

                if residual:
                    @block.vector
                    def _(dve):
                        for m in range(KD):
                            dve.wait_ge(tile_ready.sem, tile_ready.at(m + 1))
                            V.scalar_tensor_tensor(xt(m), xt(m), ALPHA, bank(m % 4), ALU.mult,
                                                   ALU.add).then_inc(tile_read.sem, 1)
                else:
                    @block.scalar
                    def _(act):
                        for m in range(KD):
                            act.wait_ge(tile_ready.sem, tile_ready.at(m + 1))
                            S.activation(out(m), bank(m % 4), ACT.Copy).then_inc(tile_read.sem, 1)
            tile_ready.close(KD)
            tile_read.close(KD)

        def stage_relu2_up():
            with nc.Block() as block:
                @block.tensor
                def _(pe):
                    product(pe, FF1, KD, ht)

                @block.sync
                def _(sp):
                    wts.load(sp)

                @block.scalar
                def _(act):
                    for m in range(FF1):
                        act.wait_ge(tile_ready.sem, tile_ready.at(m + 1))
                        S.activation(w[:, m, :], bank(m % 4), ACT.Relu).then_inc(tile_read.sem, 1)

                @block.vector
                def _(dve):
                    for m in range(FF1):
                        dve.wait_ge(tile_read.sem, tile_read.at(m + 1))
                        V.tensor_tensor(w[:, m, :], w[:, m, :], w[:, m, :], ALU.mult)
            tile_ready.close(FF1)
            tile_read.close(FF1)

        ROWS = 40
        HM, HF2 = 28, 32

        def stage_even_in():
            scale = {0: float(P) ** -0.5, 4: HD ** -0.5}
            with nc.Block() as block:
                @block.tensor
                def _(pe):
                    product(pe, 28, KD, xt)
                    for j, (a, n) in enumerate(((0, 4), (4, 4), (8, 8))):
                        for k in range(KD):
                            g = v("ev_gates", 16 * k + a, n)
                            ins = TE.matmul(ps[0:n, 4 + j, :], g, xt(k), start=(k == 0), stop=(k == KD - 1))
                        ins.then_inc(pe_out.sem, 1)

                @block.sync
                def _(sp):
                    wts.load(sp)

                @block.vector
                def _(dve):
                    for m in range(28):
                        dve.wait_ge(tile_ready.sem, tile_ready.at(m + 1))
                        V.tensor_scalar(w[:, m, :], bank(m % 4), v("ev_b", m), scale.get(m // 4, 1.0), ALU.add,
                                        ALU.mult).then_inc(tile_read.sem, 1)
                    dve.wait_ge(pe_out.sem, pe_out.at(3))
                    for j, (n, b) in enumerate(((4, "ev_bi"), (4, "ev_bf"), (8, "ev_bff"))):
                        dve_chain.link(dve, V.tensor_scalar(w[0:n, ROWS + j, :], ps[0:n, 4 + j, :], v(b, rows=n), None,
                                                            ALU.add))
                    for j, n in ((1, 4), (2, 8)):
                        z, tmp, out = (w[0:n, ROWS + j + a, :] for a in (0, 3, 5))
                        dve_chain.link(dve, V.tensor_scalar(tmp, z, -1.0, None, ALU.mult))
                        V.tensor_tensor(tmp, z, tmp, ALU.max).then_inc(dve_out.sem, 1)
                        dve.wait_ge(act_out.sem, act_out.at(j))
                        dve_chain.link(dve, V.tensor_scalar(out, z, 0.0, None, ALU.min))
                        dve_chain.link(dve, V.tensor_tensor(out, out, tmp, ALU.subtract))
                        dve_chain.link(dve, V.tensor_tensor_scan(z, ones[0:n, :], out, 0.0, ALU.mult, ALU.add))
                    V.tensor_tensor(w[0:4, ROWS, :], w[0:4, ROWS, :], w[0:4, ROWS + 1, :], ALU.subtract)
                    dve_chain.link(dve, V.tensor_scalar(w[0:8, ROWS + 3, :], w[0:8, ROWS + 2, :], -1.0, None, ALU.mult))

                @block.scalar
                def _(act):
                    for j, n in ((1, 4), (2, 8)):
                        tmp = w[0:n, ROWS + j + 3, :]
                        act.wait_ge(dve_out.sem, dve_out.at(j))
                        act_chain.link(act, S.activation(tmp, tmp, ACT.Exp, scale=-1.0))
                        S.activation(tmp, tmp, ACT.Ln, bias=ones[0:n, 0:1]).then_inc(act_out.sem, 1)
            tile_ready.close(28)
            tile_read.close(28)
            pe_out.close(3)
            act_out.close(2)
            dve_out.close(2)
            with nc.Block() as block:
                @block.tensor
                def _(pe):
                    for i in range(NT):
                        ins = TE.matmul(bank(0, 4 * i, 4), w[0:4, ROWS + 1, tok(0, i)], c("ident", 0, 4, rows=4),
                                        start=True, stop=True)
                    ins.then_inc(tile_ready.sem, 1)

                @block.vector
                def _(dve):
                    dve.wait_ge(tile_ready.sem, tile_ready.at(1))
                    dve_chain.link(dve, V.tensor_copy(col[:, 16:32], bank(0, 0, 16)))
            tile_ready.close(1)

        def stage_ml_gate():
            with nc.Block() as block:
                @block.scalar
                def _(act):
                    for t in range(4):
                        S.activation(w[:, 12 + t, :], w[:, 12 + t, :], ACT.Sigmoid).then_inc(act_out.sem, 1)

                @block.vector
                def _(dve):
                    for t in range(4):
                        dve.wait_ge(act_out.sem, act_out.at(t + 1))
                        V.tensor_tensor(w[:, HM + t, :], w[:, HM + t, :], w[:, 12 + t, :], ALU.mult)
            act_out.close(4)

        def stage_conv_ffn_up(layer):
            y0 = FF2 + 0
            with nc.Block() as block:
                @block.tensor
                def _(pe):
                    product(pe, 2 * FF2, KD, xt)

                @block.sync
                def _(sp):
                    wts.load(sp)

                def taps(m):
                    ch = layer * 132 + (m % 2) * FF2 + m // 2
                    return [v("ffn_w", ch + 44 * i) for i in range(3)]

                @block.scalar
                def _(act):
                    def gate(m):
                        act.wait_ge(tile_read.sem, tile_read.at(m + 1))
                        S.activation(w[:, y0 + 4 + (m // 2) % 2, :], w[:, y0 + m % 4, :], ACT.Sigmoid
                                     ).then_inc(act_out2.sem, 1)
                    for m in range(2 * FF2):
                        act.wait_ge(tile_ready.sem, tile_ready.at(m + 1))
                        if m >= 4:
                            act.wait_ge(dve_out2.sem, dve_out2.at((m - 4) // 2 + 1))
                        S.activation(w[:, y0 + m % 4, :], bank(m % 4), ACT.Identity, scale=taps(m)[2],
                                     bias=v("ffn_b", layer * 44 + (m % 2) * FF2 + m // 2)).then_inc(act_out.sem, 1)
                        if m % 2 == 0 and m >= 2:
                            gate(m - 1)
                    gate(2 * FF2 - 1)

                @block.vector
                def _(dve):
                    def conv(m):
                        y, b = w[:, y0 + m % 4, :], bank(m % 4)
                        dve.wait_ge(act_out.sem, act_out.at(m + 1))
                        dve_chain.link(dve, V.scalar_tensor_tensor(y[:, 1:T], b[:, 0:T - 1], taps(m)[1], y[:, 1:T],
                                                                   ALU.mult, ALU.add))
                        V.scalar_tensor_tensor(y[:, 2:T], b[:, 0:T - 2], taps(m)[0], y[:, 2:T], ALU.mult,
                                               ALU.add).then_inc(tile_read.sem, 1)

                    def join(j):
                        dve.wait_ge(act_out2.sem, act_out2.at(j + 1))
                        sg = w[:, y0 + 4 + j % 2, :]
                        dve_chain.link(dve, V.tensor_tensor(sg, sg, w[:, y0 + (2 * j + 1) % 4, :], ALU.mult))
                        V.tensor_tensor(w[:, j, :], sg, w[:, y0 + 2 * j % 4, :], ALU.mult).then_inc(dve_out2.sem, 1)

                    for m in range(2 * FF2):
                        conv(m)
                        if m % 2 == 0 and m >= 2:
                            join(m // 2 - 1)
                    join(FF2 - 1)
            tile_ready.close(2 * FF2)
            tile_read.close(2 * FF2)
            act_out.close(2 * FF2)
            act_out2.close(FF2)
            dve_out2.close(FF2)

        def layer_norm(name, layer):
            norm(xt, [list(range(KD))], D, LN_EPS, lambda t: v(name + "_g", KD * layer + t), xt, ones[:, 0:P],
                 centre=True, bias=lambda t: v(name + "_b", KD * layer + t), sq0=46)

        ZG, XS, BM, CMM, PL = 0, 4, 8, 10, 12
        XTK, YS, PO = 16, 20, 24

        def stage_odd_in():
            y0 = 46
            with nc.Block() as block:
                @block.tensor
                def _(pe):
                    product(pe, 16, KD, xt)
                    for k in range(KD):
                        ins = TE.matmul(ps[0:8, 4, :], v("od_dt", 8 * k, 8), xt(k), start=(k == 0), stop=(k == KD - 1))
                    ins.then_inc(pe_out.sem, 1)

                @block.sync
                def _(sp):
                    wts.load(sp)

                @block.scalar
                def _(act):
                    for m in range(4, 12):
                        act.wait_ge(tile_ready.sem, tile_ready.at(m + 1))
                        S.activation(w[:, m, :], bank(m % 4), ACT.Identity, scale=v("conv_w", 24 + m - 4),
                                     bias=v("conv_b", m - 4)).then_inc(act_out.sem, 1)
                        act.wait_ge(tile_read.sem, tile_read.at(m + 1))
                        S.activation(w[:, y0 + m % 2, :], w[:, m, :], ACT.Sigmoid).then_inc(act_out2.sem, 1)

                @block.vector
                def _(dve):
                    for m in range(16):
                        y, b = w[:, m, :], bank(m % 4)
                        dve.wait_ge(tile_ready.sem, tile_ready.at(m + 1))
                        if 4 <= m < 12:
                            dve.wait_ge(act_out.sem, act_out.at(m - 3))
                            for i, s in ((2, 1), (1, 2), (0, 3)):
                                ins = V.scalar_tensor_tensor(y[:, s:T], b[:, 0:T - s], v("conv_w", 8 * i + m - 4),
                                                             y[:, s:T], ALU.mult, ALU.add)
                                if i:
                                    dve_chain.link(dve, ins)
                            ins.then_inc(tile_read.sem, 1)
                            dve.wait_ge(act_out2.sem, act_out2.at(m - 3))
                            dve_chain.link(dve, V.tensor_tensor(y, y, w[:, y0 + m % 2, :], ALU.mult))
                        else:
                            V.tensor_copy(y, b).then_inc(tile_read.sem, 1)
            tile_ready.close(16)
            tile_read.close(16)
            act_out.close(8)
            act_out2.close(8)
            dt, tmp, acs, ncs = (w[0:8, ROWS + i, :] for i in range(4))
            with nc.Block() as block:
                @block.vector
                def _(dve):
                    dve.wait_ge(pe_out.sem, pe_out.at(1))
                    dve_chain.link(dve, V.tensor_scalar(acs, ps[0:8, 4, :], v("dt_bias", rows=8), None, ALU.add))
                    dve_chain.link(dve, V.tensor_scalar(tmp, acs, -1.0, None, ALU.mult))
                    V.tensor_tensor(tmp, acs, tmp, ALU.max).then_inc(dve_out.sem, 1)
                    dve.wait_ge(act_out.sem, act_out.at(1))
                    dve_chain.link(dve, V.tensor_scalar(dt, acs, 0.0, None, ALU.max))
                    dve_chain.link(dve, V.tensor_tensor(dt, dt, tmp, ALU.add))
                    dve_chain.link(dve, V.tensor_scalar(tmp, dt, col[0:8, 8:9], -1.0, ALU.mult, ALU.mult))
                    dve_chain.link(dve, V.tensor_tensor_scan(acs, ones[0:8, :], tmp, 0.0, ALU.mult, ALU.add))
                    dve_chain.link(dve, V.tensor_scalar(ncs, acs, -1.0, None, ALU.mult))

                @block.scalar
                def _(act):
                    act_chain.link(act, S.activation(col[0:8, 8:9], v("a_log", rows=8), ACT.Exp))
                    act.wait_ge(dve_out.sem, dve_out.at(1))
                    act_chain.link(act, S.activation(tmp, tmp, ACT.Exp, scale=-1.0))
                    S.activation(tmp, tmp, ACT.Ln, bias=ones[0:8, 0:1]).then_inc(act_out.sem, 1)
            pe_out.close(1)
            dve_out.close(1)
            act_out.close(1)
            with nc.Block() as block:
                @block.tensor
                def _(pe):
                    for i in range(NT):
                        ins = TE.matmul(bank(0, 8 * i, 8), w[0:8, ROWS, tok(0, i)], c("ident", 0, 8, rows=8),
                                        start=True, stop=True)
                    ins.then_inc(tile_ready.sem, 1)

                @block.vector
                def _(dve):
                    dve.wait_ge(tile_ready.sem, tile_ready.at(1))
                    dve_chain.link(dve, V.tensor_copy(col[:, 16:48], bank(0, 0, 32)))
            tile_ready.close(1)

        def stage_ssd():
            items = [(g, j, hh) for g in range(2) for j in range(NT) for hh in range(4)]
            n_items = len(items)
            acs, ncs = w[0:8, ROWS + 2, :], w[0:8, ROWS + 3, :]
            e = [w[:, 46, :], w[:, 47, :]]
            m_ = [w[:, 48, :], w[:, 49, :]]
            with nc.Block() as block:
                @block.tensor
                def _(pe):
                    def decay(n):
                        g, j, hh = items[n]
                        a, wd = j * P, T - j * P
                        hd = 4 * g + hh
                        if hh == 0:
                            if n >= 8:
                                pe.wait_ge(dve_out.sem, dve_out.at(n - 4))
                            TE.matmul(bank((n // 4) % 2, 0, wd), w[:, BM + g, a:a + P], w[:, CMM + g, a:T],
                                      start=True, stop=True)
                        if n >= 2:
                            pe.wait_ge(act_out.sem, act_out.at(n - 1))
                        d = bank(2 + n % 2, 0, wd)
                        sel = c("ident", hd, 1, rows=8)
                        TE.matmul(d, sel.to_broadcast([8, P]), acs[:, a:T], start=True, stop=False)
                        TE.matmul(d, ncs[:, a:a + P], sel.to_broadcast([8, wd]), start=False, stop=False)
                        TE.matmul(bank(2 + n % 2, 0, P), ident, c("diag_st"), start=False,
                                  stop=True).then_inc(tile_ready.sem, 1)

                    def values(n):
                        g, j, hh = items[n]
                        hd = 4 * g + hh
                        pe.wait_ge(dve_out.sem, dve_out.at(n + 1))
                        TE.matmul(bank(4 + hd // 2, j * P, T - j * P, half(hd)), w[:, XTK + j, hd * HD:(hd + 1) * HD],
                                  m_[n % 2][:, 0:T - j * P], start=(j == 0), stop=(j == NT - 1)
                                  ).then_inc(pe_out.sem, 1)

                    decay(0)
                    for n in range(n_items):
                        if n + 1 < n_items:
                            decay(n + 1)
                        values(n)

                @block.scalar
                def _(act):
                    for n, (g, j, hh) in enumerate(items):
                        wd = T - j * P
                        act.wait_ge(tile_ready.sem, tile_ready.at(n + 1))
                        if n >= 2:
                            act.wait_ge(dve_out.sem, dve_out.at(n - 1))
                        S.activation(e[n % 2][:, 0:wd], bank(2 + n % 2, 0, wd), ACT.Exp).then_inc(act_out.sem, 1)
                    for t in range(4):
                        S.activation(w[:, 50 + t, :], w[:, ZG + t, :], ACT.Sigmoid).then_inc(act_out2.sem, 1)

                @block.vector
                def _(dve):
                    for n, (g, j, hh) in enumerate(items):
                        wd = T - j * P
                        dve.wait_ge(act_out.sem, act_out.at(n + 1))
                        if n >= 2:
                            dve.wait_ge(pe_out.sem, pe_out.at(n - 1))
                        V.tensor_tensor(m_[n % 2][:, 0:wd], bank((n // 4) % 2, 0, wd), e[n % 2][:, 0:wd],
                                        ALU.mult).then_inc(dve_out.sem, 1)
                    dve.wait_ge(pe_out.sem, pe_out.at(n_items))
                    for t in range(4):
                        y, z = w[:, YS + t, :], w[:, ZG + t, :]
                        dve_chain.link(dve, V.scalar_tensor_tensor(y, w[:, XS + t, :], v("d_skip", t), bank(4 + t),
                                                                   ALU.mult, ALU.add))
                        dve.wait_ge(act_out2.sem, act_out2.at(t + 1))
                        dve_chain.link(dve, V.tensor_tensor(z, z, w[:, 50 + t, :], ALU.mult))
                        dve_chain.link(dve, V.tensor_tensor(y, y, z, ALU.mult))
            tile_ready.close(n_items)
            pe_out.close(n_items)
            act_out.close(n_items)
            act_out2.close(4)
            dve_out.close(n_items)

        def stage_pool():
            with nc.Block() as block:
                @block.vector
                def _(dve):
                    for g, win in enumerate(WINDOWS):
                        u = w[:, PL + g, :]
                        a, b = w[:, PO + g, :], w[:, 28 + g, :]
                        src, s = u, 1
                        while s < win:
                            dst = a if src is not a else b
                            V.tensor_copy(dst[:, 0:s], src[:, 0:s])
                            dve_chain.link(dve, V.tensor_tensor(dst[:, s:T], src[:, s:T], src[:, 0:T - s], ALU.add))
                            src, s = dst, 2 * s
                        V.tensor_scalar(src[:, 16:T], src[:, 16:T], 1.0 / win, None, ALU.mult)
                        dve_chain.link(dve, V.tensor_tensor(src[:, 0:16], src[:, 0:16], c("inv_count", 16 * g, 16),
                                                            ALU.mult))
                        V.tensor_tensor(a, src, u, ALU.subtract).then_inc(dve_out.sem, 1)
                        dve.wait_ge(dve_out.sem, dve_out.at(g + 1))
                    for g in range(4):
                        dve.wait_ge(tile_ready.sem, tile_ready.at(g + 1))
                        dve_chain.link(dve, V.tensor_scalar(w[:, PO + g, :], bank(g), v("pool_b", g),
                                                            v("pool_scale", g), ALU.add, ALU.mult))

                @block.tensor
                def _(pe):
                    for g in range(4):
                        pe.wait_ge(dve_out.sem, dve_out.at(g + 1))
                        TE.matmul(bank(g), v("pool_w", g * P, P), w[:, PO + g, :], start=True,
                                  stop=True).then_inc(tile_ready.sem, 1)
            dve_out.close(4)
            tile_ready.close(4)

        def stage_store():
            with nc.Block() as block:
                @block.sync
                def _(sp):
                    sp.dma_start(out_t.rearrange("(k p) t -> p k t", p=P), x[:, :, :]).then_inc(dma_out.sem, 16)
                    sp.wait_ge(dma_out.sem, dma_out.at(16))
            dma_out.close(16)

        all_d = ones[:, 0:P]
        tiles8 = [list(range(KD))]
        steps = [
            ("inputs", stage_inputs),
            ("norm1", lambda: norm(xt, tiles8, D, RMS_EPS, lambda t: v("pre_mix_g", t), ht, all_d, sq0=30)),
            ("qkv", stage_qkv),
            ("v_tok", lambda: to_token_major([(8, 28)])),
            ("band", lambda: attention("band", 0, 4, 28, YA, 32, bias0=20)),
            ("rwkv_in", stage_rwkv_in),
            ("rwkv_prep", stage_rwkv_prepare),
            ("rwkv_tok", lambda: to_token_major([(KK, BT), (K, KT), (VV, VT)])),
            ("rwkv_chunks", stage_rwkv_chunks),
            ("rwkv_out", stage_rwkv_out),
            ("merge", stage_merge),
            ("w_out", lambda: stage_linear(KD, wt(MG), wt(20))),
            ("post_mix", lambda: norm(wt(20), tiles8, D, RMS_EPS, lambda t: v("post_mix_g", t), None, all_d,
                                      add_to=xt, sq0=30)),
            ("pre_ffn", lambda: norm(xt, tiles8, D, RMS_EPS, lambda t: v("pre_ffn_g", t), ht, all_d, sq0=30)),
            ("up", stage_relu2_up),
            ("down", lambda: stage_linear(FF1, wt(0), wt(32))),
            ("post_ffn", lambda: norm(wt(32), tiles8, D, RMS_EPS, lambda t: v("post_ffn_g", t), None, all_d,
                                      add_to=xt, sq0=0)),
            ("even_in", stage_even_in),
            ("ml_tok", lambda: to_token_major([(8, 46), (24, 50)])),
            ("mlstm", lambda: attention("mlstm", 0, 4, 46, HM, 54, f_rows=w[0:4, ROWS + 1, :],
                                        g_rows=w[0:4, ROWS, :], f_cols=lambda i, hd: col[:, 16 + 4 * i + hd:17 + 4 * i + hd])),
            ("ml_norm", lambda: norm(wt(HM), [[0], [1], [2], [3]], P, LN_EPS, lambda t: v("ml_norm", t), wt(HM),
                                     all_d, centre=True, sq0=0)),
            ("ml_gate", stage_ml_gate),
            ("forget", lambda: attention("forget", 16, 20, 50, HF2, 54, f_rows=w[0:8, ROWS + 2, :],
                                         g_rows=w[0:8, ROWS + 3, :])),
            ("even_out", lambda: stage_linear(KD, wt(HM), None, residual=True)),
            ("ln1_0", lambda: layer_norm("ln1", 0)),
            ("ffn_up_0", lambda: stage_conv_ffn_up(0)),
            ("ffn_down_0", lambda: stage_linear(FF2, wt(0), None, residual=True)),
            ("ln2_0", lambda: layer_norm("ln2", 0)),
            ("odd_in", stage_odd_in),
            ("x_tok", lambda: to_token_major([(XS, XTK)], scaled=lambda i: col[:, 16 + 8 * i:24 + 8 * i])),
            ("ssd", stage_ssd),
            ("ssm_norm", lambda: norm(wt(YS), [[0, 1, 2, 3]], HALF, LN_EPS, lambda t: v("ssm_norm", t), wt(YS),
                                      all_d, sq0=28)),
            ("pool", stage_pool),
            ("odd_out", lambda: stage_linear(KD, wt(YS), None, residual=True)),
            ("ln1_1", lambda: layer_norm("ln1", 1)),
            ("ffn_up_1", lambda: stage_conv_ffn_up(1)),
            ("ffn_down_1", lambda: stage_linear(FF2, wt(0), None, residual=True)),
            ("ln2_1", lambda: layer_norm("ln2", 1)),
        ]
        for name, run in steps:
            run()
            if name == upto:
                break
        stage_store()
        if upto is None:
            assert wts.block == n_units * UNIT, (wts.block, n_units * UNIT)


def blocks(m):
    k, n = m.shape
    return m.reshape(k // P, P, n // P, P).transpose(2, 0, 1, 3).reshape(-1, P, P)


def weight_stream(a):
    w_in, ev, od = a["w_in"][0], a["ev_w_in_2"][0], a["od_w_in_2"][0]
    gates = blocks(w_in[:, 3328:]).reshape(2, KD, KD, P, P)
    pa, pb = (blocks(a[n][0]).reshape(KD, KH, P, P) for n in ("proj_a", "proj_b"))
    parts = [blocks(w_in[:, :3328])]
    for m in range(KD):
        parts += [gates[0, m], gates[1, m], pa[m], pb[m]]
    parts += [blocks(a["w_out"][0]), blocks(a["w_up"][0]), blocks(a["w_down"][0]),
              blocks(ev[:, 0:2048]), blocks(ev[:, 2056:3592]), blocks(a["ev_w_out_2"][0])]

    def ffn(layer):
        up = blocks(a["ffn_w_up_2"][layer]).reshape(2, FF2, KD, P, P).transpose(1, 0, 2, 3, 4)
        return [up.reshape(-1, P, P), blocks(a["ffn_w_down_2"][layer])]

    parts += ffn(0)
    parts += [blocks(od[:, 0:1536]), blocks(od[:, 1544:2056]), blocks(a["od_w_out_2"][0])]
    parts += ffn(1)
    flat = np.concatenate(parts)
    return np.ascontiguousarray(flat.reshape(-1, UNIT, P, P).transpose(0, 2, 1, 3)).reshape(-1, P, UNIT * P)


def vector_array(a):
    cols, n = columns(VECTORS)
    out = np.zeros((P, n), np.float32)

    def put(name, m, rows=P):
        at, k = cols[name]
        out[0:rows, at:at + k] = m

    def tiled(m):
        return m.reshape(-1, P).T

    for name in ("pre_mix_g", "gate_bias", "shift_mu", "w0", "a0", "k_k", "k_a", "r_k", "ln_x_w", "ln_x_b",
                 "post_mix_g", "pre_ffn_g", "post_ffn_g"):
        put(name, tiled(a[name]))
    b = a["ev_b_in_2"][0]
    put("ev_b", tiled(np.concatenate([b[0:2048], b[2056:3592]])))
    put("ev_bi", b[2048:2052, None], 4)
    put("ev_bf", b[2052:2056, None], 4)
    put("ev_bff", b[3592:3600, None], 8)
    put("ml_norm", tiled(a["ev_ml_norm_2"]))
    put("conv_w", tiled(a["od_conv_w_2"]))
    put("conv_b", tiled(a["od_conv_b_2"]))
    put("dt_bias", a["od_dt_bias_2"][0][:, None], 8)
    put("a_log", a["od_a_log_2"][0][:, None], 8)
    put("d_skip", tiled(np.repeat(a["od_d_skip_2"][0], HD)))
    put("ssm_norm", tiled(a["od_ssm_norm_2"]))
    put("pool_b", tiled(a["od_pool_b_2"]))
    put("pool_scale", tiled(a["od_pool_scale_2"]))
    put("ffn_w", tiled(a["ffn_conv_w_2"]))
    put("ffn_b", tiled(a["ffn_conv_b_2"]))
    for n1 in ("ln1_g", "ln1_b", "ln2_g", "ln2_b"):
        put(n1, tiled(a[n1 + "_2"]))
    put("w2a2", np.concatenate([a["w2"][0], a["a2"][0]]))
    put("g2", a["g2"][0])
    ev, od = a["ev_w_in_2"][0], a["od_w_in_2"][0]

    def narrow(m):
        return m.reshape(KD, P, -1).transpose(1, 0, 2).reshape(P, -1)

    put("ev_gates", narrow(np.concatenate([ev[:, 2048:2056], ev[:, 3592:3600]], axis=1)))
    put("od_dt", narrow(od[:, 1536:1544]))
    put("pool_w", a["od_pool_w_2"][0].transpose(1, 0, 2).reshape(P, -1))
    return out


def constant_array():
    cols, n = columns(CONSTANTS)
    out = np.zeros((P, n), np.float32)
    i = np.arange(P)
    row, colm = i[:, None], i[None, :]

    def put(name, m):
        at, k = cols[name]
        out[:, at:at + k] = m

    put("ident", row == colm)
    put("flip", row + colm == P - 1)
    put("same_head", row // HD == colm // HD)
    levels = []
    for l in range(LEVELS):
        s = 1 << l
        levels.append((row // (2 * s) == colm // (2 * s)) & (row % (2 * s) >= s) & (colm % (2 * s) < s))
    put("levels", np.concatenate(levels, axis=1))
    put("level0_t", levels[0].T)
    put("mask4", np.concatenate([row < colm, row <= colm, row < colm, row <= colm], axis=1))
    put("diag_qk", np.where(colm > row, NEG, 0.0))
    put("diag_st", np.where(colm < row, NEG, 0.0))
    t = np.arange(16)
    put("inv_count", np.concatenate([1.0 / np.minimum(t + 1, win) for win in WINDOWS])[None])
    put("eps", np.array([[RMS_EPS, LN_EPS, GN_EPS]]))
    return out


UPTO = None


def kernel(**inputs):
    import concourse.bacc as bacc
    from concourse.bass_utils import run_bass_kernel_spmd

    a = {k: np.asarray(m) for k, m in inputs.items()}
    arrays = {
        "x_t": np.ascontiguousarray(a["x"][0].T),
        "vectors": vector_array(a),
        "constants": constant_array(),
        "rel_rev": np.ascontiguousarray(a["rel_bias"][0][:, ::-1]),
        "stream": weight_stream(a),
    }
    nc = bacc.Bacc("TRN2", target_bir_lowering=False, num_devices=1)
    args = {k: nc.dram_tensor(k, m.shape, mybir.dt.from_np(m.dtype), kind="ExternalInput").ap()
            for k, m in arrays.items()}
    line = nc.dram_tensor("bias_line", (HEADS, DIAG_PAD), F32, kind="Internal").ap()
    out = nc.dram_tensor("out_t", (D, T), F32, kind="ExternalOutput").ap()
    network(nc, **args, bias_line=line, out_t=out, upto=UPTO)
    r = run_bass_kernel_spmd(nc, [arrays], core_ids=[0])
    return np.ascontiguousarray(r.results[0]["out_t"].T)[None]
```

```python
from contextlib import ExitStack

import numpy as np

import concourse.bass as bass
from concourse import mybir


F32 = mybir.dt.float32
F32R = mybir.dt.float32r
BF16 = mybir.dt.bfloat16
I32 = mybir.dt.int32
ALU = mybir.AluOpType
ACT = mybir.ActivationFunctionType
AX_X = mybir.AxisListType.X

P = 128
T = 512
NT = T // P
D = 1024
KD = D // P
HALF = D // 2
KH = HALF // P
HEADS = 8
HD = 64
ML_HEADS = 4
BAND_BIAS = 320
REL_CLIP = 256
DIAG_PAD = 704
FF1 = 4096 // P
FF2 = 2816 // P
NEG = -1e30
RMS_EPS = 1e-6
LN_EPS = 1e-5
GN_EPS = HD * 1e-5
ALPHA = 4.0 ** 0.25
WINDOWS = (2, 4, 8, 16)
LEVELS = 7

UNIT = 8
RING = 3
SPLIT = 3
WORK = 50

VECTORS = [("pre_mix_g", 8), ("gate_bias", 16), ("shift_mu", 14), ("w0", 4), ("a0", 4), ("k_k", 4),
           ("k_a", 4), ("r_k", 4), ("ln_x_w", 4), ("ln_x_b", 4), ("post_mix_g", 8), ("pre_ffn_g", 8),
           ("post_ffn_g", 8), ("ev_b", 28), ("ev_bi", 1), ("ev_bf", 1), ("ev_bff", 1), ("ml_norm", 4),
           ("conv_w", 32), ("conv_b", 8), ("dt_bias", 1), ("a_log", 1), ("d_skip", 4), ("ssm_norm", 4),
           ("pool_b", 4), ("pool_scale", 4), ("ffn_w", 264), ("ffn_b", 88), ("ln1_g", 16), ("ln1_b", 16),
           ("ln2_g", 16), ("ln2_b", 16), ("w2a2", 512), ("g2", 512), ("ev_gates", 128), ("od_dt", 64),
           ("pool_w", 512)]
CONSTANTS = [("ident", 128), ("flip", 128), ("same_head", 128), ("levels", 128 * LEVELS), ("level0_t", 128),
             ("mask4", 512), ("diag_qk", 128), ("diag_st", 128), ("inv_count", 64), ("eps", 3)]


def columns(spec):
    at, out = 0, {}
    for name, n in spec:
        out[name] = (at, n)
        at += n
    return out, at


class Signal:

    def __init__(self, sem):
        self.sem, self.base = sem, 0

    def at(self, n):
        return self.base + n

    def close(self, n):
        self.base += n


class Chain:

    def __init__(self, sem):
        self.sem, self.n = sem, 0

    def link(self, eng, ins):
        self.n += 1
        ins.then_inc(self.sem, 1)
        eng.wait_ge(self.sem, self.n)


class Weights:

    def __init__(self, raw, split, landed, high_done, low_done, unit_used, source, n_units):
        self.raw, self.split, self.landed, self.source, self.n_units = raw, split, landed, source, n_units
        self.high_done, self.low_done, self.unit_used = high_done, low_done, unit_used
        self.block, self.loaded, self.highs, self.lows, self.used = 0, 0, 0, 0, 0
        self.release = []

    def take(self, pe):
        unit, i = divmod(self.block, UNIT)
        if i == 0:
            pe.wait_ge(self.low_done, unit + 1)
        self.block += 1
        return [self.split[:, unit % SPLIT, half, i * P:(i + 1) * P] for half in range(2)]

    def free(self, ins, signal=None, n=0):
        if self.block % UNIT == 0:
            if signal is None:
                self.used += 1
                ins.then_inc(self.unit_used, 1)
                self.release.append((self.unit_used, self.used))
            else:
                self.release.append((signal.sem, signal.at(n)))

    def ahead(self):
        return min(self.n_units, len(self.release) + SPLIT - 1)

    def load(self, sp):
        while self.loaded < min(self.n_units, self.ahead() + RING):
            u = self.loaded
            if u >= RING:
                sp.wait_ge(self.low_done, u - RING + 1)
            sp.dma_start(self.raw[:, u % RING, :], self.source[u]).then_inc(self.landed[u % RING], 16)
            self.loaded += 1

    def round_high(self, act, scalar, upto=None):
        while self.highs < (self.ahead() if upto is None else min(self.ahead(), upto)):
            u = self.highs
            act.wait_ge(self.landed[u % RING], 16 * (u // RING + 1))
            if u >= SPLIT:
                act.wait_ge(*self.release[u - SPLIT])
            scalar.activation(self.split[:, u % SPLIT, 0, :], self.raw[:, u % RING, :],
                              ACT.Copy).then_inc(self.high_done, 1)
            self.highs += 1

    def subtract_low(self, pool, gpsimd):
        while self.lows < self.ahead():
            u = self.lows
            pool.wait_ge(self.high_done, u + 1)
            gpsimd.tensor_tensor(self.split[:, u % SPLIT, 1, :], self.raw[:, u % RING, :],
                                 self.split[:, u % SPLIT, 0, :].bitcast(F32), ALU.subtract
                                 ).then_inc(self.low_done, 1)
            self.lows += 1


def network(nc, x_t, vectors, constants, rel_rev, stream, bias_line, out_t, upto=None):
    n_units = stream.shape[0]
    ctx = ExitStack()
    with ctx:
        def sb(name, shape, dt=F32):
            return ctx.enter_context(nc.sbuf_tensor(name, shape, dt))

        def sem(name):
            return ctx.enter_context(nc.semaphore(name))

        x = sb("x", [P, KD, T])
        raw_units = sb("raw_units", [P, RING, UNIT * P])
        split_units = sb("split_units", [P, SPLIT, 2, UNIT * P], F32R)
        xs = sb("x_split", [P, 2, KD, T], F32R)
        arena_at = nc.sbuf_base
        w = sb("work", [P, WORK, T])

        def split_over(name, tile, n):
            return nc.alloc_sbuf_tensor_at(name, [P, 2, n, T], F32R, offset=arena_at + tile * T * 4)

        mix_split = split_over("mix_split", 8, KD)
        merged_split = split_over("merged_split", 30, KD)
        hidden1 = split_over("hidden1_split", 0, FF1 // 2)
        hidden2 = split_over("hidden2_split", 0, FF2)
        even_split = split_over("even_split", 20, KD)
        odd_split = split_over("odd_split", 0, KD)
        vec_cols, n_vec = columns(VECTORS)
        con_cols, n_con = columns(CONSTANTS)
        vec = sb("vec", [P, n_vec])
        con = sb("con", [P, n_con])
        ones = sb("ones", [P, T])
        col = sb("col", [P, 128])
        ident_h = sb("ident_h", [P, P], BF16)
        diag_qk_h = sb("diag_qk_h", [P, P], BF16)
        diag_st_h = sb("diag_st_h", [P, P], BF16)
        one_head = sb("one_head", [P, HEADS], BF16)
        ps = ctx.enter_context(nc.psum_tensor("ps", [P, 8, T], F32))

        def v(name, i=0, n=1, rows=P):
            a = vec_cols[name][0] + i
            return vec[0:rows, a:a + n]

        def c(name, i=0, n=None, rows=P):
            a, m = con_cols[name]
            return con[0:rows, a + i:a + i + (m if n is None else n)]

        ident = c("ident")
        eps_of = {RMS_EPS: c("eps", 0, 1), LN_EPS: c("eps", 1, 1), GN_EPS: c("eps", 2, 1)}
        one = ones[:, 0:1]

        dve_chain = Chain(sem("dve_chain"))
        act_chain = Chain(sem("act_chain"))
        pool_chain = Chain(sem("pool_chain"))
        inputs_landed = sem("inputs_landed")
        wts = Weights(raw_units, split_units, [sem(f"unit_landed_{i}") for i in range(RING)], sem("unit_high"),
                      sem("unit_low"), sem("unit_used"), stream, n_units)

        tile_ready = Signal(sem("tile_ready"))
        tile_read = Signal(sem("tile_read"))
        act_out = Signal(sem("act_out"))
        act_out2 = Signal(sem("act_out2"))
        dve_out = Signal(sem("dve_out"))
        dve_out2 = Signal(sem("dve_out2"))
        dve_out3 = Signal(sem("dve_out3"))
        high_out = Signal(sem("high_out"))
        low_out = Signal(sem("low_out"))
        pe_out = Signal(sem("pe_out"))
        pe_out2 = Signal(sem("pe_out2"))
        pe_out3 = Signal(sem("pe_out3"))
        dma_out = Signal(sem("dma_out"))

        V, S, TE, G = nc.vector, nc.scalar, nc.tensor, nc.gpsimd

        def bank(b, a=0, n=T, rows=slice(0, P)):
            return ps[rows, b, a:a + n]

        def tok(k, c0, n=P):
            return slice(c0 * P, c0 * P + n)

        def half(hh):
            return slice(HD * (hh % 2), HD * (hh % 2) + HD)

        def split_product(pe, out, n_k, rhs, signal, n):
            for k in range(n_k):
                high, low = wts.take(pe)
                last = k == n_k - 1
                TE.matmul(out, high, rhs(0, k), start=(k == 0), stop=False)
                TE.matmul(out, high, rhs(1, k), start=False, stop=False)
                ins = TE.matmul(out, low, rhs(0, k), start=False, stop=last)
                wts.free(ins, signal if last else None, n)
            ins.then_inc(signal.sem, 1)

        def product(pe, n_tiles, n_k, rhs, banks=4):
            for m in range(n_tiles):
                if m >= banks:
                    pe.wait_ge(tile_read.sem, tile_read.at(m - banks + 1))
                split_product(pe, bank(m % banks), n_k, rhs, tile_ready, m + 1)

        def weight_programs(block, act=True):
            @block.sync
            def _(sp):
                wts.load(sp)

            @block.gpsimd
            def _(pool):
                wts.subtract_low(pool, G)

            if act:
                @block.scalar
                def _(a):
                    wts.round_high(a, S)

        def of(t):
            return lambda half, k: t[:, half, k, :]

        def split_tiles(src, dst):
            with nc.Block() as block:
                @block.scalar
                def _(act):
                    for t in range(KD):
                        S.activation(dst[:, 0, t, :], src(t), ACT.Copy).then_inc(high_out.sem, 1)

                @block.vector
                def _(dve):
                    for t in range(0, KD, 2):
                        dve.wait_ge(high_out.sem, high_out.at(t + 1))
                        V.tensor_tensor(dst[:, 1, t, :], src(t), dst[:, 0, t, :].bitcast(F32), ALU.subtract)

                @block.gpsimd
                def _(pool):
                    for t in range(1, KD, 2):
                        pool.wait_ge(high_out.sem, high_out.at(t + 1))
                        G.tensor_tensor(dst[:, 1, t, :], src(t), dst[:, 0, t, :].bitcast(F32), ALU.subtract)
            high_out.close(KD)

        def norm(src, groups, mean_of, eps, gain, out, sums, centre=False, bias=None, add_to=None, sq0=0,
                 factor0=None, split=None):
            n_g = len(groups)
            order = [(g, t) for g, ts in enumerate(groups) for t in ts]
            size = len(groups[0])
            factor0 = sq0 + 8 if factor0 is None else factor0
            scaled = wt(sq0) if add_to is not None else out
            final = add_to if add_to is not None else out

            def subtract(eng, t):
                return eng.tensor_tensor(split[:, 1, t, :], final(t), split[:, 0, t, :].bitcast(F32), ALU.subtract)

            with nc.Block() as block:
                @block.tensor
                def _(pe):
                    if centre:
                        for g, ts in enumerate(groups):
                            for i, t in enumerate(ts):
                                ins = TE.matmul(bank(g % 4), sums, src(t), start=(i == 0), stop=(i == size - 1))
                            ins.then_inc(pe_out.sem, 1)
                    for g, ts in enumerate(groups):
                        for i, t in enumerate(ts):
                            pe.wait_ge(act_out.sem, act_out.at(g * size + i + 1))
                            ins = TE.matmul(bank(4 + g % 4), sums, w[:, sq0 + g * size + i, :],
                                            start=(i == 0), stop=(i == size - 1))
                        ins.then_inc(tile_ready.sem, 1)

                @block.scalar
                def _(act):
                    for n, (g, t) in enumerate(order):
                        if centre:
                            act.wait_ge(dve_out.sem, dve_out.at(n + 1))
                        S.activation(w[:, sq0 + n, :], src(t), ACT.Square).then_inc(act_out.sem, 1)
                    for g in range(n_g):
                        act.wait_ge(tile_ready.sem, tile_ready.at(g + 1))
                        S.activation(w[:, factor0 + g, :], bank(4 + g % 4), ACT.Sqrt, scale=1.0 / mean_of,
                                     bias=eps_of[eps]).then_inc(act_out2.sem, 1)
                    for n, (g, t) in enumerate(order):
                        if add_to is not None and split is not None:
                            sig = (dve_out3, pe_out2)[t % 2]
                            act.wait_ge(sig.sem, sig.at(t // 2 + 1))
                        elif bias is not None or split is not None:
                            act.wait_ge(dve_out2.sem, dve_out2.at(n + 1))
                        if split is not None:
                            S.activation(split[:, 0, t, :], final(t), ACT.Identity,
                                         bias=0.0 if bias is None else bias(t)).then_inc(high_out.sem, 1)
                        if bias is not None:
                            S.activation(out(t), out(t), ACT.Identity, bias=bias(t)).then_inc(act_out2.sem, 1)

                def wait_halves(eng, n):
                    eng.wait_ge(high_out.sem, high_out.at(n + 1))
                    if bias is not None:
                        eng.wait_ge(act_out2.sem, act_out2.at(n_g + n + 1))

                @block.vector
                def _(dve):
                    if centre:
                        for g, ts in enumerate(groups):
                            dve.wait_ge(pe_out.sem, pe_out.at(g + 1))
                            for t in ts:
                                V.scalar_tensor_tensor(src(t), bank(g % 4), -1.0 / mean_of, src(t), ALU.mult,
                                                       ALU.add).then_inc(dve_out.sem, 1)
                        dve.wait_ge(dve_out.sem, dve_out.at(len(order)))
                    for g, ts in enumerate(groups):
                        dve.wait_ge(act_out2.sem, act_out2.at(g + 1))
                        r = w[:, factor0 + g, :]
                        dve_chain.link(dve, V.reciprocal(r, r))
                        for n, t in enumerate(ts):
                            V.scalar_tensor_tensor(scaled(t), src(t), gain(t), r, ALU.mult,
                                                   ALU.mult).then_inc(dve_out2.sem, 1)
                            if add_to is not None and t % 2 == 0:
                                dve.wait_ge(dve_out2.sem, dve_out2.at(t + 1))
                                V.tensor_tensor(add_to(t), add_to(t), scaled(t), ALU.add).then_inc(dve_out3.sem, 1)
                    if split is not None:
                        for n in range(KD - 3, KD):
                            wait_halves(dve, n)
                            subtract(V, n)

                if add_to is not None or split is not None:
                    @block.gpsimd
                    def _(pool):
                        if add_to is not None:
                            for t in range(1, KD, 2):
                                pool.wait_ge(dve_out2.sem, dve_out2.at(t + 1))
                                G.tensor_tensor(add_to(t), add_to(t), scaled(t), ALU.add).then_inc(pe_out2.sem, 1)
                        if split is not None:
                            for n in range(KD - 3):
                                wait_halves(pool, n)
                                subtract(G, n)
            if centre:
                pe_out.close(n_g)
                dve_out.close(len(order))
            act_out.close(len(order))
            tile_ready.close(n_g)
            act_out2.close(n_g + (len(order) if bias is not None else 0))
            dve_out2.close(len(order))
            if add_to is not None:
                dve_out3.close(KD // 2)
                pe_out2.close(KD // 2)
            if split is not None:
                high_out.close(KD)

        def xt(t):
            return x[:, t, :]

        def wt(a):
            return lambda t: w[:, a + t, :]

        def to_token_major(jobs, scaled=None):
            n_banks = 4 * len(jobs)
            with nc.Block() as block:
                @block.tensor
                def _(pe):
                    for n in range(n_banks):
                        src = jobs[n // 4][0]
                        if n >= 4:
                            pe.wait_ge(tile_read.sem, tile_read.at(n - 3))
                        for t in range(4):
                            ins = TE.transpose(bank(n % 4, t * P, P), w[:, src + t, tok(0, n % 4)], ident)
                        ins.then_inc(tile_ready.sem, 1)

                @block.vector
                def _(dve):
                    for n in range(n_banks):
                        dst = jobs[n // 4][1] + n % 4
                        dve.wait_ge(tile_ready.sem, tile_ready.at(n + 1))
                        if scaled is None:
                            V.tensor_copy(w[:, dst, :], bank(n % 4)).then_inc(tile_read.sem, 1)
                        else:
                            V.tensor_tensor(w[:, dst, :].rearrange("p (h d) -> p h d", d=HD),
                                            bank(n % 4).rearrange("p (h d) -> p h d", d=HD),
                                            scaled(n % 4).unsqueeze(2).to_broadcast([P, HEADS, HD]),
                                            ALU.mult).then_inc(tile_read.sem, 1)
            tile_ready.close(n_banks)
            tile_read.close(n_banks)

        PARTS = 96

        def row_parts(tile, j):
            return w[0:PARTS, tile, 256 * j:256 * (j + 1)].bitcast(BF16)

        def split_rows(dve, rows, n, tile, j, rest, rounded):
            left, part = w[0:n, rest, :], w[0:n, rounded, 0:256].bitcast(BF16)
            src = rows
            for k in range(3):
                dve_chain.link(dve, V.tensor_copy(part, src))
                ins = V.tensor_copy(row_parts(tile, j)[32 * k:32 * k + n], part)
                if k < 2:
                    ins = V.tensor_tensor(left, src, part, ALU.subtract)
                dve_chain.link(dve, ins)
                src = left

        def one_hot(hd, n):
            return one_head[0:PARTS, hd:hd + 1].to_broadcast([PARTS, n])

        def attention(kind, q0, k0, vt0, out0, tmp, parts=None, f_cols=None, bias0=None):
            ml = kind == "mlstm"
            heads = ML_HEADS if ml else HEADS
            dim = HALF // heads
            items = [(hd, i) for hd in range(heads) for i in range(NT)]
            n_items = len(items)
            e = [w[:, tmp, :], w[:, tmp + 1, :]]
            pt = [w[:, tmp + 2, :], w[:, tmp + 3, :]]
            heads_a_tile = P // dim
            sums, negs, lows = (col[:, a:a + n_items] for a in (64, 96, 48))
            turn_bank = (lambda n: 3) if ml else (lambda n: 2 + n % 2)
            weighted = dve_out2 if ml else act_out

            def rows(hd):
                return half(hd) if dim == HD else slice(0, P)

            def query_key(n, out, stop):
                hd, i = items[n]
                t, r = hd // heads_a_tile, rows(hd)
                return TE.matmul(out, w[r, q0 + t, i * P:(i + 1) * P], w[r, k0 + t, 0:(i + 1) * P],
                                 start=True, stop=stop)

            with nc.Block() as block:
                @block.tensor
                def _(pe):
                    def scores(n):
                        hd, i = items[n]
                        wd = (i + 1) * P
                        if n >= 2:
                            pe.wait_ge(act_out.sem, act_out.at(n - 1))
                        d = bank(n % 2, 0, wd)
                        if not ml:
                            query_key(n, d, False)
                        if kind == "band":
                            ins = TE.matmul(d, c("flip"), w[:, bias0 + hd, (3 - i) * P:T], start=False, stop=True)
                        else:
                            TE.matmul(d, row_parts(parts, 0)[:, i * P:(i + 1) * P], one_hot(hd, wd),
                                      start=ml, stop=False)
                            TE.matmul(d, one_hot(hd, P), row_parts(parts, 1)[:, 0:wd], start=False, stop=False)
                            ins = TE.matmul(bank(n % 2, i * P, P), ident_h[:, :], diag_qk_h[:, :], start=False,
                                            stop=True)
                        ins.then_inc(tile_ready.sem, 1)

                    def products(n):
                        if n >= 1:
                            pe.wait_ge(dve_out2.sem, dve_out2.at(n))
                        query_key(n, bank(2, 0, (items[n][1] + 1) * P), True).then_inc(pe_out3.sem, 1)

                    def turn(n):
                        hd, i = items[n]
                        pe.wait_ge(weighted.sem, weighted.at(n + 1))
                        if n >= (1 if ml else 2):
                            pe.wait_ge(act_out2.sem, act_out2.at(n if ml else n - 1))
                        for j in range(i + 1):
                            ins = TE.transpose(bank(turn_bank(n), j * P, P), e[n % 2][:, j * P:(j + 1) * P], ident)
                        ins.then_inc(pe_out.sem, 1)

                    def values(n):
                        hd, i = items[n]
                        pe.wait_ge(act_out2.sem, act_out2.at(n + 1))
                        for j in range(i + 1):
                            ins = TE.matmul(bank(4 + i, hd * dim, dim), pt[n % 2][:, j * P:(j + 1) * P],
                                            w[:, vt0 + j, hd * dim:(hd + 1) * dim], start=(j == 0), stop=(j == i))
                        ins.then_inc(pe_out2.sem, 1)

                    scores(0)
                    if ml:
                        products(0)
                    for n in range(n_items):
                        if n + 1 < n_items:
                            scores(n + 1)
                        if n >= 1:
                            values(n - 1)
                        turn(n)
                        if ml and n + 1 < n_items:
                            products(n + 1)
                    values(n_items - 1)
                    for i in range(NT):
                        pe.wait_ge(dve_out3.sem, dve_out3.at(i + 1))
                    for t in range(KH):
                        for i in range(NT):
                            ins = TE.transpose(bank(t, i * P, P), w[:, tmp + i, t * P:(t + 1) * P], ident)
                        ins.then_inc(pe_out.sem, 1)

                @block.vector
                def _(dve):
                    def peak(n):
                        hd, i = items[n]
                        dve.wait_ge(tile_ready.sem, tile_ready.at(n + 1))
                        mx = col[:, n % 2:n % 2 + 1]
                        dve_chain.link(dve, V.reduce_max(mx, bank(n % 2, 0, (i + 1) * P), AX_X))
                        if ml:
                            dve_chain.link(dve, V.tensor_tensor(mx, mx, f_cols(i, hd), ALU.max))
                        V.tensor_scalar(negs[:, n:n + 1], mx, -1.0, None, ALU.mult).then_inc(dve_out.sem, 1)

                    def weight(n):
                        wd = (items[n][1] + 1) * P
                        a = e[n % 2][:, 0:wd]
                        dve.wait_ge(act_out.sem, act_out.at(n + 1))
                        dve.wait_ge(pe_out3.sem, pe_out3.at(n + 1))
                        V.tensor_tensor_reduce(a, bank(2, 0, wd), a, 1.0, 0.0, ALU.mult, ALU.add,
                                               sums[:, n:n + 1]).then_inc(dve_out2.sem, 1)

                    peak(0)
                    for n in range(n_items):
                        if n + 1 < n_items:
                            peak(n + 1)
                        if ml:
                            weight(n)
                    if ml:
                        scratch = col[:, 0:n_items]
                        dve.wait_ge(dve_out2.sem, dve_out2.at(n_items))
                        dve_chain.link(dve, V.tensor_scalar(scratch, sums, -1.0, None, ALU.mult))
                        dve_chain.link(dve, V.tensor_tensor(sums, sums, scratch, ALU.max))
                        dve.wait_ge(act_out2.sem, act_out2.at(n_items + 1))
                        dve_chain.link(dve, V.tensor_tensor(sums, sums, lows, ALU.max))
                    else:
                        dve.wait_ge(act_out.sem, act_out.at(n_items))
                    dve_chain.link(dve, V.reciprocal(sums, sums))
                    dve.wait_ge(pe_out2.sem, pe_out2.at(n_items))
                    for i in range(NT):
                        V.tensor_tensor(w[:, tmp + i, :].rearrange("p (h d) -> p h d", d=dim),
                                        bank(4 + i).rearrange("p (h d) -> p h d", d=dim),
                                        sums[:, i::NT].unsqueeze(2).to_broadcast([P, heads, dim]),
                                        ALU.mult).then_inc(dve_out3.sem, 1)
                    for t in range(1, KH, 2):
                        dve.wait_ge(pe_out.sem, pe_out.at(n_items + t + 1))
                        V.tensor_copy(w[:, out0 + t, :], bank(t))

                @block.scalar
                def _(act):
                    def exps(n):
                        wd = (items[n][1] + 1) * P
                        act.wait_ge(dve_out.sem, dve_out.at(n + 1))
                        if n >= 2:
                            act.wait_ge(pe_out.sem, pe_out.at(n - 1))
                        acc = {} if ml else {"accum_out": sums[:, n:n + 1]}
                        S.activation(e[n % 2][:, 0:wd], bank(n % 2, 0, wd), ACT.Exp, bias=negs[:, n:n + 1],
                                     **acc).then_inc(act_out.sem, 1)

                    def copy(n):
                        wd = (items[n][1] + 1) * P
                        act.wait_ge(pe_out.sem, pe_out.at(n + 1))
                        if n >= 2:
                            act.wait_ge(pe_out2.sem, pe_out2.at(n - 1))
                        S.activation(pt[n % 2][:, 0:wd], bank(turn_bank(n), 0, wd), ACT.Copy
                                     ).then_inc(act_out2.sem, 1)

                    exps(0)
                    for n in range(n_items):
                        if n + 1 < n_items:
                            exps(n + 1)
                        copy(n)
                    if ml:
                        S.activation(lows, negs, ACT.Exp).then_inc(act_out2.sem, 1)
                    for t in range(0, KH, 2):
                        act.wait_ge(pe_out.sem, pe_out.at(n_items + t + 1))
                        S.activation(w[:, out0 + t, :], bank(t), ACT.Copy)
            tile_ready.close(n_items)
            pe_out.close(n_items + KH)
            pe_out2.close(n_items)
            dve_out.close(n_items)
            dve_out3.close(NT)
            act_out.close(n_items)
            act_out2.close(n_items + ml)
            if ml:
                pe_out3.close(n_items)
                dve_out2.close(n_items)

        def stage_inputs():
            with nc.Block() as block:
                @block.scalar
                def _(act):
                    wts.round_high(act, S)

                @block.gpsimd
                def _(pool):
                    wts.subtract_low(pool, G)

                @block.sync
                def _(sp):
                    sp.dma_start(x[:, :, :], x_t.rearrange("(k p) t -> p k t", p=P)).then_inc(inputs_landed, 16)
                    sp.dma_start(vec[:, :], vectors).then_inc(inputs_landed, 16)
                    sp.dma_start(con[:, :], constants).then_inc(inputs_landed, 16)
                    sp.dma_start(w[0:HEADS, 0, 0:BAND_BIAS], rel_rev).then_inc(inputs_landed, 16)
                    wts.load(sp)
                    sp.wait_ge(inputs_landed, 64)
                    sp.wait_ge(dve_out.sem, dve_out.at(1))
                    sp.dma_start(bias_line, w[0:HEADS, 1:3, :].rearrange("p a t -> p (a t)")[:, 0:DIAG_PAD]
                                 ).then_inc(dma_out.sem, 16)
                    sp.wait_ge(dma_out.sem, dma_out.at(16))
                    diagonals = bass.AP(bias_line.tensor, bias_line.offset + 1, [[1, P], [DIAG_PAD, HEADS], [1, T]])
                    sp.dma_start(w[:, 20:28, :], diagonals).then_inc(dma_out.sem, 16)
                    sp.wait_ge(dma_out.sem, dma_out.at(32))

                @block.vector
                def _(dve):
                    line = w[0:HEADS, 1:3, :].rearrange("p a t -> p (a t)")
                    V.memset(ones[:, :], 1.0)
                    dve_chain.link(dve, V.memset(line, 0.0))
                    dve.wait_ge(inputs_landed, 64)
                    V.tensor_copy(line[:, REL_CLIP:REL_CLIP + BAND_BIAS], w[0:HEADS, 0, 0:BAND_BIAS])
                    V.tensor_copy(line[:, 0:REL_CLIP],
                                  w[0:HEADS, 0, 0:1].to_broadcast([HEADS, REL_CLIP])).then_inc(dve_out.sem, 1)
            dve_out.close(1)
            dma_out.close(32)
            with nc.Block() as block:
                @block.vector
                def _(dve):
                    V.tensor_copy(ident_h[:, :], ident)
                    V.tensor_copy(diag_qk_h[:, :], c("diag_qk"))
                    V.tensor_copy(diag_st_h[:, :], c("diag_st"))
                    dve_chain.link(dve, V.memset(one_head[:, :], 0.0))
                    for k in range(3):
                        r = slice(32 * k, 32 * k + HEADS)
                        V.tensor_copy(one_head[r, :], con[r, con_cols["ident"][0] + 32 * k:con_cols["ident"][0] + 32 * k + HEADS])
                    dve_chain.link(dve, V.memset(w[HD:P, 20:28, T - HD:T], NEG))

        YB, YA = 0, 4
        Q1 = 8

        def stage_qkv():
            u0 = wts.block // UNIT
            with nc.Block() as block:
                @block.tensor
                def _(pe):
                    product(pe, 12, KD, of(xs))

                weight_programs(block, act=False)

                @block.scalar
                def _(act):
                    for m in range(12):
                        wts.round_high(act, S, u0 + m + SPLIT)
                        act.wait_ge(tile_ready.sem, tile_ready.at(m + 1))
                        S.activation(w[:, Q1 + m, :], bank(m % 4), ACT.Copy,
                                     scale=HD ** -0.5 if m < 4 else 1.0).then_inc(tile_read.sem, 1)
            tile_ready.close(12)
            tile_read.close(12)

        def stage_rwkv_in():
            raw0 = 38
            raw = w[:, raw0:raw0 + 3, :].rearrange("p a t -> p (a t)")
            pads = [raw[:, 0:T + 1], raw[:, T + 8:2 * T + 9]]
            u0 = wts.block // UNIT
            with nc.Block() as block:
                @block.tensor
                def _(pe):
                    product(pe, 14, KD, of(xs))

                weight_programs(block, act=False)

                @block.scalar
                def _(act):
                    act.wait_ge(dve_out2.sem, dve_out2.at(1))
                    for m in range(14):
                        wts.round_high(act, S, u0 + m + SPLIT)
                        act.wait_ge(tile_ready.sem, tile_ready.at(m + 1))
                        if m >= 2:
                            act.wait_ge(dve_out.sem, dve_out.at(m - 1))
                        S.activation(pads[m % 2][:, 1:T + 1], bank(m % 4), ACT.Copy).then_inc(tile_read.sem, 1)

                @block.vector
                def _(dve):
                    V.memset(pads[0][:, 0:1], 0.0)
                    V.memset(pads[1][:, 0:1], 0.0).then_inc(dve_out2.sem, 1)
                    dve.wait_ge(dve_out2.sem, dve_out2.at(1))
                    for m in range(14):
                        p = pads[m % 2]
                        mixed = w[:, m if m < 4 else m + 4, :]
                        dve.wait_ge(tile_read.sem, tile_read.at(m + 1))
                        dve_chain.link(dve, V.tensor_tensor(mixed, p[:, 0:T], p[:, 1:T + 1], ALU.subtract))
                        V.scalar_tensor_tensor(mixed, mixed, v("shift_mu", m), p[:, 1:T + 1], ALU.mult,
                                               ALU.add).then_inc(dve_out.sem, 1)
            tile_ready.close(14)
            tile_read.close(14)
            dve_out.close(14)
            dve_out2.close(1)

        R, K, VV, CW, CG = 0, 8, 12, 16, 17
        LW, CM, AA, KK, GG, EE, AT, BO = 18, 22, 26, 30, 34, 38, 42, 46

        def stage_rwkv_prepare():
            with nc.Block() as block:
                @block.scalar
                def _(act):
                    act_chain.link(act, S.activation(w[0:HD, CW, :], w[0:HD, CW, :], ACT.Tanh))
                    S.activation(w[:, CG, :], w[:, CG, :], ACT.Sigmoid).then_inc(act_out.sem, 1)
                    for t in range(4):
                        act.wait_ge(tile_ready.sem, tile_ready.at(3 * t + 1))
                        S.activation(w[:, LW + t, :], bank(0), ACT.Sigmoid, bias=v("w0", t)).then_inc(tile_read.sem, 1)
                        act.wait_ge(tile_ready.sem, tile_ready.at(3 * t + 2))
                        S.activation(w[:, AA + t, :], bank(1), ACT.Sigmoid, bias=v("a0", t)).then_inc(tile_read.sem, 1)
                        act.wait_ge(tile_ready.sem, tile_ready.at(3 * t + 3))
                        S.activation(w[:, GG + t, :], bank(2), ACT.Copy).then_inc(tile_read.sem, 1)
                    for t in range(4):
                        act.wait_ge(pe_out.sem, pe_out.at(t + 1))
                        S.activation(w[:, EE + t, :], bank(4 + t), ACT.Sqrt).then_inc(act_out2.sem, 1)

                @block.tensor
                def _(pe):
                    pe.wait_ge(act_out.sem, act_out.at(1))
                    for t in range(4):
                        if t >= 1:
                            pe.wait_ge(tile_read.sem, tile_read.at(3 * t - 2))
                        TE.matmul(bank(0), v("w2a2", t * P, P)[0:HD], w[0:HD, CW, :], start=True,
                                  stop=True).then_inc(tile_ready.sem, 1)
                        if t >= 1:
                            pe.wait_ge(tile_read.sem, tile_read.at(3 * t - 1))
                        TE.matmul(bank(1), v("w2a2", t * P, P)[HD:P], w[HD:P, CW, :], start=True,
                                  stop=True).then_inc(tile_ready.sem, 1)
                        if t >= 1:
                            pe.wait_ge(tile_read.sem, tile_read.at(3 * t))
                        TE.matmul(bank(2), v("g2", t * P, P), w[:, CG, :], start=True,
                                  stop=True).then_inc(tile_ready.sem, 1)
                    for t in range(4):
                        pe.wait_ge(dve_out.sem, dve_out.at(t + 1))
                        TE.matmul(bank(4 + t), c("same_head"), w[:, AT + t, :], start=True,
                                  stop=True).then_inc(pe_out.sem, 1)
                    for t in range(4):
                        pe.wait_ge(act_out2.sem, act_out2.at(t + 1))
                        pe.wait_ge(dve_out2.sem, dve_out2.at(t + 1))
                        TE.matmul(bank(4 + t), c("same_head"), w[:, BO + t, :], start=True,
                                  stop=True).then_inc(pe_out.sem, 1)

                @block.vector
                def _(dve):
                    for t in range(4):
                        kk, sq = w[:, KK + t, :], w[:, AT + t, :]
                        dve_chain.link(dve, V.tensor_scalar(kk, w[:, K + t, :], v("k_k", t), None, ALU.mult))
                        V.tensor_tensor(sq, kk, kk, ALU.mult).then_inc(dve_out.sem, 1)
                    for t in range(4):
                        kt, lw, a = w[:, K + t, :], w[:, LW + t, :], w[:, AA + t, :]
                        cm = w[:, CM + t, :]
                        dve.wait_ge(tile_read.sem, tile_read.at(3 * t + 2))
                        tmp = w[:, BO + t, :]
                        dve_chain.link(dve, V.tensor_scalar(tmp, a, -1.0, v("k_a", t), ALU.add, ALU.mult))
                        dve_chain.link(dve, V.scalar_tensor_tensor(kt, tmp, 1.0, kt, ALU.add, ALU.mult))
                        V.scalar_tensor_tensor(tmp, w[:, R + t, :], v("r_k", t), kt, ALU.mult,
                                               ALU.mult).then_inc(dve_out2.sem, 1)
                        dve_chain.link(dve, V.tensor_scalar(lw, lw, -float(np.exp(-0.5)), None, ALU.mult))
                        for ch in range(NT):
                            s = slice(ch * P, (ch + 1) * P)
                            dve_chain.link(dve, V.tensor_tensor_scan(cm[:, s], ones[:, 0:P], lw[:, s], 0.0,
                                                                     ALU.mult, ALU.add))
                            mid = col[:, 0:1]
                            dve_chain.link(dve, V.tensor_copy(mid, cm[:, ch * P + HD - 1:ch * P + HD]))
                            dve_chain.link(dve, V.tensor_scalar(cm[:, s], cm[:, s], mid, None, ALU.subtract))
                    dve.wait_ge(dve_out2.sem, dve_out2.at(4))
                    for t in range(4):
                        kk, rn = w[:, KK + t, :], w[:, EE + t, :]
                        dve.wait_ge(act_out2.sem, act_out2.at(t + 1))
                        dve_chain.link(dve, V.tensor_scalar(rn, rn, 1e-12, None, ALU.max))
                        dve_chain.link(dve, V.reciprocal(rn, rn))
                        dve_chain.link(dve, V.tensor_tensor(kk, kk, rn, ALU.mult))
                    for t in range(4):
                        dve.wait_ge(pe_out.sem, pe_out.at(5 + t))
                        dve_chain.link(dve, V.tensor_tensor(w[:, BO + t, :], bank(4 + t), w[:, VV + t, :], ALU.mult))
            tile_ready.close(12)
            tile_read.close(12)
            pe_out.close(8)
            act_out.close(1)
            act_out2.close(4)
            dve_out.close(4)
            dve_out2.close(4)
            with nc.Block() as block:
                @block.scalar
                def _(act):
                    for t in range(4):
                        act.wait_ge(dve_out.sem, dve_out.at(t + 1))
                        e = w[:, EE + t, :]
                        S.activation(e, e, ACT.Exp).then_inc(act_out.sem, 1)
                    for t in range(4):
                        act.wait_ge(dve_out2.sem, dve_out2.at(t + 1))
                        e, cm = w[:, EE + t, :], w[:, CM + t, :]
                        S.activation(e, cm, ACT.Exp, scale=-1.0).then_inc(act_out.sem, 1)
                        act_chain.link(act, S.activation(cm, cm, ACT.Exp))
                        S.activation(col[:, 32 + 4 * t:36 + 4 * t], cm[:, P - 1::P], ACT.Copy).then_inc(act_out2.sem, 1)
                    act.wait_ge(dve_out2.sem, dve_out2.at(4))
                    S.activation(col[:, 16:32], col[:, 16:32], ACT.Exp).then_inc(act_out2.sem, 1)

                @block.vector
                def _(dve):
                    for t in range(4):
                        e = w[:, EE + t, :]
                        dve_chain.link(dve, V.tensor_tensor(e, w[:, CM + t, :], w[:, LW + t, :], ALU.subtract))
                        V.tensor_scalar(col[:, 16 + 4 * t:20 + 4 * t], e[:, 0::P], -1.0, None,
                                        ALU.mult).then_inc(dve_out.sem, 1)
                    for t in range(4):
                        kk = w[:, KK + t, :]
                        dve.wait_ge(act_out.sem, act_out.at(t + 1))
                        dve_chain.link(dve, V.scalar_tensor_tensor(w[:, AT + t, :], kk, -1.0, w[:, EE + t, :],
                                                                   ALU.mult, ALU.mult))
                        V.tensor_tensor(kk, kk, w[:, AA + t, :], ALU.mult).then_inc(dve_out2.sem, 1)
                    dve.wait_ge(dve_out2.sem, dve_out2.at(4))
                    for t in range(4):
                        e = w[:, EE + t, :]
                        dve.wait_ge(act_out.sem, act_out.at(5 + t))
                        V.tensor_tensor(w[:, KK + t, :], w[:, KK + t, :], e, ALU.mult)
                        V.tensor_tensor(w[:, K + t, :], w[:, K + t, :], e, ALU.mult)
                        dve.wait_ge(act_out2.sem, act_out2.at(t + 1))
                        dve_chain.link(dve, V.tensor_tensor(w[:, R + t, :], w[:, R + t, :], w[:, CM + t, :], ALU.mult))
            act_out.close(8)
            act_out2.close(5)
            dve_out.close(4)
            dve_out2.close(4)

        N4, UU, TT, XX, BK = (LW, CM), (38, 41), (39, 29), (40, 17), (26, 27)
        VTOK = 28
        ZS = CW

        def stage_rwkv_chunks():
            z = w[:, ZS, :]
            pe_s = (pe_out, pe_out2)
            dve_s = (dve_out, dve_out2)
            act_s = (act_out, act_out2)
            PE_TOK, PE_PAIR, PE_TURN, PE_G, PE_SA, PE_YZ = 1, 2, 6, 19, 20, 21
            DVE_U, DVE_Z = 1, 14
            ACT_TOK, ACT_T, ACT_G, ACT_SA, ACT_Y = 1, 2, 3, 4, 5

            def pe_x(l):
                return 5 + 2 * l

            def pe_u(l):
                return 6 + 2 * l

            def wait(eng, sig, g, ch, n, per):
                eng.wait_ge(sig[g].sem, sig[g].at(ch * per + n))

            def wait_pe(eng, g, ch, n):
                wait(eng, pe_s, g, ch, n, PE_YZ)

            def wait_dve(eng, g, ch, n):
                wait(eng, dve_s, g, ch, n, DVE_Z)

            def wait_act(eng, g, ch, n):
                wait(eng, act_s, g, ch, n, ACT_Y)

            def n4(g, i, j):
                return w[:, N4[g] + i, j * P:(j + 1) * P]

            def part(tile, i):
                return w[:, tile, i * P:(i + 1) * P]

            def quad(ap):
                return ap.rearrange("p (a t) -> p a t", a=4)

            def wide(m):
                return m.unsqueeze(1).to_broadcast([P, 4, P])

            def cols(ch):
                return slice(ch * P, (ch + 1) * P)

            def state(g):
                return z[:, 2 * g * HD:2 * (g + 1) * HD].rearrange("p (a d) -> p a d", d=HD)

            with nc.Block() as block:
                @block.vector
                def _(dve):
                    V.memset(w[:, N4[0]:N4[0] + 4, :], 0.0)
                    V.memset(w[:, N4[1]:N4[1] + 4, :], 0.0)
                    dve_chain.link(dve, V.memset(z, 0.0))

            with nc.Block() as block:
                @block.tensor
                def _(pe):
                    def token_major(g, ch):
                        if ch:
                            wait_act(pe, g, ch - 1, ACT_Y)
                        for j, src in enumerate((KK, K, VV)):
                            for a in range(2):
                                ins = TE.transpose(bank(4 * g + 2 + j // 2, (j % 2) * 256 + a * P, P),
                                                   w[:, src + 2 * g + a, cols(ch)], ident)
                        ins.then_inc(pe_s[g].sem, 1)

                    def pairs(g, ch):
                        if ch:
                            wait_dve(pe, g, ch - 1, DVE_Z)
                        for i in range(4):
                            if i == 2:
                                wait_act(pe, g, ch, ACT_TOK)
                            t, r = 2 * g + i // 2, half(i)
                            a, rr = w[r, AT + t, cols(ch)], w[r, R + t, cols(ch)]
                            bt, kt = w[r, KK + t, cols(ch)], w[r, K + t, cols(ch)]
                            for j, (lhs, rhs) in enumerate(((bt, a), (bt, rr), (kt, a), (kt, rr))):
                                ins = TE.matmul(bank(4 * g + i, j * P, P), lhs, rhs, start=True, stop=True)
                            ins.then_inc(pe_s[g].sem, 1)

                    def turn(g, ch):
                        wait_dve(pe, g, ch, DVE_U)
                        for i in range(4):
                            ins = TE.transpose(bank(4 * g, i * P, P), part(UU[g], i), ident)
                        ins.then_inc(pe_s[g].sem, 1)

                    def level_x(l):
                        def step(g, ch):
                            if l == 1:
                                wait_act(pe, g, ch, ACT_T)
                            else:
                                wait_dve(pe, g, ch, 2 * l - 1)
                            for i in range(4):
                                ins = TE.matmul(bank(4 * g + 1, i * P, P), n4(g, i, 0), part(TT[g], i), start=True,
                                                stop=True)
                            ins.then_inc(pe_s[g].sem, 1)
                        return step

                    def level_u(l):
                        def step(g, ch):
                            wait_dve(pe, g, ch, 2 * l)
                            if l < LEVELS - 1:
                                for i in range(4):
                                    TE.matmul(bank(4 * g, i * P, P), part(UU[g], i), part(XX[g], i), start=True,
                                              stop=True)
                            for i in range(4):
                                ins = TE.matmul(bank(4 * g + 2, i * P, P), part(XX[g], i), part(UU[g], i), start=True,
                                                stop=True)
                            ins.then_inc(pe_s[g].sem, 1)
                        return step

                    def values_of(g, i):
                        return w[:, VTOK, g * 256 + i * HD:g * 256 + (i + 1) * HD]

                    def right_side(g, ch):
                        wait_dve(pe, g, ch, 2 * LEVELS - 1)
                        for i in range(4):
                            t, r = 2 * g + i // 2, half(i)
                            out = bank(4 * g + (3, 1)[i % 2], (i // 2) * HD, HD)
                            TE.matmul(out, w[r, AT + t, cols(ch)], z[r, t * HD:(t + 1) * HD], start=True, stop=False)
                            ins = TE.matmul(out, n4(g, i, 2), values_of(g, i), start=False, stop=True)
                        ins.then_inc(pe_s[g].sem, 1)

                    def solve(g, ch):
                        wait_act(pe, g, ch, ACT_G)
                        for i in range(4):
                            ins = TE.matmul(bank(4 * g, i * HD, HD), part(UU[g], i), w[:, XX[g], i * HD:(i + 1) * HD],
                                            start=True, stop=True)
                        ins.then_inc(pe_s[g].sem, 1)

                    def output(g, ch):
                        wait_act(pe, g, ch, ACT_SA)
                        for i in range(4):
                            t, r = 2 * g + i // 2, half(i)
                            sa = w[:, XX[g], 256 + i * HD:256 + (i + 1) * HD]
                            y = bank(4 * g + 2, (i // 2) * P, P, r)
                            TE.matmul(y, z[r, t * HD:(t + 1) * HD], w[r, R + t, cols(ch)], start=True, stop=False)
                            TE.matmul(y, sa, n4(g, i, 1), start=False, stop=False)
                            TE.matmul(y, values_of(g, i), n4(g, i, 3), start=False, stop=True)
                            zz = bank(4 * g + 1, (i // 2) * HD, HD, r)
                            TE.matmul(zz, w[:, BK[g], i * HD:(i + 1) * HD], sa, start=True, stop=False)
                            ins = TE.matmul(zz, w[:, BK[g], 256 + i * HD:256 + (i + 1) * HD], values_of(g, i),
                                            start=False, stop=True)
                        ins.then_inc(pe_s[g].sem, 1)

                    steps = [token_major, pairs, turn]
                    for l in range(1, LEVELS):
                        steps += [level_x(l), level_u(l)]
                    for ch in range(NT):
                        for step in steps + [right_side, solve, output]:
                            for g in range(2):
                                step(g, ch)

                @block.vector
                def _(dve):
                    def first(g, ch):
                        for i in range(4):
                            wait_pe(dve, g, ch, PE_PAIR + i)
                            ins = V.copy_predicated(w[:, N4[g] + i, :], c("mask4").bitcast(I32), bank(4 * g + i))
                        dve_chain.link(dve, ins)
                        uu, zt = quad(w[:, UU[g], :]), state(g)
                        dve_chain.link(dve, V.tensor_tensor(uu, w[:, N4[g]:N4[g] + 4, 0:P], wide(c("level0_t")),
                                                            ALU.mult))
                        at = 16 + 8 * g + ch
                        before = col[:, at:at + 5:4].unsqueeze(2).to_broadcast([P, 2, HD])
                        dve_chain.link(dve, V.tensor_tensor(zt, zt, before, ALU.mult))
                        V.tensor_tensor(uu, uu, wide(ident), ALU.add).then_inc(dve_s[g].sem, 1)

                    def mask_x(l):
                        def step(g, ch):
                            wait_pe(dve, g, ch, pe_x(l))
                            V.tensor_tensor(quad(w[:, XX[g], :]), quad(bank(4 * g + 1)), wide(c("levels", l * P, P)),
                                            ALU.mult).then_inc(dve_s[g].sem, 1)
                        return step

                    def add_u(l):
                        def step(g, ch):
                            wait_pe(dve, g, ch, pe_u(l))
                            if l < LEVELS - 1:
                                V.tensor_tensor(w[:, TT[g], :], w[:, TT[g], :], bank(4 * g), ALU.add)
                            V.tensor_tensor(w[:, UU[g], :], w[:, UU[g], :], bank(4 * g + 2),
                                            ALU.add).then_inc(dve_s[g].sem, 1)
                        return step

                    def next_state(g, ch):
                        zt = state(g)
                        at = 32 + 8 * g + ch
                        after = col[:, at:at + 5:4].unsqueeze(2).to_broadcast([P, 2, HD])
                        wait_pe(dve, g, ch, PE_YZ)
                        dve_chain.link(dve, V.tensor_tensor(
                            zt, zt, bank(4 * g + 1, 0, P).rearrange("p (a d) -> p a d", d=HD), ALU.add))
                        V.tensor_tensor(zt, zt, after, ALU.mult).then_inc(dve_s[g].sem, 1)
                        wait_dve(dve, g, ch, DVE_Z)

                    steps = [first]
                    for l in range(1, LEVELS):
                        steps += [mask_x(l), add_u(l)]
                    for ch in range(NT):
                        for step in steps + [next_state]:
                            for g in range(2):
                                step(g, ch)

                @block.scalar
                def _(act):
                    def token_major(g, ch):
                        wait_pe(act, g, ch, PE_TOK)
                        S.activation(w[:, BK[g], :], bank(4 * g + 2), ACT.Copy)
                        S.activation(w[:, VTOK, g * 256:(g + 1) * 256], bank(4 * g + 3, 0, 256),
                                     ACT.Copy).then_inc(act_s[g].sem, 1)

                    def inverse(g, ch):
                        wait_pe(act, g, ch, PE_TURN)
                        S.activation(w[:, TT[g], :], bank(4 * g), ACT.Copy).then_inc(act_s[g].sem, 1)

                    def right_side(g, ch):
                        wait_pe(act, g, ch, PE_G)
                        out = w[:, XX[g], 0:256].rearrange("p (a b d) -> p a b d", a=2, b=2)
                        for b in range(2):
                            ins = S.activation(out[:, :, b, :], bank(4 * g + (3, 1)[b], 0, P).rearrange(
                                "p (a d) -> p a d", d=HD), ACT.Copy)
                        ins.then_inc(act_s[g].sem, 1)

                    def taken_up(g, ch):
                        wait_pe(act, g, ch, PE_SA)
                        S.activation(w[:, XX[g], 256:512], bank(4 * g, 0, 256), ACT.Copy).then_inc(act_s[g].sem, 1)

                    def output(g, ch):
                        wait_pe(act, g, ch, PE_YZ)
                        S.activation(w[:, YB + 2 * g:YB + 2 * g + 2, cols(ch)],
                                     bank(4 * g + 2, 0, 256).rearrange("p (a t) -> p a t", a=2),
                                     ACT.Copy).then_inc(act_s[g].sem, 1)

                    for ch in range(NT):
                        for step in (token_major, inverse, right_side, taken_up, output):
                            for g in range(2):
                                step(g, ch)
            for g in range(2):
                pe_s[g].close(PE_YZ * NT)
                dve_s[g].close(DVE_Z * NT)
                act_s[g].close(ACT_Y * NT)

        def stage_rwkv_out():
            norm(wt(YB), [[0], [1], [2], [3]], HD, GN_EPS, lambda t: v("ln_x_w", t), wt(YB), c("same_head"),
                 centre=True, bias=lambda t: v("ln_x_b", t), sq0=18)
            with nc.Block() as block:
                @block.vector
                def _(dve):
                    for t in range(4):
                        y = w[:, YB + t, :]
                        dve_chain.link(dve, V.tensor_tensor(y, y, w[:, BO + t, :], ALU.add))
                        dve_chain.link(dve, V.tensor_tensor(y, y, w[:, GG + t, :], ALU.mult))


        def stage_merge():
            GA, MG = 24, 28

            def part(a):
                return lambda half, k: mix_split[:, half, a + k, :]

            u0 = wts.block // UNIT
            with nc.Block() as block:
                @block.tensor
                def _(pe):
                    for m in range(KD):
                        for j, (n_k, src) in enumerate(((KD, of(xs)), (KD, of(xs)), (KH, part(4)), (KH, part(0)))):
                            n = 4 * m + j
                            if n >= 8:
                                if j < 2:
                                    pe.wait_ge(tile_read.sem, tile_read.at(2 * (m - 2) + j + 1))
                                else:
                                    pe.wait_ge(dve_out.sem, dve_out.at(2 * (m - 2) + j - 1))
                            split_product(pe, bank(n % 8), n_k, src, tile_ready, n + 1)

                weight_programs(block, act=False)

                @block.scalar
                def _(act):
                    def high(m):
                        act.wait_ge(dve_out.sem, dve_out.at(2 * m + 2))
                        S.activation(merged_split[:, 0, m, :], w[:, MG + m % 2, :], ACT.Copy).then_inc(high_out.sem, 1)

                    for m in range(KD):
                        for j in range(2):
                            n = 4 * m + j
                            wts.round_high(act, S, u0 + 3 * m + j + SPLIT)
                            act.wait_ge(tile_ready.sem, tile_ready.at(n + 1))
                            if m >= 2:
                                act.wait_ge(dve_out.sem, dve_out.at(2 * (m - 2) + 2))
                            S.activation(w[:, GA + 2 * (m % 2) + j, :], bank(n % 8),
                                         ACT.Sigmoid, bias=v("gate_bias", 8 * j + m)).then_inc(tile_read.sem, 1)
                        wts.round_high(act, S, u0 + 3 * m + 2 + SPLIT)
                        high(m)
                    wts.round_high(act, S)

                @block.vector
                def _(dve):
                    for m in range(KD):
                        ga, gb = w[:, GA + 2 * (m % 2), :], w[:, GA + 2 * (m % 2) + 1, :]
                        mg = w[:, MG + m % 2, :]
                        dve.wait_ge(tile_ready.sem, tile_ready.at(4 * m + 3))
                        dve.wait_ge(tile_read.sem, tile_read.at(2 * m + 1))
                        V.tensor_tensor(mg, bank((4 * m + 2) % 8), ga, ALU.mult).then_inc(dve_out.sem, 1)
                        dve.wait_ge(tile_ready.sem, tile_ready.at(4 * m + 4))
                        dve.wait_ge(tile_read.sem, tile_read.at(2 * m + 2))
                        dve_chain.link(dve, V.tensor_tensor(gb, bank((4 * m + 3) % 8), gb, ALU.mult))
                        dve.wait_ge(dve_out.sem, dve_out.at(2 * m + 1))
                        V.tensor_tensor(mg, mg, gb, ALU.add).then_inc(dve_out.sem, 1)
                        dve.wait_ge(high_out.sem, high_out.at(m + 1))
                        dve_chain.link(dve, V.tensor_tensor(merged_split[:, 1, m, :], mg,
                                                            merged_split[:, 0, m, :].bitcast(F32), ALU.subtract))
            tile_ready.close(4 * KD)
            tile_read.close(2 * KD)
            dve_out.close(2 * KD)
            high_out.close(KD)

        def stage_linear(n_k, src, mode, out=None):
            with nc.Block() as block:
                @block.tensor
                def _(pe):
                    product(pe, KD, n_k, src)

                weight_programs(block)

                @block.vector
                def _(dve):
                    for m in range(KD):
                        dve.wait_ge(tile_ready.sem, tile_ready.at(m + 1))
                        if mode == "residual":
                            ins = V.scalar_tensor_tensor(xt(m), xt(m), ALPHA, bank(m % 4), ALU.mult, ALU.add)
                        elif mode == "add":
                            ins = V.tensor_tensor(out(m), out(m), bank(m % 4), ALU.add)
                        else:
                            ins = V.tensor_copy(out(m), bank(m % 4))
                        ins.then_inc(tile_read.sem, 1)
            tile_ready.close(KD)
            tile_read.close(KD)

        def stage_relu2_up():
            n_tiles = FF1 // 2
            RL, SQ = 32, 34
            u0 = wts.block // UNIT
            with nc.Block() as block:
                @block.tensor
                def _(pe):
                    product(pe, n_tiles, KD, of(xs))

                weight_programs(block, act=False)

                @block.scalar
                def _(act):
                    def high(m):
                        act.wait_ge(dve_out.sem, dve_out.at(m + 1))
                        S.activation(hidden1[:, 0, m, :], w[:, SQ + m % 2, :], ACT.Copy).then_inc(high_out.sem, 1)

                    for m in range(n_tiles):
                        wts.round_high(act, S, u0 + m + SPLIT)
                        act.wait_ge(tile_ready.sem, tile_ready.at(m + 1))
                        if m >= 2:
                            act.wait_ge(dve_out.sem, dve_out.at(m - 1))
                        S.activation(w[:, RL + m % 2, :], bank(m % 4), ACT.Relu).then_inc(tile_read.sem, 1)
                        high(m)

                @block.vector
                def _(dve):
                    for m in range(n_tiles):
                        r, q = w[:, RL + m % 2, :], w[:, SQ + m % 2, :]
                        dve.wait_ge(tile_read.sem, tile_read.at(m + 1))
                        V.tensor_tensor(q, r, r, ALU.mult).then_inc(dve_out.sem, 1)
                        dve.wait_ge(high_out.sem, high_out.at(m + 1))
                        dve_chain.link(dve, V.tensor_tensor(hidden1[:, 1, m, :], q,
                                                            hidden1[:, 0, m, :].bitcast(F32), ALU.subtract))
            tile_ready.close(n_tiles)
            tile_read.close(n_tiles)
            dve_out.close(n_tiles)
            high_out.close(n_tiles)

        ROWS = 28
        ML_PARTS, FORGET_PARTS = ROWS + 4, ROWS + 5
        HM, HF2 = 0, 16

        def stage_even_in():
            scale = {0: float(P) ** -0.5, 4: HD ** -0.5}
            u0 = wts.block // UNIT
            with nc.Block() as block:
                @block.tensor
                def _(pe):
                    product(pe, 28, KD, of(xs))
                    for j, (a, n) in enumerate(((0, 4), (4, 4), (8, 8))):
                        for k in range(KD):
                            g = v("ev_gates", 16 * k + a, n)
                            ins = TE.matmul(ps[0:n, 4 + j, :], g, xt(k), start=(k == 0), stop=(k == KD - 1))
                        ins.then_inc(pe_out.sem, 1)

                weight_programs(block, act=False)

                @block.vector
                def _(dve):
                    for m in range(28):
                        dve.wait_ge(tile_ready.sem, tile_ready.at(m + 1))
                        V.tensor_scalar(w[:, m, :], bank(m % 4), v("ev_b", m), scale.get(m // 4, 1.0), ALU.add,
                                        ALU.mult).then_inc(tile_read.sem, 1)
                    dve.wait_ge(pe_out.sem, pe_out.at(3))
                    for j, (n, b) in enumerate(((4, "ev_bi"), (4, "ev_bf"), (8, "ev_bff"))):
                        dve_chain.link(dve, V.tensor_scalar(w[0:n, ROWS + j, :], ps[0:n, 4 + j, :], v(b, rows=n), None,
                                                            ALU.add))
                    for j, n in ((1, 4), (2, 8)):
                        z, tmp, out = (w[0:n, ROWS + j + a, :] for a in (0, 3, 5))
                        dve_chain.link(dve, V.tensor_scalar(tmp, z, -1.0, None, ALU.mult))
                        V.tensor_tensor(tmp, z, tmp, ALU.max).then_inc(dve_out.sem, 1)
                        dve.wait_ge(act_out.sem, act_out.at(j))
                        dve_chain.link(dve, V.tensor_scalar(out, z, 0.0, None, ALU.min))
                        dve_chain.link(dve, V.tensor_tensor(out, out, tmp, ALU.subtract))
                        dve_chain.link(dve, V.tensor_tensor_scan(z, ones[0:n, :], out, 0.0, ALU.mult, ALU.add))
                    V.tensor_tensor(w[0:4, ROWS, :], w[0:4, ROWS, :], w[0:4, ROWS + 1, :], ALU.subtract)
                    dve_chain.link(dve, V.tensor_scalar(w[0:8, ROWS + 3, :], w[0:8, ROWS + 2, :], -1.0, None, ALU.mult))

                @block.scalar
                def _(act):
                    wts.round_high(act, S)
                    for j, n in ((1, 4), (2, 8)):
                        tmp = w[0:n, ROWS + j + 3, :]
                        act.wait_ge(dve_out.sem, dve_out.at(j))
                        act_chain.link(act, S.activation(tmp, tmp, ACT.Exp, scale=-1.0))
                        S.activation(tmp, tmp, ACT.Ln, bias=ones[0:n, 0:1]).then_inc(act_out.sem, 1)
            tile_ready.close(28)
            tile_read.close(28)
            pe_out.close(3)
            act_out.close(2)
            dve_out.close(2)
            with nc.Block() as block:
                @block.tensor
                def _(pe):
                    for i in range(NT):
                        ins = TE.matmul(bank(0, 4 * i, 4), w[0:4, ROWS + 1, tok(0, i)], c("ident", 0, 4, rows=4),
                                        start=True, stop=True)
                    ins.then_inc(tile_ready.sem, 1)

                @block.vector
                def _(dve):
                    dve.wait_ge(tile_ready.sem, tile_ready.at(1))
                    dve_chain.link(dve, V.tensor_copy(col[:, 16:32], bank(0, 0, 16)))
                    dve_chain.link(dve, V.memset(w[:, ML_PARTS:ML_PARTS + 2, :], 0.0))
                    for n, first, tile in ((4, (ROWS + 1, ROWS), ML_PARTS), (8, (ROWS + 2, ROWS + 3), FORGET_PARTS)):
                        for j in range(2):
                            split_rows(dve, w[0:n, first[j], :], n, tile, j, ROWS + 6, ROWS + 7)
            tile_ready.close(1)

        def stage_ml_gate():
            with nc.Block() as block:
                @block.scalar
                def _(act):
                    for t in range(4):
                        S.activation(w[:, 12 + t, :], w[:, 12 + t, :], ACT.Sigmoid).then_inc(act_out.sem, 1)

                @block.vector
                def _(dve):
                    for t in range(4):
                        dve.wait_ge(act_out.sem, act_out.at(t + 1))
                        V.tensor_tensor(w[:, HM + t, :], w[:, HM + t, :], w[:, 12 + t, :], ALU.mult)
            act_out.close(4)

        def stage_conv_ffn_up(layer):
            y0 = 2 * FF2
            u0 = wts.block // UNIT
            with nc.Block() as block:
                @block.tensor
                def _(pe):
                    product(pe, 2 * FF2, KD, of(xs))

                weight_programs(block, act=False)

                def taps(m):
                    ch = layer * 132 + (m % 2) * FF2 + m // 2
                    return [v("ffn_w", ch + 44 * i) for i in range(3)]

                @block.scalar
                def _(act):
                    def gate(j):
                        act.wait_ge(tile_read.sem, tile_read.at(2 * j + 2))
                        S.activation(w[:, y0 + 4 + j % 2, :], w[:, y0 + (2 * j + 1) % 4, :], ACT.Sigmoid
                                     ).then_inc(act_out2.sem, 1)
                        act.wait_ge(dve_out.sem, dve_out.at(j + 1))
                        S.activation(hidden2[:, 0, j, :], w[:, y0 + 2 * j % 4, :], ACT.Copy).then_inc(high_out.sem, 1)

                    for m in range(2 * FF2):
                        wts.round_high(act, S, u0 + m + SPLIT)
                        act.wait_ge(tile_ready.sem, tile_ready.at(m + 1))
                        if m >= 4:
                            act.wait_ge(dve_out2.sem, dve_out2.at((m - 4) // 2 + 1))
                        S.activation(w[:, y0 + m % 4, :], bank(m % 4), ACT.Identity, scale=taps(m)[2],
                                     bias=v("ffn_b", layer * 44 + (m % 2) * FF2 + m // 2)).then_inc(act_out.sem, 1)
                        if m % 2 == 0 and m >= 2:
                            gate(m // 2 - 1)
                    gate(FF2 - 1)

                @block.vector
                def _(dve):
                    def conv(m):
                        y, b = w[:, y0 + m % 4, :], bank(m % 4)
                        dve.wait_ge(act_out.sem, act_out.at(m + 1))
                        dve_chain.link(dve, V.scalar_tensor_tensor(y[:, 1:T], b[:, 0:T - 1], taps(m)[1], y[:, 1:T],
                                                                   ALU.mult, ALU.add))
                        V.scalar_tensor_tensor(y[:, 2:T], b[:, 0:T - 2], taps(m)[0], y[:, 2:T], ALU.mult,
                                               ALU.add).then_inc(tile_read.sem, 1)

                    def join(j):
                        act_gate = w[:, y0 + 4 + j % 2, :]
                        value = w[:, y0 + 2 * j % 4, :]
                        dve.wait_ge(act_out2.sem, act_out2.at(j + 1))
                        dve_chain.link(dve, V.tensor_tensor(act_gate, act_gate, w[:, y0 + (2 * j + 1) % 4, :], ALU.mult))
                        V.tensor_tensor(value, act_gate, value, ALU.mult).then_inc(dve_out.sem, 1)
                        dve.wait_ge(high_out.sem, high_out.at(j + 1))
                        V.tensor_tensor(hidden2[:, 1, j, :], value, hidden2[:, 0, j, :].bitcast(F32),
                                        ALU.subtract).then_inc(dve_out2.sem, 1)

                    for m in range(2 * FF2):
                        conv(m)
                        if m % 2 == 0 and m >= 2:
                            join(m // 2 - 1)
                    join(FF2 - 1)
            tile_ready.close(2 * FF2)
            tile_read.close(2 * FF2)
            act_out.close(2 * FF2)
            act_out2.close(FF2)
            dve_out.close(FF2)
            high_out.close(FF2)
            dve_out2.close(FF2)

        def layer_norm(name, layer, split=None):
            norm(xt, [list(range(KD))], D, LN_EPS, lambda t: v(name + "_g", KD * layer + t), xt, ones[:, 0:P],
                 centre=True, bias=lambda t: v(name + "_b", KD * layer + t), sq0=0, split=split)

        ZG, XS, BM, CMM, PL = 0, 4, 8, 10, 12
        ROWS2, SSD_PARTS = 40, 44
        XTK, YS, PO = 16, 20, 24

        def stage_odd_in():
            y0 = 46
            u0 = wts.block // UNIT
            with nc.Block() as block:
                @block.tensor
                def _(pe):
                    product(pe, 16, KD, of(xs))
                    for k in range(KD):
                        ins = TE.matmul(ps[0:8, 4, :], v("od_dt", 8 * k, 8), xt(k), start=(k == 0), stop=(k == KD - 1))
                    ins.then_inc(pe_out.sem, 1)

                weight_programs(block, act=False)

                @block.scalar
                def _(act):
                    for m in range(16):
                        wts.round_high(act, S, u0 + m + SPLIT)
                        if not 4 <= m < 12:
                            continue
                        act.wait_ge(tile_ready.sem, tile_ready.at(m + 1))
                        S.activation(w[:, m, :], bank(m % 4), ACT.Identity, scale=v("conv_w", 24 + m - 4),
                                     bias=v("conv_b", m - 4)).then_inc(act_out.sem, 1)
                        act.wait_ge(tile_read.sem, tile_read.at(m + 1))
                        S.activation(w[:, y0 + m % 2, :], w[:, m, :], ACT.Sigmoid).then_inc(act_out2.sem, 1)
                    wts.round_high(act, S)

                @block.vector
                def _(dve):
                    for m in range(16):
                        y, b = w[:, m, :], bank(m % 4)
                        dve.wait_ge(tile_ready.sem, tile_ready.at(m + 1))
                        if 4 <= m < 12:
                            dve.wait_ge(act_out.sem, act_out.at(m - 3))
                            for i, s in ((2, 1), (1, 2), (0, 3)):
                                ins = V.scalar_tensor_tensor(y[:, s:T], b[:, 0:T - s], v("conv_w", 8 * i + m - 4),
                                                             y[:, s:T], ALU.mult, ALU.add)
                                if i:
                                    dve_chain.link(dve, ins)
                            ins.then_inc(tile_read.sem, 1)
                            dve.wait_ge(act_out2.sem, act_out2.at(m - 3))
                            dve_chain.link(dve, V.tensor_tensor(y, y, w[:, y0 + m % 2, :], ALU.mult))
                        else:
                            V.tensor_copy(y, b).then_inc(tile_read.sem, 1)
            tile_ready.close(16)
            tile_read.close(16)
            act_out.close(8)
            act_out2.close(8)
            dt, tmp, acs, ncs = (w[0:8, ROWS2 + i, :] for i in range(4))
            with nc.Block() as block:
                @block.vector
                def _(dve):
                    dve.wait_ge(pe_out.sem, pe_out.at(1))
                    dve_chain.link(dve, V.tensor_scalar(acs, ps[0:8, 4, :], v("dt_bias", rows=8), None, ALU.add))
                    dve_chain.link(dve, V.tensor_scalar(tmp, acs, -1.0, None, ALU.mult))
                    V.tensor_tensor(tmp, acs, tmp, ALU.max).then_inc(dve_out.sem, 1)
                    dve.wait_ge(act_out.sem, act_out.at(1))
                    dve_chain.link(dve, V.tensor_scalar(dt, acs, 0.0, None, ALU.max))
                    dve_chain.link(dve, V.tensor_tensor(dt, dt, tmp, ALU.add))
                    dve_chain.link(dve, V.tensor_scalar(tmp, dt, col[0:8, 8:9], -1.0, ALU.mult, ALU.mult))
                    dve_chain.link(dve, V.tensor_tensor_scan(acs, ones[0:8, :], tmp, 0.0, ALU.mult, ALU.add))
                    dve_chain.link(dve, V.tensor_scalar(ncs, acs, -1.0, None, ALU.mult))

                @block.scalar
                def _(act):
                    act_chain.link(act, S.activation(col[0:8, 8:9], v("a_log", rows=8), ACT.Exp))
                    act.wait_ge(dve_out.sem, dve_out.at(1))
                    act_chain.link(act, S.activation(tmp, tmp, ACT.Exp, scale=-1.0))
                    S.activation(tmp, tmp, ACT.Ln, bias=ones[0:8, 0:1]).then_inc(act_out.sem, 1)
            pe_out.close(1)
            dve_out.close(1)
            act_out.close(1)
            with nc.Block() as block:
                @block.tensor
                def _(pe):
                    for i in range(NT):
                        ins = TE.matmul(bank(0, 8 * i, 8), w[0:8, ROWS2, tok(0, i)], c("ident", 0, 8, rows=8),
                                        start=True, stop=True)
                    ins.then_inc(tile_ready.sem, 1)

                @block.vector
                def _(dve):
                    dve.wait_ge(tile_ready.sem, tile_ready.at(1))
                    dve_chain.link(dve, V.tensor_copy(col[:, 16:48], bank(0, 0, 32)))
                    dve_chain.link(dve, V.memset(w[:, SSD_PARTS, :], 0.0))
                    for j in range(2):
                        split_rows(dve, w[0:8, ROWS2 + 2 + j, :], 8, SSD_PARTS, j, ROWS2 + 5, ROWS2 + 1)
            tile_ready.close(1)

        def stage_ssd():
            items = [(g, j, hh) for g in range(2) for j in range(NT) for hh in range(4)]
            n_items = len(items)
            e = [w[:, 46, :], w[:, 47, :]]
            m_ = [w[:, 48, :], w[:, 49, :]]
            with nc.Block() as block:
                @block.tensor
                def _(pe):
                    def decay(n):
                        g, j, hh = items[n]
                        a, wd = j * P, T - j * P
                        hd = 4 * g + hh
                        if hh == 0:
                            if n >= 8:
                                pe.wait_ge(dve_out.sem, dve_out.at(n - 4))
                            TE.matmul(bank((n // 4) % 2, 0, wd), w[:, BM + g, a:a + P], w[:, CMM + g, a:T],
                                      start=True, stop=True)
                        if n >= 2:
                            pe.wait_ge(act_out.sem, act_out.at(n - 1))
                        d = bank(2 + n % 2, 0, wd)
                        TE.matmul(d, one_hot(hd, P), row_parts(SSD_PARTS, 0)[:, a:T], start=True, stop=False)
                        TE.matmul(d, row_parts(SSD_PARTS, 1)[:, a:a + P], one_hot(hd, wd), start=False, stop=False)
                        TE.matmul(bank(2 + n % 2, 0, P), ident_h[:, :], diag_st_h[:, :], start=False,
                                  stop=True).then_inc(tile_ready.sem, 1)

                    def values(n):
                        g, j, hh = items[n]
                        hd = 4 * g + hh
                        pe.wait_ge(dve_out.sem, dve_out.at(n + 1))
                        TE.matmul(bank(4 + hd // 2, j * P, T - j * P, half(hd)), w[:, XTK + j, hd * HD:(hd + 1) * HD],
                                  m_[n % 2][:, 0:T - j * P], start=(j == 0), stop=(j == NT - 1)
                                  ).then_inc(pe_out.sem, 1)

                    decay(0)
                    for n in range(n_items):
                        if n + 1 < n_items:
                            decay(n + 1)
                        values(n)

                @block.scalar
                def _(act):
                    for n, (g, j, hh) in enumerate(items):
                        wd = T - j * P
                        act.wait_ge(tile_ready.sem, tile_ready.at(n + 1))
                        if n >= 2:
                            act.wait_ge(dve_out.sem, dve_out.at(n - 1))
                        S.activation(e[n % 2][:, 0:wd], bank(2 + n % 2, 0, wd), ACT.Exp).then_inc(act_out.sem, 1)
                    for t in range(4):
                        S.activation(w[:, 32 + t, :], w[:, ZG + t, :], ACT.Sigmoid).then_inc(act_out2.sem, 1)

                @block.vector
                def _(dve):
                    for n, (g, j, hh) in enumerate(items):
                        wd = T - j * P
                        dve.wait_ge(act_out.sem, act_out.at(n + 1))
                        if n >= 2:
                            dve.wait_ge(pe_out.sem, pe_out.at(n - 1))
                        V.tensor_tensor(m_[n % 2][:, 0:wd], bank((n // 4) % 2, 0, wd), e[n % 2][:, 0:wd],
                                        ALU.mult).then_inc(dve_out.sem, 1)
                    dve.wait_ge(pe_out.sem, pe_out.at(n_items))
                    for t in range(4):
                        y, z = w[:, YS + t, :], w[:, ZG + t, :]
                        dve_chain.link(dve, V.scalar_tensor_tensor(y, w[:, XS + t, :], v("d_skip", t), bank(4 + t),
                                                                   ALU.mult, ALU.add))
                        dve.wait_ge(act_out2.sem, act_out2.at(t + 1))
                        dve_chain.link(dve, V.tensor_tensor(z, z, w[:, 32 + t, :], ALU.mult))
                        dve_chain.link(dve, V.tensor_tensor(y, y, z, ALU.mult))
            tile_ready.close(n_items)
            pe_out.close(n_items)
            act_out.close(n_items)
            act_out2.close(4)
            dve_out.close(n_items)

        def stage_pool():
            with nc.Block() as block:
                @block.vector
                def _(dve):
                    for g, win in enumerate(WINDOWS):
                        u = w[:, PL + g, :]
                        a, b = w[:, PO + g, :], w[:, 28 + g, :]
                        src, s = u, 1
                        while s < win:
                            dst = a if src is not a else b
                            V.tensor_copy(dst[:, 0:s], src[:, 0:s])
                            dve_chain.link(dve, V.tensor_tensor(dst[:, s:T], src[:, s:T], src[:, 0:T - s], ALU.add))
                            src, s = dst, 2 * s
                        V.tensor_scalar(src[:, 16:T], src[:, 16:T], 1.0 / win, None, ALU.mult)
                        dve_chain.link(dve, V.tensor_tensor(src[:, 0:16], src[:, 0:16], c("inv_count", 16 * g, 16),
                                                            ALU.mult))
                        V.tensor_tensor(a, src, u, ALU.subtract).then_inc(dve_out.sem, 1)
                        dve.wait_ge(dve_out.sem, dve_out.at(g + 1))
                    for g in range(4):
                        dve.wait_ge(tile_ready.sem, tile_ready.at(g + 1))
                        dve_chain.link(dve, V.tensor_scalar(w[:, PO + g, :], bank(g), v("pool_b", g),
                                                            v("pool_scale", g), ALU.add, ALU.mult))

                @block.tensor
                def _(pe):
                    for g in range(4):
                        pe.wait_ge(dve_out.sem, dve_out.at(g + 1))
                        TE.matmul(bank(g), v("pool_w", g * P, P), w[:, PO + g, :], start=True,
                                  stop=True).then_inc(tile_ready.sem, 1)
            dve_out.close(4)
            tile_ready.close(4)

        def stage_store():
            with nc.Block() as block:
                @block.sync
                def _(sp):
                    sp.dma_start(out_t.rearrange("(k p) t -> p k t", p=P), x[:, :, :]).then_inc(dma_out.sem, 16)
                    sp.wait_ge(dma_out.sem, dma_out.at(16))
            dma_out.close(16)

        all_d = ones[:, 0:P]
        tiles8 = [list(range(KD))]
        steps = [
            ("inputs", stage_inputs),
            ("norm1", lambda: norm(xt, tiles8, D, RMS_EPS, lambda t: v("pre_mix_g", t), wt(40), all_d, sq0=30,
                                   split=xs)),
            ("qkv", stage_qkv),
            ("v_tok", lambda: to_token_major([(Q1 + 8, 28)])),
            ("band", lambda: attention("band", Q1, Q1 + 4, 28, YA, 32, bias0=20)),
            ("rwkv_in", stage_rwkv_in),
            ("rwkv_prep", stage_rwkv_prepare),
            ("rwkv_chunks", stage_rwkv_chunks),
            ("rwkv_out", stage_rwkv_out),
            ("mix_split", lambda: split_tiles(wt(0), mix_split)),
            ("merge", stage_merge),
            ("w_out", lambda: stage_linear(KD, of(merged_split), "copy", wt(0))),
            ("post_mix", lambda: norm(wt(0), tiles8, D, RMS_EPS, lambda t: v("post_mix_g", t), None, all_d,
                                      add_to=xt, sq0=8)),
            ("pre_ffn", lambda: norm(xt, tiles8, D, RMS_EPS, lambda t: v("pre_ffn_g", t), wt(20), all_d, sq0=8,
                                     split=xs)),
            ("up_a", stage_relu2_up),
            ("down_a", lambda: stage_linear(FF1 // 2, of(hidden1), "copy", wt(36))),
            ("up_b", stage_relu2_up),
            ("down_b", lambda: stage_linear(FF1 // 2, of(hidden1), "add", wt(36))),
            ("post_ffn", lambda: norm(wt(36), tiles8, D, RMS_EPS, lambda t: v("post_ffn_g", t), None, all_d,
                                      add_to=xt, sq0=0, split=xs)),
            ("even_in", stage_even_in),
            ("ml_tok", lambda: to_token_major([(8, 36), (24, 40)])),
            ("mlstm", lambda: attention("mlstm", 0, 4, 36, HM, 44, parts=ML_PARTS,
                                        f_cols=lambda i, hd: col[:, 16 + 4 * i + hd:17 + 4 * i + hd])),
            ("ml_norm", lambda: norm(wt(HM), [[0], [1], [2], [3]], P, LN_EPS, lambda t: v("ml_norm", t), wt(HM),
                                     all_d, centre=True, sq0=4, factor0=8)),
            ("ml_gate", stage_ml_gate),
            ("forget", lambda: attention("forget", 16, 20, 40, HF2, 44, parts=FORGET_PARTS)),
            ("even_split", lambda: split_tiles(lambda t: w[:, t if t < 4 else HF2 + t - 4, :], even_split)),
            ("even_out", lambda: stage_linear(KD, of(even_split), "residual")),
            ("ln1_0", lambda: layer_norm("ln1", 0, xs)),
            ("ffn_up_0", lambda: stage_conv_ffn_up(0)),
            ("ffn_down_0", lambda: stage_linear(FF2, of(hidden2), "residual")),
            ("ln2_0", lambda: layer_norm("ln2", 0, xs)),
            ("odd_in", stage_odd_in),
            ("x_tok", lambda: to_token_major([(XS, XTK)], scaled=lambda i: col[:, 16 + 8 * i:24 + 8 * i])),
            ("ssd", stage_ssd),
            ("ssm_norm", lambda: norm(wt(YS), [[0, 1, 2, 3]], HALF, LN_EPS, lambda t: v("ssm_norm", t), wt(YS),
                                      all_d, sq0=28)),
            ("pool", stage_pool),
            ("odd_split", lambda: split_tiles(wt(YS), odd_split)),
            ("odd_out", lambda: stage_linear(KD, of(odd_split), "residual")),
            ("ln1_1", lambda: layer_norm("ln1", 1, xs)),
            ("ffn_up_1", lambda: stage_conv_ffn_up(1)),
            ("ffn_down_1", lambda: stage_linear(FF2, of(hidden2), "residual")),
            ("ln2_1", lambda: layer_norm("ln2", 1)),
        ]
        for name, run in steps:
            run()
            if name == upto:
                break
        stage_store()
        if upto is None:
            assert wts.block == n_units * UNIT, (wts.block, n_units * UNIT)


def blocks(m):
    k, n = m.shape
    return m.reshape(k // P, P, n // P, P).transpose(2, 0, 1, 3).reshape(-1, P, P)


def weight_stream(a):
    w_in, ev, od = a["w_in"][0], a["ev_w_in_2"][0], a["od_w_in_2"][0]
    gates = blocks(w_in[:, 3328:]).reshape(2, KD, KD, P, P)
    pa, pb = (blocks(a[n][0]).reshape(KD, KH, P, P) for n in ("proj_a", "proj_b"))
    parts = [blocks(w_in[:, :3328])]
    for m in range(KD):
        parts += [gates[0, m], gates[1, m], pa[m], pb[m]]
    up, down, half = a["w_up"][0], a["w_down"][0], FF1 // 2 * P
    parts += [blocks(a["w_out"][0]), blocks(up[:, :half]), blocks(down[:half]), blocks(up[:, half:]),
              blocks(down[half:]), blocks(ev[:, 0:2048]), blocks(ev[:, 2056:3592]), blocks(a["ev_w_out_2"][0])]

    def ffn(layer):
        up = blocks(a["ffn_w_up_2"][layer]).reshape(2, FF2, KD, P, P).transpose(1, 0, 2, 3, 4)
        return [up.reshape(-1, P, P), blocks(a["ffn_w_down_2"][layer])]

    parts += ffn(0)
    parts += [blocks(od[:, 0:1536]), blocks(od[:, 1544:2056]), blocks(a["od_w_out_2"][0])]
    parts += ffn(1)
    flat = np.concatenate(parts)
    return np.ascontiguousarray(flat.reshape(-1, UNIT, P, P).transpose(0, 2, 1, 3)).reshape(-1, P, UNIT * P)


def vector_array(a):
    cols, n = columns(VECTORS)
    out = np.zeros((P, n), np.float32)

    def put(name, m, rows=P):
        at, k = cols[name]
        out[0:rows, at:at + k] = m

    def tiled(m):
        return m.reshape(-1, P).T

    for name in ("pre_mix_g", "gate_bias", "shift_mu", "w0", "a0", "k_k", "k_a", "r_k", "ln_x_w", "ln_x_b",
                 "post_mix_g", "pre_ffn_g", "post_ffn_g"):
        put(name, tiled(a[name]))
    b = a["ev_b_in_2"][0]
    put("ev_b", tiled(np.concatenate([b[0:2048], b[2056:3592]])))
    put("ev_bi", b[2048:2052, None], 4)
    put("ev_bf", b[2052:2056, None], 4)
    put("ev_bff", b[3592:3600, None], 8)
    put("ml_norm", tiled(a["ev_ml_norm_2"]))
    put("conv_w", tiled(a["od_conv_w_2"]))
    put("conv_b", tiled(a["od_conv_b_2"]))
    put("dt_bias", a["od_dt_bias_2"][0][:, None], 8)
    put("a_log", a["od_a_log_2"][0][:, None], 8)
    put("d_skip", tiled(np.repeat(a["od_d_skip_2"][0], HD)))
    put("ssm_norm", tiled(a["od_ssm_norm_2"]))
    put("pool_b", tiled(a["od_pool_b_2"]))
    put("pool_scale", tiled(a["od_pool_scale_2"]))
    put("ffn_w", tiled(a["ffn_conv_w_2"]))
    put("ffn_b", tiled(a["ffn_conv_b_2"]))
    for n1 in ("ln1_g", "ln1_b", "ln2_g", "ln2_b"):
        put(n1, tiled(a[n1 + "_2"]))
    put("w2a2", np.concatenate([a["w2"][0], a["a2"][0]]))
    put("g2", a["g2"][0])
    ev, od = a["ev_w_in_2"][0], a["od_w_in_2"][0]

    def narrow(m):
        return m.reshape(KD, P, -1).transpose(1, 0, 2).reshape(P, -1)

    put("ev_gates", narrow(np.concatenate([ev[:, 2048:2056], ev[:, 3592:3600]], axis=1)))
    put("od_dt", narrow(od[:, 1536:1544]))
    put("pool_w", a["od_pool_w_2"][0].transpose(1, 0, 2).reshape(P, -1))
    return out


def constant_array():
    cols, n = columns(CONSTANTS)
    out = np.zeros((P, n), np.float32)
    i = np.arange(P)
    row, colm = i[:, None], i[None, :]

    def put(name, m):
        at, k = cols[name]
        out[:, at:at + k] = m

    put("ident", row == colm)
    put("flip", row + colm == P - 1)
    put("same_head", row // HD == colm // HD)
    levels = []
    for l in range(LEVELS):
        s = 1 << l
        levels.append((row // (2 * s) == colm // (2 * s)) & (row % (2 * s) >= s) & (colm % (2 * s) < s))
    put("levels", np.concatenate(levels, axis=1))
    put("level0_t", levels[0].T)
    put("mask4", np.concatenate([row < colm, row <= colm, row < colm, row <= colm], axis=1))
    put("diag_qk", np.where(colm > row, NEG, 0.0))
    put("diag_st", np.where(colm < row, NEG, 0.0))
    t = np.arange(16)
    put("inv_count", np.concatenate([1.0 / np.minimum(t + 1, win) for win in WINDOWS])[None])
    put("eps", np.array([[RMS_EPS, LN_EPS, GN_EPS]]))
    return out


UPTO = None


def kernel(**inputs):
    import concourse.bacc as bacc
    from concourse.bass_utils import run_bass_kernel_spmd

    a = {k: np.asarray(m) for k, m in inputs.items()}
    arrays = {
        "x_t": np.ascontiguousarray(a["x"][0].T),
        "vectors": vector_array(a),
        "constants": constant_array(),
        "rel_rev": np.ascontiguousarray(a["rel_bias"][0][:, ::-1]),
        "stream": weight_stream(a),
    }
    nc = bacc.Bacc("TRN2", target_bir_lowering=False, num_devices=1)
    args = {k: nc.dram_tensor(k, m.shape, mybir.dt.from_np(m.dtype), kind="ExternalInput").ap()
            for k, m in arrays.items()}
    line = nc.dram_tensor("bias_line", (HEADS, DIAG_PAD), F32, kind="Internal").ap()
    out = nc.dram_tensor("out_t", (D, T), F32, kind="ExternalOutput").ap()
    network(nc, **args, bias_line=line, out_t=out, upto=UPTO)
    r = run_bass_kernel_spmd(nc, [arrays], core_ids=[0])
    return np.ascontiguousarray(r.results[0]["out_t"].T)[None]
```

```python
from contextlib import ExitStack

import numpy as np

import concourse.bass as bass
from concourse import mybir


F32 = mybir.dt.float32
F32R = mybir.dt.float32r
BF16 = mybir.dt.bfloat16
I32 = mybir.dt.int32
ALU = mybir.AluOpType
ACT = mybir.ActivationFunctionType
AX_X = mybir.AxisListType.X

P = 128
T = 512
NT = T // P
D = 1024
KD = D // P
HALF = D // 2
KH = HALF // P
HEADS = 8
HD = 64
ML_HEADS = 4
BAND_BIAS = 320
REL_CLIP = 256
DIAG_PAD = 704
FF1 = 4096 // P
FF2 = 2816 // P
NEG = -1e30
RMS_EPS = 1e-6
LN_EPS = 1e-5
GN_EPS = HD * 1e-5
ALPHA = 4.0 ** 0.25
WINDOWS = (2, 4, 8, 16)
ODD_ORDER = (12, 4, 13, 5, 14, 6, 15, 7, 0, 8, 1, 9, 2, 10, 3, 11)
RWKV_ORDER = (12, 13, 4, 5, 6, 7, 0, 1, 2, 3, 8, 9, 10, 11)
LEVELS = 7

UNIT = 8
RING = 3
SPLIT = 3
WORK = 50

VECTORS = [("pre_mix_g", 8), ("gate_bias", 16), ("shift_mu", 14), ("w0", 4), ("a0", 4), ("k_k", 4),
           ("k_a", 4), ("r_k", 4), ("ln_x_w", 4), ("ln_x_b", 4), ("post_mix_g", 8), ("pre_ffn_g", 8),
           ("post_ffn_g", 8), ("ev_b", 28), ("ev_bi", 1), ("ev_bf", 1), ("ev_bff", 1), ("ml_norm", 4),
           ("conv_w", 32), ("conv_b", 8), ("dt_bias", 1), ("a_log", 1), ("d_skip", 4), ("ssm_norm", 4),
           ("pool_b", 4), ("pool_scale", 4), ("ffn_w", 264), ("ffn_b", 88), ("ln1_g", 16), ("ln1_b", 16),
           ("ln2_g", 16), ("ln2_b", 16), ("w2a2", 512), ("g2", 512), ("ev_gates", 128), ("od_dt", 64),
           ("pool_w", 512)]
CONSTANTS = [("ident", 128), ("flip", 128), ("same_head", 128), ("levels", 128 * LEVELS), ("level0_t", 128),
             ("mask4", 512), ("diag_qk", 128), ("diag_st", 128), ("inv_count", 64), ("eps", 3)]


def merge_order():
    order = [("gate", 0)]
    for m in range(KD):
        order += [("gate", m + 1)] if m + 1 < KD else []
        order += [("projection", m)]
    return order


def columns(spec):
    at, out = 0, {}
    for name, n in spec:
        out[name] = (at, n)
        at += n
    return out, at


class Signal:

    def __init__(self, sem):
        self.sem, self.base = sem, 0

    def at(self, n):
        return self.base + n

    def close(self, n):
        self.base += n


class Chain:

    def __init__(self, sem):
        self.sem, self.n = sem, 0

    def mark(self, ins):
        self.n += 1
        ins.then_inc(self.sem, 1)
        return self.n

    def link(self, eng, ins):
        eng.wait_ge(self.sem, self.mark(ins))


class Weights:

    def __init__(self, raw, split, landed, high_done, low_done, unit_used, source, n_units):
        self.raw, self.split, self.landed, self.source, self.n_units = raw, split, landed, source, n_units
        self.high_done, self.low_done, self.unit_used = high_done, low_done, unit_used
        self.block, self.loaded, self.highs, self.lows, self.used = 0, 0, 0, 0, 0
        self.release = []

    def take(self, pe):
        unit, i = divmod(self.block, UNIT)
        if i == 0:
            pe.wait_ge(self.low_done, unit + 1)
        self.block += 1
        return [self.split[:, unit % SPLIT, half, i * P:(i + 1) * P] for half in range(2)]

    def free(self, ins, signal=None, n=0):
        if self.block % UNIT == 0:
            if signal is None:
                self.used += 1
                ins.then_inc(self.unit_used, 1)
                self.release.append((self.unit_used, self.used))
            else:
                self.release.append((signal.sem, signal.at(n)))

    def ahead(self):
        return min(self.n_units, len(self.release) + SPLIT - 1)

    def load(self, sp, upto=None):
        while self.loaded < (min(self.n_units, self.ahead() + RING) if upto is None else upto):
            u = self.loaded
            if u >= RING:
                sp.wait_ge(self.low_done, u - RING + 1)
            sp.dma_start(self.raw[:, u % RING, :], self.source[u]).then_inc(self.landed[u % RING], 16)
            self.loaded += 1

    def round_high(self, act, scalar, upto=None):
        while self.highs < (self.ahead() if upto is None else min(self.ahead(), upto)):
            u = self.highs
            act.wait_ge(self.landed[u % RING], 16 * (u // RING + 1))
            if u >= SPLIT:
                act.wait_ge(*self.release[u - SPLIT])
            scalar.activation(self.split[:, u % SPLIT, 0, :], self.raw[:, u % RING, :],
                              ACT.Copy).then_inc(self.high_done, 1)
            self.highs += 1

    def subtract_low(self, pool, gpsimd, upto=None):
        while self.lows < (self.ahead() if upto is None else min(self.ahead(), upto)):
            u = self.lows
            pool.wait_ge(self.high_done, u + 1)
            gpsimd.tensor_tensor(self.split[:, u % SPLIT, 1, :], self.raw[:, u % RING, :],
                                 self.split[:, u % SPLIT, 0, :].bitcast(F32), ALU.subtract
                                 ).then_inc(self.low_done, 1)
            self.lows += 1


class Before:

    def __init__(self, pe, act, dve, pool, ready, counts, order=tuple(range(KD))):
        self.order = order
        self.pe, self.act, self.dve, self.pool, self.ready, self.counts = pe, act, dve, pool, ready, counts

    def count(self, signal):
        return sum(n for sig, n in self.counts if sig is signal)

    def close(self):
        for signal, n in self.counts:
            signal.close(n)


def network(nc, x_t, vectors, constants, rel_rev, stream, bias_line, out_t):
    n_units = stream.shape[0]
    ctx = ExitStack()
    with ctx:
        def sb(name, shape, dt=F32):
            return ctx.enter_context(nc.sbuf_tensor(name, shape, dt))

        def sem(name):
            return ctx.enter_context(nc.semaphore(name))

        x = sb("x", [P, KD, T])
        raw_units = sb("raw_units", [P, RING, UNIT * P])
        split_units = sb("split_units", [P, SPLIT, 2, UNIT * P], F32R)
        xs = sb("x_split", [P, 2, KD, T], F32R)
        arena_at = nc.sbuf_base
        w = sb("work", [P, WORK, T])

        def split_over(name, tile, n):
            return nc.alloc_sbuf_tensor_at(name, [P, 2, n, T], F32R, offset=arena_at + tile * T * 4)

        mix_split = split_over("mix_split", 8, KD)
        merged_split = split_over("merged_split", 30, KD)
        hidden1 = split_over("hidden1_split", 0, FF1 // 2)
        hidden2 = split_over("hidden2_split", 0, FF2)
        even_split = split_over("even_split", 20, KD)
        odd_split = split_over("odd_split", 0, KD)
        vec_cols, n_vec = columns(VECTORS)
        con_cols, n_con = columns(CONSTANTS)
        vec = sb("vec", [P, n_vec])
        con = sb("con", [P, n_con])
        ones = sb("ones", [P, T])
        col = sb("col", [P, 128])
        ident_h = sb("ident_h", [P, P], BF16)
        diag_qk_h = sb("diag_qk_h", [P, P], BF16)
        diag_st_h = sb("diag_st_h", [P, P], BF16)
        one_head = sb("one_head", [P, HEADS], BF16)
        ps = ctx.enter_context(nc.psum_tensor("ps", [P, 8, T], F32))

        def v(name, i=0, n=1, rows=P):
            a = vec_cols[name][0] + i
            return vec[0:rows, a:a + n]

        def c(name, i=0, n=None, rows=P):
            a, m = con_cols[name]
            return con[0:rows, a + i:a + i + (m if n is None else n)]

        ident = c("ident")
        eps_of = {RMS_EPS: c("eps", 0, 1), LN_EPS: c("eps", 1, 1), GN_EPS: c("eps", 2, 1)}
        one = ones[:, 0:1]

        dve_chain = Chain(sem("dve_chain"))
        act_chain = Chain(sem("act_chain"))
        pool_chain = Chain(sem("pool_chain"))
        x_landed = [sem(f"x_landed_{i}") for i in range(4)]
        con_landed, vec_landed, bias_landed = sem("con_landed"), sem("vec_landed"), sem("bias_landed")
        wts = Weights(raw_units, split_units, [sem(f"unit_landed_{i}") for i in range(RING)], sem("unit_high"),
                      sem("unit_low"), sem("unit_used"), stream, n_units)

        tile_ready = Signal(sem("tile_ready"))
        tile_read = Signal(sem("tile_read"))
        act_out = Signal(sem("act_out"))
        act_out2 = Signal(sem("act_out2"))
        dve_out = Signal(sem("dve_out"))
        dve_out2 = Signal(sem("dve_out2"))
        dve_out3 = Signal(sem("dve_out3"))
        high_out = Signal(sem("high_out"))
        pe_out = Signal(sem("pe_out"))
        pe_out2 = Signal(sem("pe_out2"))
        pe_out3 = Signal(sem("pe_out3"))
        dma_out = Signal(sem("dma_out"))
        norm_pe = Signal(sem("norm_pe"))
        norm_act = Signal(sem("norm_act"))
        norm_dve = Signal(sem("norm_dve"))
        norm_pool = Signal(sem("norm_pool"))
        norm_high = Signal(sem("norm_high"))
        norm_low = Signal(sem("norm_low"))
        norm_low2 = Signal(sem("norm_low2"))
        side_pe, side_act, side_dve = Signal(sem("side_pe")), Signal(sem("side_act")), Signal(sem("side_dve"))

        V, S, TE, G = nc.vector, nc.scalar, nc.tensor, nc.gpsimd

        def bank(b, a=0, n=T, rows=slice(0, P)):
            return ps[rows, b, a:a + n]

        def tok(k, c0, n=P):
            return slice(c0 * P, c0 * P + n)

        def half(hh):
            return slice(HD * (hh % 2), HD * (hh % 2) + HD)

        def split_product(pe, out, n_k, rhs, signal, n):
            for k in range(n_k):
                high, low = wts.take(pe)
                last = k == n_k - 1
                TE.matmul(out, high, rhs(0, k), start=(k == 0), stop=False)
                TE.matmul(out, high, rhs(1, k), start=False, stop=False)
                ins = TE.matmul(out, low, rhs(0, k), start=False, stop=last)
                wts.free(ins, signal if last else None, n)
            ins.then_inc(signal.sem, 1)

        def first_products(pe, rhs, before):
            unit = wts.block // UNIT
            for i, k in enumerate(before.order):
                before.ready(pe, k)
                for m in range(2):
                    if i == 0:
                        pe.wait_ge(wts.low_done, unit + m + 1)
                    high, low = (wts.split[:, (unit + m) % SPLIT, h, k * P:(k + 1) * P] for h in range(2))
                    last = i == UNIT - 1
                    TE.matmul(bank(m), high, rhs(0, k), start=(i == 0), stop=False)
                    TE.matmul(bank(m), high, rhs(1, k), start=False, stop=False)
                    ins = TE.matmul(bank(m), low, rhs(0, k), start=False, stop=last)
                    if last:
                        wts.block += UNIT
                        wts.free(ins, tile_ready, m + 1)
                        ins.then_inc(tile_ready.sem, 1)

        def product(pe, n_tiles, n_k, rhs, before=None, beside=None):
            if before is not None:
                before.pe(pe)
                first_products(pe, rhs, before)
                if beside is not None:
                    beside(pe, 1)
            for m in range(0 if before is None else 2, n_tiles):
                if m >= 4:
                    pe.wait_ge(tile_read.sem, tile_read.at(m - 3))
                split_product(pe, bank(m % 4), n_k, rhs, tile_ready, m + 1)
                if beside is not None:
                    beside(pe, m)

        def weight_programs(block, act=True, before=None):
            u0 = wts.lows

            @block.sync
            def _(sp):
                wts.load(sp)

            @block.gpsimd
            def _(pool):
                if before is not None:
                    wts.subtract_low(pool, G, u0 + 1)
                    before.pool(pool)
                wts.subtract_low(pool, G)

            if act:
                @block.scalar
                def _(a):
                    wts.round_high(a, S)

        def of(t):
            return lambda half, k: t[:, half, k, :]

        def nothing(engine):
            pass

        def split_tiles(src, dst):
            def act(a):
                for t in range(KD):
                    S.activation(dst[:, 0, t, :], src(t), ACT.Copy).then_inc(norm_high.sem, 1)

            def dve(d):
                for t in range(KD):
                    d.wait_ge(norm_high.sem, norm_high.at(t + 1))
                    V.tensor_tensor(dst[:, 1, t, :], src(t), dst[:, 0, t, :].bitcast(F32),
                                    ALU.subtract).then_inc(norm_low.sem, 1)

            def ready(pe, t):
                pe.wait_ge(norm_low.sem, norm_low.at(t + 1))

            return Before(pe=nothing, act=act, dve=dve, pool=nothing, ready=ready,
                          counts=((norm_high, KD), (norm_low, KD)))

        def xt(t):
            return x[:, t, :]

        def wt(a):
            return lambda t: w[:, a + t, :]

        SQ_SUM, X_SUM, SQ, NEG_MEAN = 46, 47, 48, 45
        LAST_SQ = SQ + (KD - 1) % 2
        FACTOR, MEAN, SUMS = 7, 6, 5

        def factor_pe(pe, squares, sums=(), dve_n=1):
            for a, tiles in ((0, sums), (4, squares)):
                for i in range(NT):
                    for j, tile in enumerate(tiles):
                        ins = TE.matmul(bank(SUMS, a + i, 1), tile[:, tok(0, i)], one, start=(j == 0),
                                        stop=(j == len(tiles) - 1))
            ins.then_inc(norm_pe.sem, 1)
            pe.wait_ge(norm_dve.sem, norm_dve.at(dve_n))
            for b, at in ((FACTOR, 8), (MEAN, 4)) if sums else ((FACTOR, 8),):
                for i in range(NT):
                    ins = TE.matmul(bank(b, i * P, P), col[:, at + i:at + i + 1].to_broadcast([P, P]), ident,
                                    start=True, stop=True)
            ins.then_inc(norm_pe.sem, 1)

        def factor_act(act, n_pe, eps, centre=False, n_dve=0, mean_of=D):
            if centre:
                act.wait_ge(norm_dve.sem, norm_dve.at(n_dve))
                S.activation(col[:, 8:12], col[:, 4:8], ACT.Sqrt, bias=eps_of[eps]).then_inc(norm_act.sem, 1)
            else:
                act.wait_ge(norm_pe.sem, norm_pe.at(n_pe))
                S.activation(col[:, 8:12], bank(SUMS, 4, 4), ACT.Sqrt, scale=1.0 / mean_of,
                             bias=eps_of[eps]).then_inc(norm_act.sem, 1)

        def factor_dve(dve, n_act, centre=False):
            mean, var, r = col[:, 0:4], col[:, 4:8], col[:, 8:12]
            if centre:
                dve.wait_ge(norm_pe.sem, norm_pe.at(1))
                dve_chain.link(dve, V.tensor_scalar(mean, bank(SUMS, 0, 4), -1.0 / D, None, ALU.mult))
                dve_chain.link(dve, V.tensor_tensor(var, mean, mean, ALU.mult))
                dve_chain.link(dve, V.scalar_tensor_tensor(var, bank(SUMS, 4, 4), 1.0 / D, var, ALU.mult,
                                                           ALU.subtract))
                V.tensor_scalar(var, var, 0.0, None, ALU.max).then_inc(norm_dve.sem, 1)
            dve.wait_ge(norm_act.sem, norm_act.at(n_act))
            ins = V.reciprocal(r, r)
            if centre:
                dve_chain.link(dve, ins)
                ins = V.tensor_tensor(var, mean, r, ALU.mult)
            ins.then_inc(norm_dve.sem, 1)

        def in_pairs(dve, first, second):
            marks = []
            for t in range(KD + 1):
                if t < KD:
                    marks.append(dve_chain.mark(first(t)))
                if t >= 1:
                    dve.wait_ge(dve_chain.sem, marks[t - 1])
                    second(t - 1)

        def subtract_low(eng, src, t, sig):
            eng.tensor_tensor(xs[:, 1, t, :], src, xs[:, 0, t, :].bitcast(F32), ALU.subtract).then_inc(sig.sem, 1)

        def scale_dve(dve, gain, tmp, n_pe):
            def low(t):
                dve.wait_ge(norm_high.sem, norm_high.at(t + 1))
                subtract_low(V, w[:, tmp + t, :], t, norm_low)

            dve.wait_ge(norm_pe.sem, norm_pe.at(n_pe))
            for t in range(KD):
                V.scalar_tensor_tensor(w[:, tmp + t, :], xt(t), v(gain, t), bank(FACTOR), ALU.mult,
                                       ALU.mult).then_inc(norm_dve.sem, 1)
                if t % 2 == 0 and t:
                    low(t - 1)
            low(KD - 1)

        def scale_act(act, tmp, n_dve):
            for t in range(KD):
                act.wait_ge(norm_dve.sem, norm_dve.at(n_dve + t + 1))
                S.activation(xs[:, 0, t, :], w[:, tmp + t, :], ACT.Copy).then_inc(norm_high.sem, 1)

        def scale_pool(pool, tmp):
            for t in range(0, KD, 2):
                pool.wait_ge(norm_high.sem, norm_high.at(t + 1))
                subtract_low(G, w[:, tmp + t, :], t, norm_low2)

        def ready_scaled(pe, t):
            if t:
                pe.wait_ge(norm_low.sem, norm_low.at((t + 1) // 2))
            pe.wait_ge(norm_low2.sem, norm_low2.at(t // 2 + 1))

        def first_norm():
            SQS, SUM, TMP = 30, 38, 40

            def pe(p):
                p.wait_ge(con_landed, 16)
                p.wait_ge(norm_act.sem, norm_act.at(KD))
                p.wait_ge(norm_dve.sem, norm_dve.at(1))
                factor_pe(p, (w[:, SUM, :], w[:, SQS + KD - 1, :]), dve_n=2)

            def act(a):
                for t in range(KD):
                    if t % 2 == 0:
                        a.wait_ge(x_landed[t // 2], 16)
                    S.activation(w[:, SQS + t, :], xt(t), ACT.Square).then_inc(norm_act.sem, 1)
                a.wait_ge(con_landed, 16)
                factor_act(a, 1, RMS_EPS)
                wts.round_high(a, S, 2)
                scale_act(a, TMP, 2)

            def dve(d):
                for t in range(1, KD - 1):
                    d.wait_ge(norm_act.sem, norm_act.at(t + 1))
                    ins = V.tensor_tensor(w[:, SUM, :], w[:, SQS if t == 1 else SUM, :], w[:, SQS + t, :], ALU.add)
                    if t < KD - 2:
                        dve_chain.link(d, ins)
                ins.then_inc(norm_dve.sem, 1)
                factor_dve(d, KD + 1)
                d.wait_ge(vec_landed, 16)
                scale_dve(d, "pre_mix_g", TMP, 2)

            return Before(pe=pe, act=act, dve=dve, pool=lambda p: scale_pool(p, TMP), ready=ready_scaled,
                          counts=((norm_pe, 2), (norm_act, KD + 1), (norm_dve, 2 + KD), (norm_high, KD),
                                  (norm_low, KD // 2), (norm_low2, KD // 2)))

        def add_normed(y0, gain):
            def scaled(t):
                return V.scalar_tensor_tensor(w[:, y0 + t, :], w[:, y0 + t, :], v(gain, t), bank(FACTOR), ALU.mult,
                                              ALU.mult)

            def added(t):
                V.tensor_tensor(xt(t), xt(t), w[:, y0 + t, :], ALU.add).then_inc(norm_dve.sem, 1)
            return scaled, added

        def post_mix_pre_ffn():
            SQS, SUM, TMP = 8, 16, 20
            scaled, added = add_normed(0, "post_mix_g")

            def pe(p):
                factor_pe(p, (w[:, SQ_SUM, :], w[:, LAST_SQ, :]))
                p.wait_ge(norm_act.sem, norm_act.at(1 + KD))
                p.wait_ge(norm_pool.sem, norm_pool.at(1))
                factor_pe(p, (w[:, SUM, :], w[:, SQS + KD - 2, :], w[:, SQS + KD - 1, :]), dve_n=KD + 2)

            def act(a):
                factor_act(a, 1, RMS_EPS)
                for t in range(KD):
                    a.wait_ge(norm_dve.sem, norm_dve.at(t + 2))
                    S.activation(w[:, SQS + t, :], xt(t), ACT.Square).then_inc(norm_act.sem, 1)
                factor_act(a, 3, RMS_EPS)
                scale_act(a, TMP, KD + 2)

            def dve(d):
                factor_dve(d, 1)
                d.wait_ge(norm_pe.sem, norm_pe.at(2))
                in_pairs(d, scaled, added)
                factor_dve(d, KD + 2)
                scale_dve(d, "pre_ffn_g", TMP, 4)

            def pool(p):
                for t in range(1, KD - 2):
                    p.wait_ge(norm_act.sem, norm_act.at(t + 2))
                    ins = G.tensor_tensor(w[:, SUM, :], w[:, SQS if t == 1 else SUM, :], w[:, SQS + t, :], ALU.add)
                    if t < KD - 3:
                        pool_chain.link(p, ins)
                ins.then_inc(norm_pool.sem, 1)
                scale_pool(p, TMP)

            return Before(pe=pe, act=act, dve=dve, pool=pool, ready=ready_scaled,
                          counts=((norm_pe, 4), (norm_act, KD + 2), (norm_dve, 2 * KD + 2), (norm_pool, 1),
                                  (norm_high, KD), (norm_low, KD // 2), (norm_low2, KD // 2)))

        def post_ffn():
            scaled, added = add_normed(36, "post_ffn_g")

            def act(a):
                factor_act(a, 1, RMS_EPS)
                for t in range(KD):
                    a.wait_ge(norm_dve.sem, norm_dve.at(t + 2))
                    S.activation(xs[:, 0, t, :], xt(t), ACT.Copy).then_inc(norm_high.sem, 1)

            def dve(d):
                factor_dve(d, 1)
                d.wait_ge(norm_pe.sem, norm_pe.at(2))
                in_pairs(d, scaled, added)

            def pool(p):
                for t in range(KD):
                    p.wait_ge(norm_high.sem, norm_high.at(t + 1))
                    subtract_low(G, xt(t), t, norm_low)

            return Before(pe=lambda p: factor_pe(p, (w[:, SQ_SUM, :], w[:, LAST_SQ, :])), act=act, dve=dve,
                          pool=pool, ready=lambda p, t: p.wait_ge(norm_low.sem, norm_low.at(t + 1)),
                          counts=((norm_pe, 2), (norm_act, 1), (norm_dve, KD + 1), (norm_high, KD), (norm_low, KD)))

        def layer_norm(name, layer, split=True):
            def pe(p):
                factor_pe(p, (w[:, SQ_SUM, :], w[:, LAST_SQ, :]), sums=(w[:, X_SUM, :], xt(KD - 1)), dve_n=2)

            def act(a):
                factor_act(a, 0, LN_EPS, centre=True, n_dve=1)
                for t in range(KD):
                    g, b = (v(name + part, KD * layer + t) for part in ("_g", "_b"))
                    a.wait_ge(norm_dve.sem, norm_dve.at(t + 3))
                    if split:
                        S.activation(xs[:, 0, t, :], xt(t), ACT.Identity, scale=g, bias=b).then_inc(norm_high.sem, 1)
                    S.activation(xt(t), xt(t), ACT.Identity, scale=g, bias=b).then_inc(norm_act.sem, 1)

            def dve(d):
                factor_dve(d, 1, centre=True)
                d.wait_ge(norm_pe.sem, norm_pe.at(2))
                in_pairs(d, lambda t: V.tensor_tensor(xt(t), xt(t), bank(FACTOR), ALU.mult),
                         lambda t: V.tensor_tensor(xt(t), xt(t), bank(MEAN), ALU.add).then_inc(norm_dve.sem, 1))

            def pool(p):
                for t in range(KD):
                    p.wait_ge(norm_act.sem, norm_act.at(t + 2))
                    p.wait_ge(norm_high.sem, norm_high.at(t + 1))
                    subtract_low(G, xt(t), t, norm_low)

            counts = ((norm_pe, 2), (norm_act, 1 + KD), (norm_dve, 2 + KD))
            return Before(pe=pe, act=act, dve=dve, pool=pool,
                          ready=lambda p, t: p.wait_ge(norm_low.sem, norm_low.at(t + 1)),
                          counts=counts + ((norm_high, KD), (norm_low, KD)) if split else counts)

        def ssm_norm():
            SQS = 28
            dst = odd_split

            def pe(p):
                p.wait_ge(norm_act.sem, norm_act.at(4))
                factor_pe(p, [w[:, SQS + t, :] for t in range(4)])

            def act(a):
                def high(t):
                    S.activation(dst[:, 0, t, :], w[:, YS + t, :], ACT.Copy).then_inc(norm_high.sem, 1)

                for t in range(4):
                    S.activation(w[:, SQS + t, :], w[:, YS + t, :], ACT.Square).then_inc(norm_act.sem, 1)
                high(4)
                high(5)
                factor_act(a, 1, LN_EPS, mean_of=HALF)
                high(6)
                high(7)
                for t in range(4):
                    a.wait_ge(norm_dve.sem, norm_dve.at(t + 2))
                    high(t)

            def dve(d):
                def low(t, n):
                    d.wait_ge(norm_high.sem, norm_high.at(n))
                    V.tensor_tensor(dst[:, 1, t, :], w[:, YS + t, :], dst[:, 0, t, :].bitcast(F32),
                                    ALU.subtract).then_inc(norm_low.sem, 1)

                low(4, 1)
                low(5, 2)
                factor_dve(d, 5)
                d.wait_ge(norm_pe.sem, norm_pe.at(2))
                for t in range(4):
                    V.scalar_tensor_tensor(w[:, YS + t, :], w[:, YS + t, :], v("ssm_norm", t), bank(FACTOR), ALU.mult,
                                           ALU.mult).then_inc(norm_dve.sem, 1)
                low(6, 3)
                low(7, 4)
                for t in range(4):
                    low(t, t + 5)

            def ready(p, t):
                p.wait_ge(norm_low.sem, norm_low.at(t + 5 if t < 4 else t - 3))

            return Before(pe=pe, act=act, dve=dve, pool=nothing, ready=ready, order=(4, 5, 6, 7, 0, 1, 2, 3),
                          counts=((norm_pe, 2), (norm_act, 5), (norm_dve, 5), (norm_high, KD), (norm_low, KD)))

        def to_token_major(jobs, scaled=None):
            n_banks = 4 * len(jobs)
            with nc.Block() as block:
                @block.tensor
                def _(pe):
                    for n in range(n_banks):
                        src = jobs[n // 4][0]
                        if n >= 4:
                            pe.wait_ge(tile_read.sem, tile_read.at(n - 3))
                        for t in range(4):
                            ins = TE.transpose(bank(n % 4, t * P, P), w[:, src + t, tok(0, n % 4)], ident)
                        ins.then_inc(tile_ready.sem, 1)

                @block.vector
                def _(dve):
                    for n in range(n_banks):
                        dst = jobs[n // 4][1] + n % 4
                        dve.wait_ge(tile_ready.sem, tile_ready.at(n + 1))
                        if scaled is None:
                            V.tensor_copy(w[:, dst, :], bank(n % 4)).then_inc(tile_read.sem, 1)
                        else:
                            V.tensor_tensor(w[:, dst, :].rearrange("p (h d) -> p h d", d=HD),
                                            bank(n % 4).rearrange("p (h d) -> p h d", d=HD),
                                            scaled(n % 4).unsqueeze(2).to_broadcast([P, HEADS, HD]),
                                            ALU.mult).then_inc(tile_read.sem, 1)
            tile_ready.close(n_banks)
            tile_read.close(n_banks)

        PARTS = P

        def row_parts(tile, j):
            return w[0:PARTS, tile, 256 * j:256 * (j + 1)].bitcast(BF16)

        def split_rows(dve, rows, n, tile, j, rest, rounded):
            left, part = w[0:n, rest, :], w[0:n, rounded, 0:256].bitcast(BF16)
            src = rows
            for k in range(3):
                dve_chain.link(dve, V.tensor_copy(part, src))
                ins = V.tensor_copy(row_parts(tile, j)[32 * k:32 * k + n], part)
                if k < 2:
                    ins = V.tensor_tensor(left, src, part, ALU.subtract)
                dve_chain.link(dve, ins)
                src = left

        def one_hot(hd, n):
            return one_head[0:PARTS, hd:hd + 1].to_broadcast([PARTS, n])

        def attention(kind, q0, k0, vt0, out0, scratch, parts=None, f_cols=None, bias0=None, gate0=None):
            ml = kind == "mlstm"
            heads = ML_HEADS if ml else HEADS
            dim = HALF // heads
            items = [(hd, i) for i in range(NT) for hd in range(heads)]
            n_items = len(items)
            deep = 2 if ml else 3
            e = [w[:, a, :] for a in scratch[0:deep]]
            pt = [w[:, a, :] for a in scratch[deep:2 * deep]]
            divided = [w[:, a, :] for a in scratch[2 * deep:2 * deep + 2]]
            extra = [w[:, a, :] for a in scratch[2 * deep + 2:2 * deep + 4]]
            heads_a_tile = P // dim
            sums, negs, lows = (col[:, a:a + n_items] for a in (64, 96, 48))
            turn_bank = (lambda n: 2 + n % 2) if ml else (lambda n: 3 + n % 3)
            weighted = dve_out2 if ml else act_out

            def rows(hd):
                return half(hd) if dim == HD else slice(0, P)

            def value_bank(i, a=0, n=T):
                return bank(6 + i % 2, a, n)

            def by_head(ap):
                return ap.rearrange("p (h d) -> p h d", d=dim)

            def each(cols):
                return cols.unsqueeze(2).to_broadcast([P, heads, dim])

            def query_key(n, out, stop):
                hd, i = items[n]
                t, r = hd // heads_a_tile, rows(hd)
                return TE.matmul(out, w[r, q0 + t, i * P:(i + 1) * P], w[r, k0 + t, 0:(i + 1) * P],
                                 start=True, stop=stop)

            with nc.Block() as block:
                @block.tensor
                def _(pe):
                    def scores(n):
                        hd, i = items[n]
                        wd = (i + 1) * P
                        b = n % deep
                        if n >= deep:
                            pe.wait_ge(act_out.sem, act_out.at(n - deep + 1))
                        d = bank(b, 0, wd)
                        if not ml:
                            query_key(n, d, False)
                        if kind == "band":
                            ins = TE.matmul(d, c("flip"), w[:, bias0 + hd, (3 - i) * P:T], start=False, stop=True)
                        else:
                            TE.matmul(d, row_parts(parts, 0)[:, i * P:(i + 1) * P], one_hot(hd, wd),
                                      start=ml, stop=False)
                            TE.matmul(d, one_hot(hd, P), row_parts(parts, 1)[:, 0:wd], start=False, stop=False)
                            ins = TE.matmul(bank(b, i * P, P), ident_h[:, :], diag_qk_h[:, :], start=False,
                                            stop=True)
                        ins.then_inc(tile_ready.sem, 1)

                    def products(n):
                        if n >= 2:
                            pe.wait_ge(dve_out2.sem, dve_out2.at(n - 1))
                        query_key(n, bank(4 + n % 2, 0, (items[n][1] + 1) * P), True).then_inc(pe_out3.sem, 1)

                    def turn(n):
                        hd, i = items[n]
                        pe.wait_ge(weighted.sem, weighted.at(n + 1))
                        if n >= deep:
                            pe.wait_ge(act_out2.sem, act_out2.at(n - deep + 1))
                        for j in range(i + 1):
                            ins = TE.transpose(bank(turn_bank(n), j * P, P), e[n % deep][:, j * P:(j + 1) * P], ident)
                        ins.then_inc(pe_out.sem, 1)

                    def values(n):
                        hd, i = items[n]
                        pe.wait_ge(act_out2.sem, act_out2.at(n + 1))
                        if hd == 0 and i >= 2:
                            pe.wait_ge(side_dve.sem, side_dve.at(i - 1))
                        for j in range(i + 1):
                            ins = TE.matmul(value_bank(i, hd * dim, dim), pt[n % deep][:, j * P:(j + 1) * P],
                                            w[:, vt0 + j, hd * dim:(hd + 1) * dim], start=(j == 0), stop=(j == i))
                        ins.then_inc(pe_out2.sem, 1)

                    def back(i):
                        pe.wait_ge(dve_out3.sem, dve_out3.at(i + 1))
                        for t in range(KH):
                            ins = TE.transpose(value_bank(i, t * P, P), divided[i % 2][:, t * P:(t + 1) * P], ident)
                        ins.then_inc(side_pe.sem, 1)

                    for n in range(deep - 1):
                        scores(n)
                        if ml:
                            products(n)
                    for n in range(n_items):
                        if n + deep - 1 < n_items:
                            scores(n + deep - 1)
                            if ml:
                                products(n + deep - 1)
                        if n >= 1:
                            values(n - 1)
                        done, off = divmod(n, heads)
                        if done and off == 3:
                            back(done - 1)
                        turn(n)
                    values(n_items - 1)
                    back(NT - 1)

                @block.vector
                def _(dve):
                    def peak(n):
                        hd, i = items[n]
                        dve.wait_ge(tile_ready.sem, tile_ready.at(n + 1))
                        mx = col[:, n % 2:n % 2 + 1]
                        dve_chain.link(dve, V.reduce_max(mx, bank(n % deep, 0, (i + 1) * P), AX_X))
                        if ml:
                            dve_chain.link(dve, V.tensor_tensor(mx, mx, f_cols(i, hd), ALU.max))
                        V.tensor_scalar(negs[:, n:n + 1], mx, -1.0, None, ALU.mult).then_inc(dve_out.sem, 1)

                    def weight(n):
                        wd = (items[n][1] + 1) * P
                        a = e[n % deep][:, 0:wd]
                        dve.wait_ge(act_out.sem, act_out.at(n + 1))
                        dve.wait_ge(pe_out3.sem, pe_out3.at(n + 1))
                        V.tensor_tensor_reduce(a, bank(4 + n % 2, 0, wd), a, 1.0, 0.0, ALU.mult, ALU.add,
                                               sums[:, n:n + 1]).then_inc(dve_out2.sem, 1)

                    def divide(i):
                        own = slice(i * heads, (i + 1) * heads)
                        s = sums[:, own]
                        out, vals = by_head(divided[i % 2]), by_head(value_bank(i))
                        if ml:
                            tmp = col[:, 4:4 + heads]
                            dve.wait_ge(dve_out2.sem, dve_out2.at((i + 1) * heads))
                            dve_chain.link(dve, V.tensor_scalar(tmp, s, -1.0, None, ALU.mult))
                            dve_chain.link(dve, V.tensor_tensor(s, s, tmp, ALU.max))
                            dve.wait_ge(side_act.sem, side_act.at(2 * i + 1))
                            dve_chain.link(dve, V.tensor_tensor(s, s, lows[:, own], ALU.max))
                        else:
                            dve.wait_ge(act_out.sem, act_out.at((i + 1) * heads))
                        dve_chain.link(dve, V.reciprocal(s, s))
                        dve.wait_ge(pe_out2.sem, pe_out2.at((i + 1) * heads))
                        if i >= 2:
                            dve.wait_ge(side_pe.sem, side_pe.at(i - 1))
                        if not ml:
                            V.tensor_tensor(out, vals, each(s), ALU.mult).then_inc(dve_out3.sem, 1)
                            return
                        mean, var, r = (col[:, a:a + heads] for a in (4, 8, 12))
                        sq = by_head(extra[0])
                        dve_chain.link(dve, V.tensor_reduce(mean, vals, AX_X, ALU.add))
                        dve_chain.link(dve, V.tensor_scalar(mean, mean, 1.0 / dim, None, ALU.mult))
                        dve_chain.link(dve, V.tensor_tensor(out, vals, each(mean), ALU.subtract))
                        dve_chain.link(dve, V.tensor_tensor(sq, out, each(s), ALU.mult))
                        dve_chain.link(dve, V.tensor_tensor(sq, sq, sq, ALU.mult))
                        V.tensor_reduce(var, sq, AX_X, ALU.add).then_inc(high_out.sem, 1)
                        dve.wait_ge(side_act.sem, side_act.at(2 * i + 2))
                        dve_chain.link(dve, V.reciprocal(r, r))
                        dve_chain.link(dve, V.tensor_tensor(r, r, s, ALU.mult))
                        V.tensor_tensor(out, out, each(r), ALU.mult).then_inc(dve_out3.sem, 1)

                    def store(i):
                        dve.wait_ge(side_pe.sem, side_pe.at(i + 1))
                        own = slice(i * P, (i + 1) * P)
                        if ml:
                            for t in range(KH):
                                ins = V.scalar_tensor_tensor(w[:, out0 + t, own], value_bank(i, t * P, P),
                                                             v("ml_norm", t), w[:, gate0 + t, own], ALU.mult, ALU.mult)
                        else:
                            ins = V.tensor_copy(w[:, out0:out0 + KH, own],
                                                value_bank(i).rearrange("p (a t) -> p a t", a=KH))
                        ins.then_inc(side_dve.sem, 1)

                    for n in range(deep - 1):
                        peak(n)
                    for n in range(n_items):
                        if n + deep - 1 < n_items:
                            peak(n + deep - 1)
                        if ml:
                            weight(n)
                        done, off = divmod(n, heads)
                        if done and off == 1:
                            divide(done - 1)
                        if done and off == 3:
                            store(done - 1)
                    divide(NT - 1)
                    store(NT - 1)

                @block.scalar
                def _(act):
                    def exps(n):
                        wd = (items[n][1] + 1) * P
                        act.wait_ge(dve_out.sem, dve_out.at(n + 1))
                        if n >= deep:
                            act.wait_ge(pe_out.sem, pe_out.at(n - deep + 1))
                        acc = {} if ml else {"accum_out": sums[:, n:n + 1]}
                        S.activation(e[n % deep][:, 0:wd], bank(n % deep, 0, wd), ACT.Exp, bias=negs[:, n:n + 1],
                                     **acc).then_inc(act_out.sem, 1)

                    def copy(n):
                        wd = (items[n][1] + 1) * P
                        act.wait_ge(pe_out.sem, pe_out.at(n + 1))
                        if n >= deep:
                            act.wait_ge(pe_out2.sem, pe_out2.at(n - deep + 1))
                        S.activation(pt[n % deep][:, 0:wd], bank(turn_bank(n), 0, wd), ACT.Copy
                                     ).then_inc(act_out2.sem, 1)

                    def floor(i):
                        own = slice(i * heads, (i + 1) * heads)
                        S.activation(lows[:, own], negs[:, own], ACT.Exp).then_inc(side_act.sem, 1)

                    def root(i):
                        act.wait_ge(high_out.sem, high_out.at(i + 1))
                        S.activation(col[:, 12:12 + heads], col[:, 8:8 + heads], ACT.Sqrt, scale=1.0 / dim,
                                     bias=eps_of[LN_EPS]).then_inc(side_act.sem, 1)

                    exps(0)
                    for n in range(n_items):
                        if n + 1 < n_items:
                            exps(n + 1)
                        copy(n)
                        if ml:
                            done, off = divmod(n, heads)
                            if off == heads - 1:
                                floor(done)
                            if done and off == 1:
                                root(done - 1)
                    if ml:
                        root(NT - 1)
            tile_ready.close(n_items)
            pe_out.close(n_items)
            pe_out2.close(n_items)
            dve_out.close(n_items)
            dve_out3.close(NT)
            act_out.close(n_items)
            act_out2.close(n_items)
            side_pe.close(NT)
            side_dve.close(NT)
            if ml:
                pe_out3.close(n_items)
                dve_out2.close(n_items)
                high_out.close(NT)
                side_act.close(2 * NT)

        def stage_inputs():
            with nc.Block() as block:
                @block.sync
                def _(sp):
                    for i in range(4):
                        sp.dma_start(x[:, 2 * i:2 * i + 2, :], x_t[2 * i * P:(2 * i + 2) * P].rearrange(
                            "(k p) t -> p k t", p=P)).then_inc(x_landed[i], 16)
                    sp.dma_start(con[:, :], constants).then_inc(con_landed, 16)
                    wts.load(sp, 1)
                    sp.dma_start(vec[:, :], vectors).then_inc(vec_landed, 16)
                    wts.load(sp, RING)
                    sp.dma_start(w[0:HEADS, 0, 0:BAND_BIAS], rel_rev).then_inc(bias_landed, 16)

                @block.vector
                def _(dve):
                    V.memset(ones[:, :], 1.0)
                    V.memset(one_head[:, :], 0.0)
                    V.memset(w[0:HEADS, 1:3, :], 0.0)

        YB, YA = 0, 4
        Q1 = 8

        def stage_qkv():
            line = w[0:HEADS, 1:3, :].rearrange("p a t -> p (a t)")
            before = first_norm()
            with nc.Block() as block:
                @block.tensor
                def _(pe):
                    product(pe, 12, KD, of(xs), before)

                @block.sync
                def _(sp):
                    sp.wait_ge(dve_out.sem, dve_out.at(1))
                    sp.dma_start(bias_line, line[:, 0:DIAG_PAD]).then_inc(dma_out.sem, 16)
                    sp.wait_ge(dma_out.sem, dma_out.at(16))
                    diagonals = bass.AP(bias_line.tensor, bias_line.offset + 1, [[1, P], [DIAG_PAD, HEADS], [1, T]])
                    sp.dma_start(w[:, 20:28, :], diagonals).then_inc(dma_out.sem, 16)
                    wts.load(sp)

                @block.gpsimd
                def _(pool):
                    wts.subtract_low(pool, G, 2)
                    before.pool(pool)
                    wts.subtract_low(pool, G)

                @block.scalar
                def _(act):
                    before.act(act)
                    for m in range(12):
                        wts.round_high(act, S, m + SPLIT)
                        act.wait_ge(tile_ready.sem, tile_ready.at(m + 1))
                        S.activation(w[:, Q1 + m, :], bank(m % 4), ACT.Copy,
                                     scale=HD ** -0.5 if m < 4 else 1.0).then_inc(tile_read.sem, 1)

                @block.vector
                def _(dve):
                    before.dve(dve)
                    dve.wait_ge(bias_landed, 16)
                    V.tensor_copy(line[:, REL_CLIP:REL_CLIP + BAND_BIAS], w[0:HEADS, 0, 0:BAND_BIAS])
                    V.tensor_copy(line[:, 0:REL_CLIP],
                                  w[0:HEADS, 0, 0:1].to_broadcast([HEADS, REL_CLIP])).then_inc(dve_out.sem, 1)
                    dve.wait_ge(con_landed, 16)
                    V.tensor_copy(ident_h[:, :], ident)
                    V.tensor_copy(diag_qk_h[:, :], c("diag_qk"))
                    V.tensor_copy(diag_st_h[:, :], c("diag_st"))
                    for k in range(3):
                        r = slice(32 * k, 32 * k + HEADS)
                        at = con_cols["ident"][0] + 32 * k
                        V.tensor_copy(one_head[r, :], con[r, at:at + HEADS])
                    dve.wait_ge(dma_out.sem, dma_out.at(32))
                    V.memset(w[HD:P, 20:28, T - HD:T], NEG)
            tile_ready.close(12)
            tile_read.close(12)
            dve_out.close(1)
            dma_out.close(32)
            before.close()

        R, K, VV, CW, CG = 0, 8, 12, 16, 17
        LW, CM, AA, KK, GG, EE, AT, BO = 18, 22, 26, 30, 34, 38, 42, 46

        def stage_rwkv_in():
            raw = w[:, EE:EE + 3, :].rearrange("p a t -> p (a t)")
            pads = [raw[:, 0:T + 1], raw[:, T + 8:2 * T + 9]]
            u0 = wts.block // UNIT
            norms = col[:, 64:96]
            by_head = c("same_head")[:, 0::HD]
            PE_LOW, PE_SPREAD = 12, 13
            ACT_ROOTS, ACT_EXP = 14, 14
            DVE_SQ, DVE_RN, DVE_KK = 0, 8, 13
            DVE_SHIFTED = (5, 6, 7, 9)

            def beside_pe(pe, n):
                t = n - 3
                if 0 <= t < 4:
                    pe.wait_ge(side_dve.sem, side_dve.at(DVE_SQ + t + 1))
                    for i in range(NT):
                        TE.matmul(bank(7, 8 * t + 2 * i, 2), w[:, AT + t, tok(0, i)], by_head, start=True, stop=True)
                    pe.wait_ge(side_act.sem, side_act.at(1 + 3 * t))
                    for b, lhs, rhs in ((4, v("w2a2", t * P, P)[0:HD], w[0:HD, CW, :]),
                                        (5, v("w2a2", t * P, P)[HD:P], w[HD:P, CW, :]),
                                        (6, v("g2", t * P, P), w[:, CG, :])):
                        TE.matmul(bank(b), lhs, rhs, start=True, stop=True).then_inc(side_pe.sem, 1)
                elif n == 9:
                    pe.wait_ge(side_dve.sem, side_dve.at(DVE_RN))
                    for t in range(4):
                        for i in range(NT):
                            for h in range(2):
                                at = 8 * t + 2 * i + h
                                ins = TE.matmul(bank(4 + t, i * P, P, half(h)),
                                                norms[:, at:at + 1].to_broadcast([P, HD]), ident, start=True,
                                                stop=True)
                    ins.then_inc(side_pe.sem, 1)
                elif n == 12:
                    pe.wait_ge(side_dve.sem, side_dve.at(DVE_KK + 4))
                    for t in range(4):
                        ins = TE.matmul(bank(4 + t), c("same_head"), w[:, BO + t, :], start=True, stop=True)
                    ins.then_inc(side_pe.sem, 1)

            def beside_act(act, n):
                t = n - 4
                if n == 3:
                    act.wait_ge(dve_out.sem, dve_out.at(2))
                    act_chain.link(act, S.activation(w[0:HD, CW, :], w[0:HD, CW, :], ACT.Tanh))
                    S.activation(w[:, CG, :], w[:, CG, :], ACT.Sigmoid).then_inc(side_act.sem, 1)
                elif 0 <= t < 4:
                    for j, (out, f, bias) in enumerate(((LW, ACT.Sigmoid, v("w0", t)), (AA, ACT.Sigmoid, v("a0", t)),
                                                        (GG, ACT.Copy, 0.0))):
                        act.wait_ge(side_pe.sem, side_pe.at(3 * t + j + 1))
                        S.activation(w[:, out + t, :], bank(4 + j), f, bias=bias).then_inc(side_act.sem, 1)
                if n == 8:
                    act.wait_ge(side_pe.sem, side_pe.at(PE_LOW))
                    S.activation(norms, bank(7, 0, 32), ACT.Sqrt).then_inc(side_act.sem, 1)
                if 8 <= n < 12:
                    t = n - 8
                    at, lw, cm = w[:, AT + t, :], w[:, LW + t, :], w[:, CM + t, :]
                    act.wait_ge(side_dve.sem, side_dve.at(DVE_SHIFTED[t]))
                    S.activation(at, at, ACT.Exp).then_inc(side_act.sem, 1)
                    S.activation(lw, cm, ACT.Exp, scale=-1.0)
                    act_chain.link(act, S.activation(cm, cm, ACT.Exp))
                    S.activation(col[:, 32 + 4 * t:36 + 4 * t], cm[:, P - 1::P], ACT.Copy).then_inc(side_act.sem, 1)
                elif n == 12:
                    S.activation(col[:, 16:32], col[:, 16:32], ACT.Exp)

            def keys(dve, t):
                kk, sq = w[:, KK + t, :], w[:, AT + t, :]
                dve_chain.link(dve, V.tensor_scalar(kk, w[:, K + t, :], v("k_k", t), None, ALU.mult))
                V.tensor_tensor(sq, kk, kk, ALU.mult).then_inc(side_dve.sem, 1)

            def rates(dve, t):
                tmp, kt = w[:, BO + t, :], w[:, K + t, :]
                dve.wait_ge(side_act.sem, side_act.at(3 * t + 3))
                dve.wait_ge(side_dve.sem, side_dve.at(DVE_SQ + t + 1))
                dve_chain.link(dve, V.tensor_scalar(tmp, w[:, AA + t, :], -1.0, v("k_a", t), ALU.add, ALU.mult))
                dve_chain.link(dve, V.scalar_tensor_tensor(kt, tmp, 1.0, kt, ALU.add, ALU.mult))

            def decays(dve, t):
                lw, cm = w[:, LW + t, :], w[:, CM + t, :]
                middles = col[:, 0:NT]
                dve_chain.link(dve, V.tensor_scalar(lw, lw, -float(np.exp(-0.5)), None, ALU.mult))
                for ch in range(NT):
                    s = slice(ch * P, (ch + 1) * P)
                    ins = V.tensor_tensor_scan(cm[:, s], ones[:, 0:P], lw[:, s], 0.0, ALU.mult, ALU.add)
                dve_chain.link(dve, ins)
                dve_chain.link(dve, V.tensor_copy(middles, cm[:, HD - 1::P]))
                chunks = cm.rearrange("p (a t) -> p a t", a=NT)
                dve_chain.link(dve, V.tensor_tensor(chunks, chunks, middles.unsqueeze(2).to_broadcast([P, NT, P]),
                                                    ALU.subtract))

            def shifted(dve, t):
                at = w[:, AT + t, :]
                dve_chain.link(dve, V.tensor_tensor(at, w[:, CM + t, :], w[:, LW + t, :], ALU.subtract))
                V.tensor_scalar(col[:, 16 + 4 * t:20 + 4 * t], at[:, 0::P], -1.0, None,
                                ALU.mult).then_inc(side_dve.sem, 1)

            def decayed(dve, t):
                kk, at, e, kt, r = (w[:, a + t, :] for a in (KK, AT, LW, K, R))
                dve.wait_ge(side_act.sem, side_act.at(ACT_EXP + 2 * t + 2))
                dve_chain.link(dve, V.scalar_tensor_tensor(at, kk, -1.0, at, ALU.mult, ALU.mult))
                last = dve_chain.mark(V.tensor_tensor(kk, kk, w[:, AA + t, :], ALU.mult))
                V.tensor_tensor(kt, kt, e, ALU.mult)
                V.tensor_tensor(r, r, w[:, CM + t, :], ALU.mult)
                dve.wait_ge(dve_chain.sem, last)
                V.tensor_tensor(kk, kk, e, ALU.mult)

            def beside_dve(dve, n):
                if 2 <= n < 6:
                    keys(dve, n - 2)
                if 4 <= n < 8:
                    rates(dve, n - 4)
                if 6 <= n < 10:
                    decays(dve, n - 6)
                    shifted(dve, n - 6)
                if n == 8:
                    dve.wait_ge(side_act.sem, side_act.at(ACT_ROOTS))
                    dve_chain.link(dve, V.tensor_scalar(norms, norms, 1e-12, None, ALU.max))
                    V.reciprocal(norms, norms).then_inc(side_dve.sem, 1)
                elif n == 10:
                    for t in range(4):
                        V.scalar_tensor_tensor(w[:, BO + t, :], w[:, R + t, :], v("r_k", t), w[:, K + t, :], ALU.mult,
                                               ALU.mult).then_inc(side_dve.sem, 1)
                    dve.wait_ge(side_pe.sem, side_pe.at(PE_SPREAD))
                    for t in range(4):
                        kk = w[:, KK + t, :]
                        V.tensor_tensor(kk, kk, bank(4 + t), ALU.mult).then_inc(side_dve.sem, 1)
                    dve.wait_ge(side_dve.sem, side_dve.at(DVE_KK + 4))
                elif n == 11:
                    decayed(dve, 0)
                    decayed(dve, 1)
                elif n in (12, 13):
                    decayed(dve, n - 10)
                if n == 13:
                    dve.wait_ge(side_pe.sem, side_pe.at(PE_SPREAD + 1))
                    for t in range(4):
                        V.tensor_tensor(w[:, BO + t, :], bank(4 + t), w[:, VV + t, :], ALU.mult)

            with nc.Block() as block:
                @block.tensor
                def _(pe):
                    product(pe, 14, KD, of(xs), beside=beside_pe)

                weight_programs(block, act=False)

                @block.scalar
                def _(act):
                    act.wait_ge(dve_out2.sem, dve_out2.at(1))
                    for n in range(14):
                        wts.round_high(act, S, u0 + n + SPLIT)
                        beside_act(act, n)
                        act.wait_ge(tile_ready.sem, tile_ready.at(n + 1))
                        if n >= 2:
                            act.wait_ge(dve_out.sem, dve_out.at(n - 1))
                        S.activation(pads[n % 2][:, 1:T + 1], bank(n % 4), ACT.Copy).then_inc(tile_read.sem, 1)

                @block.vector
                def _(dve):
                    V.memset(pads[0][:, 0:1], 0.0)
                    V.memset(pads[1][:, 0:1], 0.0).then_inc(dve_out2.sem, 1)
                    dve.wait_ge(dve_out2.sem, dve_out2.at(1))
                    for n, m in enumerate(RWKV_ORDER):
                        p = pads[n % 2]
                        mixed = w[:, m if m < 4 else m + 4, :]
                        dve.wait_ge(tile_read.sem, tile_read.at(n + 1))
                        dve_chain.link(dve, V.tensor_tensor(mixed, p[:, 0:T], p[:, 1:T + 1], ALU.subtract))
                        V.scalar_tensor_tensor(mixed, mixed, v("shift_mu", m), p[:, 1:T + 1], ALU.mult,
                                               ALU.add).then_inc(dve_out.sem, 1)
                        dve.wait_ge(dve_out.sem, dve_out.at(n + 1))
                        beside_dve(dve, n)
            tile_ready.close(14)
            tile_read.close(14)
            dve_out.close(14)
            dve_out2.close(1)
            side_pe.close(PE_SPREAD + 1)
            side_act.close(ACT_EXP + 8)
            side_dve.close(DVE_KK + 4)

        N4, UU, TT, XX, BK = (LW, CM), (38, 41), (39, 29), (40, 17), (26, 27)
        VTOK = 28
        ZS = CW

        def stage_rwkv_chunks():
            z = w[:, ZS, :]
            pe_s = (pe_out, pe_out2)
            dve_s = (dve_out, dve_out2)
            act_s = (act_out, act_out2)
            PE_TOK, PE_PAIR, PE_TURN, PE_G, PE_SA, PE_YZ = 1, 2, 6, 19, 20, 21
            DVE_U, DVE_Z = 1, 14
            ACT_TOK, ACT_T, ACT_G, ACT_SA, ACT_Y = 1, 2, 3, 4, 5

            def pe_x(l):
                return 5 + 2 * l

            def pe_u(l):
                return 6 + 2 * l

            def wait(eng, sig, g, ch, n, per):
                eng.wait_ge(sig[g].sem, sig[g].at(ch * per + n))

            def wait_pe(eng, g, ch, n):
                wait(eng, pe_s, g, ch, n, PE_YZ)

            def wait_dve(eng, g, ch, n):
                wait(eng, dve_s, g, ch, n, DVE_Z)

            def wait_act(eng, g, ch, n):
                wait(eng, act_s, g, ch, n, ACT_Y)

            def n4(g, i, j):
                return w[:, N4[g] + i, j * P:(j + 1) * P]

            def part(tile, i):
                return w[:, tile, i * P:(i + 1) * P]

            def quad(ap):
                return ap.rearrange("p (a t) -> p a t", a=4)

            def wide(m):
                return m.unsqueeze(1).to_broadcast([P, 4, P])

            def cols(ch):
                return slice(ch * P, (ch + 1) * P)

            def state(g):
                return z[:, 2 * g * HD:2 * (g + 1) * HD].rearrange("p (a d) -> p a d", d=HD)

            with nc.Block() as block:
                @block.vector
                def _(dve):
                    V.memset(w[:, N4[0]:N4[0] + 4, :], 0.0)
                    V.memset(w[:, N4[1]:N4[1] + 4, :], 0.0)
                    dve_chain.link(dve, V.memset(z, 0.0))

            with nc.Block() as block:
                @block.tensor
                def _(pe):
                    def token_major(g, ch):
                        if ch:
                            wait_act(pe, g, ch - 1, ACT_Y)
                        for j, src in enumerate((KK, K, VV)):
                            for a in range(2):
                                ins = TE.transpose(bank(4 * g + 2 + j // 2, (j % 2) * 256 + a * P, P),
                                                   w[:, src + 2 * g + a, cols(ch)], ident)
                        ins.then_inc(pe_s[g].sem, 1)

                    def pairs(g, ch):
                        if ch:
                            wait_dve(pe, g, ch - 1, DVE_Z)
                        for i in range(4):
                            if i == 2:
                                wait_act(pe, g, ch, ACT_TOK)
                            t, r = 2 * g + i // 2, half(i)
                            a, rr = w[r, AT + t, cols(ch)], w[r, R + t, cols(ch)]
                            bt, kt = w[r, KK + t, cols(ch)], w[r, K + t, cols(ch)]
                            for j, (lhs, rhs) in enumerate(((bt, a), (bt, rr), (kt, a), (kt, rr))):
                                ins = TE.matmul(bank(4 * g + i, j * P, P), lhs, rhs, start=True, stop=True)
                            ins.then_inc(pe_s[g].sem, 1)

                    def turn(g, ch):
                        wait_dve(pe, g, ch, DVE_U)
                        for i in range(4):
                            ins = TE.transpose(bank(4 * g, i * P, P), part(UU[g], i), ident)
                        ins.then_inc(pe_s[g].sem, 1)

                    def level_x(l):
                        def step(g, ch):
                            if l == 1:
                                wait_act(pe, g, ch, ACT_T)
                            else:
                                wait_dve(pe, g, ch, 2 * l - 1)
                            for i in range(4):
                                ins = TE.matmul(bank(4 * g + 1, i * P, P), n4(g, i, 0), part(TT[g], i), start=True,
                                                stop=True)
                            ins.then_inc(pe_s[g].sem, 1)
                        return step

                    def level_u(l):
                        def step(g, ch):
                            wait_dve(pe, g, ch, 2 * l)
                            if l < LEVELS - 1:
                                for i in range(4):
                                    TE.matmul(bank(4 * g, i * P, P), part(UU[g], i), part(XX[g], i), start=True,
                                              stop=True)
                            for i in range(4):
                                ins = TE.matmul(bank(4 * g + 2, i * P, P), part(XX[g], i), part(UU[g], i), start=True,
                                                stop=True)
                            ins.then_inc(pe_s[g].sem, 1)
                        return step

                    def values_of(g, i):
                        return w[:, VTOK, g * 256 + i * HD:g * 256 + (i + 1) * HD]

                    def right_side(g, ch):
                        wait_dve(pe, g, ch, 2 * LEVELS - 1)
                        for i in range(4):
                            t, r = 2 * g + i // 2, half(i)
                            out = bank(4 * g + (3, 1)[i % 2], (i // 2) * HD, HD)
                            TE.matmul(out, w[r, AT + t, cols(ch)], z[r, t * HD:(t + 1) * HD], start=True, stop=False)
                            ins = TE.matmul(out, n4(g, i, 2), values_of(g, i), start=False, stop=True)
                        ins.then_inc(pe_s[g].sem, 1)

                    def solve(g, ch):
                        wait_act(pe, g, ch, ACT_G)
                        for i in range(4):
                            ins = TE.matmul(bank(4 * g, i * HD, HD), part(UU[g], i), w[:, XX[g], i * HD:(i + 1) * HD],
                                            start=True, stop=True)
                        ins.then_inc(pe_s[g].sem, 1)

                    def output(g, ch):
                        wait_act(pe, g, ch, ACT_SA)
                        for i in range(4):
                            t, r = 2 * g + i // 2, half(i)
                            sa = w[:, XX[g], 256 + i * HD:256 + (i + 1) * HD]
                            y = bank(4 * g + 2, (i // 2) * P, P, r)
                            TE.matmul(y, z[r, t * HD:(t + 1) * HD], w[r, R + t, cols(ch)], start=True, stop=False)
                            TE.matmul(y, sa, n4(g, i, 1), start=False, stop=False)
                            TE.matmul(y, values_of(g, i), n4(g, i, 3), start=False, stop=True)
                            zz = bank(4 * g + 1, (i // 2) * HD, HD, r)
                            TE.matmul(zz, w[:, BK[g], i * HD:(i + 1) * HD], sa, start=True, stop=False)
                            ins = TE.matmul(zz, w[:, BK[g], 256 + i * HD:256 + (i + 1) * HD], values_of(g, i),
                                            start=False, stop=True)
                        ins.then_inc(pe_s[g].sem, 1)

                    steps = [token_major, pairs, turn]
                    for l in range(1, LEVELS):
                        steps += [level_x(l), level_u(l)]
                    for ch in range(NT):
                        for step in steps + [right_side, solve, output]:
                            for g in range(2):
                                step(g, ch)

                @block.vector
                def _(dve):
                    def first(g, ch):
                        for i in range(4):
                            wait_pe(dve, g, ch, PE_PAIR + i)
                            ins = V.copy_predicated(w[:, N4[g] + i, :], c("mask4").bitcast(I32), bank(4 * g + i))
                        dve_chain.link(dve, ins)
                        uu, zt = quad(w[:, UU[g], :]), state(g)
                        dve_chain.link(dve, V.tensor_tensor(uu, w[:, N4[g]:N4[g] + 4, 0:P], wide(c("level0_t")),
                                                            ALU.mult))
                        at = 16 + 8 * g + ch
                        before = col[:, at:at + 5:4].unsqueeze(2).to_broadcast([P, 2, HD])
                        dve_chain.link(dve, V.tensor_tensor(zt, zt, before, ALU.mult))
                        V.tensor_tensor(uu, uu, wide(ident), ALU.add).then_inc(dve_s[g].sem, 1)

                    def mask_x(l):
                        def step(g, ch):
                            wait_pe(dve, g, ch, pe_x(l))
                            V.tensor_tensor(quad(w[:, XX[g], :]), quad(bank(4 * g + 1)), wide(c("levels", l * P, P)),
                                            ALU.mult).then_inc(dve_s[g].sem, 1)
                        return step

                    def add_u(l):
                        def step(g, ch):
                            wait_pe(dve, g, ch, pe_u(l))
                            if l < LEVELS - 1:
                                V.tensor_tensor(w[:, TT[g], :], w[:, TT[g], :], bank(4 * g), ALU.add)
                            V.tensor_tensor(w[:, UU[g], :], w[:, UU[g], :], bank(4 * g + 2),
                                            ALU.add).then_inc(dve_s[g].sem, 1)
                        return step

                    def next_state(g, ch):
                        zt = state(g)
                        at = 32 + 8 * g + ch
                        after = col[:, at:at + 5:4].unsqueeze(2).to_broadcast([P, 2, HD])
                        wait_pe(dve, g, ch, PE_YZ)
                        dve_chain.link(dve, V.tensor_tensor(
                            zt, zt, bank(4 * g + 1, 0, P).rearrange("p (a d) -> p a d", d=HD), ALU.add))
                        V.tensor_tensor(zt, zt, after, ALU.mult).then_inc(dve_s[g].sem, 1)
                        wait_dve(dve, g, ch, DVE_Z)

                    steps = [first]
                    for l in range(1, LEVELS):
                        steps += [mask_x(l), add_u(l)]
                    for ch in range(NT):
                        for step in steps + [next_state]:
                            for g in range(2):
                                step(g, ch)

                @block.scalar
                def _(act):
                    def token_major(g, ch):
                        wait_pe(act, g, ch, PE_TOK)
                        S.activation(w[:, BK[g], :], bank(4 * g + 2), ACT.Copy)
                        S.activation(w[:, VTOK, g * 256:(g + 1) * 256], bank(4 * g + 3, 0, 256),
                                     ACT.Copy).then_inc(act_s[g].sem, 1)

                    def inverse(g, ch):
                        wait_pe(act, g, ch, PE_TURN)
                        S.activation(w[:, TT[g], :], bank(4 * g), ACT.Copy).then_inc(act_s[g].sem, 1)

                    def right_side(g, ch):
                        wait_pe(act, g, ch, PE_G)
                        out = w[:, XX[g], 0:256].rearrange("p (a b d) -> p a b d", a=2, b=2)
                        for b in range(2):
                            ins = S.activation(out[:, :, b, :], bank(4 * g + (3, 1)[b], 0, P).rearrange(
                                "p (a d) -> p a d", d=HD), ACT.Copy)
                        ins.then_inc(act_s[g].sem, 1)

                    def taken_up(g, ch):
                        wait_pe(act, g, ch, PE_SA)
                        S.activation(w[:, XX[g], 256:512], bank(4 * g, 0, 256), ACT.Copy).then_inc(act_s[g].sem, 1)

                    def output(g, ch):
                        wait_pe(act, g, ch, PE_YZ)
                        S.activation(w[:, YB + 2 * g:YB + 2 * g + 2, cols(ch)],
                                     bank(4 * g + 2, 0, 256).rearrange("p (a t) -> p a t", a=2),
                                     ACT.Copy).then_inc(act_s[g].sem, 1)

                    for ch in range(NT):
                        for step in (token_major, inverse, right_side, taken_up, output):
                            for g in range(2):
                                step(g, ch)
            for g in range(2):
                pe_s[g].close(PE_YZ * NT)
                dve_s[g].close(DVE_Z * NT)
                act_s[g].close(ACT_Y * NT)

        def stage_merge():
            GA, MG = 24, 28
            SQS = 38
            norms = col[:, 64:96]
            by_head = c("same_head")[:, 0::HD]
            order = [(kind, m, j) for kind, m in merge_order() for j in range(2)]
            number = {p: n + 1 for n, p in enumerate(order)}
            unit_of, n = {}, 0
            for kind, m, j in order:
                unit_of[kind, m, j] = n
                n += 1 if kind == "gate" or j == 1 else 0

            def bank_of(kind, m, j):
                return bank((0 if kind == "gate" else 4) + 2 * (m % 2) + j)

            def part(a):
                return lambda half, k: mix_split[:, half, a + k, :]

            def norm_mean(pe):
                for t in range(4):
                    TE.matmul(bank(4 + t), c("same_head"), w[:, YB + t, :], start=True, stop=True
                              ).then_inc(norm_pe.sem, 1)

            def norm_sums(pe):
                for t in range(4):
                    pe.wait_ge(norm_act.sem, norm_act.at(t + 1))
                    for i in range(NT):
                        ins = TE.matmul(bank(4, 8 * t + 2 * i, 2), w[:, SQS + t, tok(0, i)], by_head, start=True,
                                        stop=True)
                ins.then_inc(norm_pe.sem, 1)

            def norm_spread(pe):
                pe.wait_ge(norm_dve.sem, norm_dve.at(5))
                for t in range(4):
                    for i in range(NT):
                        for h in range(2):
                            at = 8 * t + 2 * i + h
                            ins = TE.matmul(bank(4 + t, i * P, P, half(h)), norms[:, at:at + 1].to_broadcast([P, HD]),
                                            ident, start=True, stop=True)
                    ins.then_inc(norm_pe.sem, 1)

            def norm_wait(pe):
                pe.wait_ge(norm_low.sem, norm_low.at(KD))

            between = {1: norm_sums, 2: norm_spread, 4: norm_wait}
            u0 = wts.block // UNIT
            with nc.Block() as block:
                @block.tensor
                def _(pe):
                    norm_mean(pe)
                    for n, (kind, m, j) in enumerate(order):
                        if n in between:
                            between[n](pe)
                        if m >= 2 and kind == "gate":
                            pe.wait_ge(tile_read.sem, tile_read.at(2 * (m - 2) + j + 1))
                        elif m >= 2:
                            pe.wait_ge(dve_out.sem, dve_out.at(2 * (m - 2) + j + 1))
                        src = (KD, of(xs)) if kind == "gate" else (KH, part((4, 0)[j]))
                        split_product(pe, bank_of(kind, m, j), *src, tile_ready, n + 1)

                weight_programs(block, act=False)

                @block.scalar
                def _(act):
                    def high_in(t):
                        S.activation(mix_split[:, 0, t, :], w[:, t, :], ACT.Copy).then_inc(norm_high.sem, 1)

                    wts.round_high(act, S, u0 + SPLIT)
                    for t in range(4):
                        high_in(YA + t)
                    for t in range(4):
                        act.wait_ge(norm_dve.sem, norm_dve.at(t + 1))
                        S.activation(w[:, SQS + t, :], w[:, YB + t, :], ACT.Square).then_inc(norm_act.sem, 1)
                    wts.round_high(act, S, u0 + 1 + SPLIT)
                    act.wait_ge(norm_pe.sem, norm_pe.at(5))
                    S.activation(norms, bank(4, 0, 32), ACT.Sqrt, scale=1.0 / HD,
                                 bias=eps_of[GN_EPS]).then_inc(norm_act.sem, 1)
                    wts.round_high(act, S, u0 + 2 + SPLIT)
                    for t in range(4):
                        act.wait_ge(norm_dve.sem, norm_dve.at(6 + t))
                        high_in(YB + t)
                    for kind, m in merge_order():
                        if kind == "gate":
                            for j in range(2):
                                wts.round_high(act, S, u0 + unit_of[kind, m, j] + SPLIT)
                                act.wait_ge(tile_ready.sem, tile_ready.at(number[kind, m, j]))
                                if m >= 2:
                                    act.wait_ge(dve_out.sem, dve_out.at(2 * (m - 2) + 2))
                                S.activation(w[:, GA + 2 * (m % 2) + j, :], bank_of(kind, m, j),
                                             ACT.Sigmoid, bias=v("gate_bias", 8 * j + m)).then_inc(tile_read.sem, 1)
                        else:
                            wts.round_high(act, S, u0 + unit_of[kind, m, 0] + SPLIT)
                            act.wait_ge(dve_out.sem, dve_out.at(2 * m + 2))
                            S.activation(merged_split[:, 0, m, :], w[:, MG + m % 2, :], ACT.Copy
                                         ).then_inc(high_out.sem, 1)
                    wts.round_high(act, S)

                @block.vector
                def _(dve):
                    def low_in(t, n):
                        dve.wait_ge(norm_high.sem, norm_high.at(n))
                        V.tensor_tensor(mix_split[:, 1, t, :], w[:, t, :], mix_split[:, 0, t, :].bitcast(F32),
                                        ALU.subtract).then_inc(norm_low.sem, 1)

                    y = [w[:, YB + t, :] for t in range(4)]
                    for t in range(4):
                        dve.wait_ge(norm_pe.sem, norm_pe.at(t + 1))
                        V.scalar_tensor_tensor(y[t], bank(4 + t), -1.0 / HD, y[t], ALU.mult,
                                               ALU.add).then_inc(norm_dve.sem, 1)
                    for t in range(4):
                        low_in(YA + t, t + 1)
                    dve.wait_ge(norm_act.sem, norm_act.at(5))
                    V.reciprocal(norms, norms).then_inc(norm_dve.sem, 1)
                    normed, bonus = [], []
                    for t in range(4):
                        dve.wait_ge(norm_pe.sem, norm_pe.at(6 + t))
                        normed.append(dve_chain.mark(V.scalar_tensor_tensor(y[t], y[t], v("ln_x_w", t), bank(4 + t),
                                                                            ALU.mult, ALU.mult)))
                    for t in range(4):
                        dve.wait_ge(dve_chain.sem, normed[t])
                        bonus.append(dve_chain.mark(V.scalar_tensor_tensor(y[t], y[t], v("ln_x_b", t), w[:, BO + t, :],
                                                                           ALU.add, ALU.add)))
                    for t in range(4):
                        dve.wait_ge(dve_chain.sem, bonus[t])
                        V.tensor_tensor(y[t], y[t], w[:, GG + t, :], ALU.mult).then_inc(norm_dve.sem, 1)
                    for t in range(4):
                        low_in(YB + t, 5 + t)
                    for m in range(KD):
                        ga, gb = w[:, GA + 2 * (m % 2), :], w[:, GA + 2 * (m % 2) + 1, :]
                        mg = w[:, MG + m % 2, :]
                        dve.wait_ge(tile_ready.sem, tile_ready.at(number["projection", m, 0]))
                        dve.wait_ge(tile_read.sem, tile_read.at(2 * m + 1))
                        V.tensor_tensor(mg, bank_of("projection", m, 0), ga, ALU.mult).then_inc(dve_out.sem, 1)
                        dve.wait_ge(tile_ready.sem, tile_ready.at(number["projection", m, 1]))
                        dve.wait_ge(tile_read.sem, tile_read.at(2 * m + 2))
                        dve_chain.link(dve, V.tensor_tensor(gb, bank_of("projection", m, 1), gb, ALU.mult))
                        dve.wait_ge(dve_out.sem, dve_out.at(2 * m + 1))
                        V.tensor_tensor(mg, mg, gb, ALU.add).then_inc(dve_out.sem, 1)
                        dve.wait_ge(high_out.sem, high_out.at(m + 1))
                        dve_chain.link(dve, V.tensor_tensor(merged_split[:, 1, m, :], mg,
                                                            merged_split[:, 0, m, :].bitcast(F32), ALU.subtract))
            norm_pe.close(9)
            norm_act.close(5)
            norm_dve.close(9)
            norm_high.close(KD)
            norm_low.close(KD)
            tile_ready.close(4 * KD)
            tile_read.close(2 * KD)
            dve_out.close(2 * KD)
            high_out.close(KD)

        def stage_linear(n_k, src, mode, out=None, sums=None, before=None):
            centre = sums == "both"
            out = xt if mode == "residual" else out
            block0, u0 = wts.block, wts.highs
            shift = 1 if centre else 0

            pe0, act0, dve0 = (0 if before is None else before.count(sig) for sig in (norm_pe, norm_act, norm_dve))

            def squares_added(k):
                return norm_dve.at(dve0 + max(k, 1) + shift)

            with nc.Block() as block:
                @block.tensor
                def _(pe):
                    def first_mean(p):
                        p.wait_ge(tile_read.sem, tile_read.at(1))
                        TE.matmul(bank(FACTOR), w[:, NEG_MEAN, 0:P], xt(0), start=True,
                                  stop=True).then_inc(norm_pe.sem, 1)

                    if before is not None:
                        before.pe(pe)
                        first_products(pe, src, before)
                    for m in range(0 if before is None else 2, KD):
                        if m == 2 and centre:
                            first_mean(pe)
                        if m >= 4:
                            pe.wait_ge(tile_read.sem, tile_read.at(m - 3))
                        split_product(pe, bank(m % 4), n_k, src, tile_ready, m + 1)

                weight_programs(block, act=False, before=before)

                @block.scalar
                def _(act):
                    if before is not None:
                        wts.round_high(act, S, u0 + 1)
                        before.act(act)
                    for m in range(KD):
                        wts.round_high(act, S, (block0 + (m + 1) * n_k) // UNIT + SPLIT)
                        for t in () if sums is None or m == 0 else (0, 1) if m == 1 else (m,):
                            if centre and t == 0:
                                act.wait_ge(norm_dve.sem, norm_dve.at(dve0 + 1))
                            else:
                                act.wait_ge(tile_read.sem, tile_read.at(t + 1))
                            if t >= 2:
                                act.wait_ge(norm_dve.sem, squares_added(t - 2))
                            S.activation(w[:, SQ + t % 2, :], out(t), ACT.Square).then_inc(norm_act.sem, 1)

                @block.vector
                def _(dve):
                    def add_square(k):
                        dve.wait_ge(norm_act.sem, norm_act.at(act0 + k + 1))
                        a = w[:, SQ if k == 1 else SQ_SUM, :]
                        V.tensor_tensor(w[:, SQ_SUM, :], a, w[:, SQ + k % 2, :], ALU.add).then_inc(norm_dve.sem, 1)
                        dve.wait_ge(norm_dve.sem, squares_added(k))

                    if centre:
                        dve_chain.link(dve, V.memset(w[:, NEG_MEAN, 0:P], -1.0 / P))
                    if before is not None:
                        before.dve(dve)
                    for m in range(KD):
                        if centre and m >= 1:
                            dve_chain.link(dve, V.scalar_tensor_tensor(xt(m), xt(m), ALPHA, bank(FACTOR), ALU.mult,
                                                                       ALU.add))
                        if sums is not None and m >= 2:
                            add_square(m - 1)
                        dve.wait_ge(tile_ready.sem, tile_ready.at(m + 1))
                        if mode == "residual" and m == 0:
                            ins = V.scalar_tensor_tensor(xt(m), xt(m), ALPHA, bank(m % 4), ALU.mult, ALU.add)
                        elif mode == "copy":
                            ins = V.tensor_copy(out(m), bank(m % 4))
                        else:
                            ins = V.tensor_tensor(out(m), out(m), bank(m % 4), ALU.add)
                        ins.then_inc(tile_read.sem, 1)
                        if centre and m == 0:
                            dve.wait_ge(norm_pe.sem, norm_pe.at(pe0 + 1))
                            V.tensor_tensor(xt(0), xt(0), bank(FACTOR), ALU.add).then_inc(norm_dve.sem, 1)
                        if centre and 1 <= m < KD - 1:
                            dve.wait_ge(tile_read.sem, tile_read.at(m + 1))
                            if m == 1:
                                dve.wait_ge(norm_dve.sem, norm_dve.at(dve0 + 1))
                            dve_chain.link(dve, V.tensor_tensor(w[:, X_SUM, :], xt(0) if m == 1 else w[:, X_SUM, :],
                                                                xt(m), ALU.add))
            tile_ready.close(KD)
            tile_read.close(KD)
            if sums is not None:
                norm_act.close(KD)
                norm_dve.close(KD - 2 + shift)
            if centre:
                norm_pe.close(1)
            if before is not None:
                before.close()

        def stage_relu2_up(before=None):
            n_tiles = FF1 // 2
            RL, SQ = 32, 34
            u0 = wts.block // UNIT
            with nc.Block() as block:
                @block.tensor
                def _(pe):
                    product(pe, n_tiles, KD, of(xs), before)

                weight_programs(block, act=False, before=before)

                @block.scalar
                def _(act):
                    def high(m):
                        act.wait_ge(dve_out.sem, dve_out.at(m + 1))
                        S.activation(hidden1[:, 0, m, :], w[:, SQ + m % 2, :], ACT.Copy).then_inc(high_out.sem, 1)

                    if before is not None:
                        wts.round_high(act, S, u0 + SPLIT)
                        before.act(act)
                    for m in range(n_tiles):
                        wts.round_high(act, S, u0 + m + SPLIT)
                        act.wait_ge(tile_ready.sem, tile_ready.at(m + 1))
                        if m >= 2:
                            act.wait_ge(dve_out.sem, dve_out.at(m - 1))
                        S.activation(w[:, RL + m % 2, :], bank(m % 4), ACT.Relu).then_inc(tile_read.sem, 1)
                        high(m)

                @block.vector
                def _(dve):
                    if before is not None:
                        before.dve(dve)
                    for m in range(n_tiles):
                        r, q = w[:, RL + m % 2, :], w[:, SQ + m % 2, :]
                        dve.wait_ge(tile_read.sem, tile_read.at(m + 1))
                        V.tensor_tensor(q, r, r, ALU.mult).then_inc(dve_out.sem, 1)
                        dve.wait_ge(high_out.sem, high_out.at(m + 1))
                        dve_chain.link(dve, V.tensor_tensor(hidden1[:, 1, m, :], q,
                                                            hidden1[:, 0, m, :].bitcast(F32), ALU.subtract))
            tile_ready.close(n_tiles)
            tile_read.close(n_tiles)
            dve_out.close(n_tiles)
            high_out.close(n_tiles)
            if before is not None:
                before.close()

        ROWS = 28
        ML_PARTS, FORGET_PARTS = ROWS + 4, ROWS + 5
        HM, HF2 = 0, 16

        def stage_even_in():
            scale = {0: float(P) ** -0.5, 4: HD ** -0.5}
            u0 = wts.block // UNIT
            before = post_ffn()
            GATES = 36
            rows = ((0, 4, "ev_bi"), (4, 4, "ev_bf"), (8, 8, "ev_bff"))

            def row(i, n=8):
                return w[0:n, ROWS + i, :]

            def gates_pe(pe, m):
                if m == 1:
                    for k in range(KD):
                        ins = TE.matmul(ps[0:16, 4, :], v("ev_gates", 16 * k, 16), xt(k), start=(k == 0),
                                        stop=(k == KD - 1))
                    ins.then_inc(side_pe.sem, 1)
                elif m == 3:
                    pe.wait_ge(side_dve.sem, side_dve.at(1))
                    for j, (first, n, _) in enumerate(rows):
                        ins = TE.matmul(ps[0:n, 4 + j, :], c("ident", first, n, rows=16), w[0:16, GATES, :],
                                        start=True, stop=True)
                    ins.then_inc(side_pe.sem, 1)
                elif m == 14:
                    pe.wait_ge(side_dve.sem, side_dve.at(4))
                    for i in range(NT):
                        ins = TE.matmul(bank(7, 4 * i, 4), w[0:4, ROWS + 1, tok(0, i)], c("ident", 0, 4, rows=4),
                                        start=True, stop=True)
                    ins.then_inc(side_pe.sem, 1)

            def gates_act(act, m):
                if m == 6:
                    for j, n in ((1, 4), (2, 8)):
                        tmp = row(j + 3, n)
                        act.wait_ge(side_dve.sem, side_dve.at(j + 1))
                        act_chain.link(act, S.activation(tmp, tmp, ACT.Exp, scale=-1.0))
                        S.activation(tmp, tmp, ACT.Ln, bias=ones[0:n, 0:1]).then_inc(side_act.sem, 1)

            def gates_dve(dve, m):
                if m == 2:
                    dve.wait_ge(side_pe.sem, side_pe.at(1))
                    V.tensor_copy(w[0:16, GATES, :], ps[0:16, 4, :]).then_inc(side_dve.sem, 1)
                elif m == 4:
                    dve.wait_ge(side_pe.sem, side_pe.at(2))
                    for j, (_, n, b) in enumerate(rows):
                        dve_chain.link(dve, V.tensor_scalar(row(j, n), ps[0:n, 4 + j, :], v(b, rows=n), None, ALU.add))
                    for j, n in ((1, 4), (2, 8)):
                        dve_chain.link(dve, V.tensor_scalar(row(j + 3, n), row(j, n), -1.0, None, ALU.mult))
                        V.tensor_tensor(row(j + 3, n), row(j, n), row(j + 3, n), ALU.max).then_inc(side_dve.sem, 1)
                elif m in (8, 9):
                    j, n = m - 7, (4, 8)[m - 8]
                    z, tmp, out = row(j, n), row(j + 3, n), row(j + 5, n)
                    dve.wait_ge(side_act.sem, side_act.at(j))
                    dve_chain.link(dve, V.tensor_scalar(out, z, 0.0, None, ALU.min))
                    dve_chain.link(dve, V.tensor_tensor(out, out, tmp, ALU.subtract))
                    dve_chain.link(dve, V.tensor_tensor_scan(z, ones[0:n, :], out, 0.0, ALU.mult, ALU.add))
                elif m == 10:
                    V.tensor_tensor(row(0, 4), row(0, 4), row(1, 4), ALU.subtract).then_inc(side_dve.sem, 1)
                    dve_chain.link(dve, V.tensor_scalar(row(3), row(2), -1.0, None, ALU.mult))
                elif m == 11:
                    dve_chain.link(dve, V.memset(w[:, ML_PARTS:ML_PARTS + 2, :], 0.0))
                    dve.wait_ge(side_dve.sem, side_dve.at(4))
                elif m in (12, 14, 16, 18):
                    n, first, tile, j = {12: (4, ROWS + 1, ML_PARTS, 0), 14: (4, ROWS, ML_PARTS, 1),
                                         16: (8, ROWS + 2, FORGET_PARTS, 0), 18: (8, ROWS + 3, FORGET_PARTS, 1)}[m]
                    split_rows(dve, w[0:n, first, :], n, tile, j, ROWS + 6, ROWS + 7)
                elif m == 20:
                    dve.wait_ge(side_pe.sem, side_pe.at(3))
                    V.tensor_copy(col[:, 16:32], bank(7, 0, 16))

            with nc.Block() as block:
                @block.tensor
                def _(pe):
                    product(pe, 28, KD, of(xs), before, gates_pe)

                weight_programs(block, act=False, before=before)

                @block.vector
                def _(dve):
                    before.dve(dve)
                    for m in range(28):
                        dve.wait_ge(tile_ready.sem, tile_ready.at(m + 1))
                        V.tensor_scalar(w[:, m, :], bank(m % 4), v("ev_b", m), scale.get(m // 4, 1.0), ALU.add,
                                        ALU.mult).then_inc(tile_read.sem, 1)
                        gates_dve(dve, m)

                @block.scalar
                def _(act):
                    wts.round_high(act, S, u0 + SPLIT)
                    before.act(act)
                    for m in range(28):
                        wts.round_high(act, S, u0 + m + SPLIT)
                        gates_act(act, m)
                        if m in (19, 20, 21, 22):
                            act.wait_ge(tile_read.sem, tile_read.at(m - 2))
                            o = w[:, m - 7, :]
                            S.activation(o, o, ACT.Sigmoid)
            before.close()
            tile_ready.close(28)
            tile_read.close(28)
            side_pe.close(3)
            side_act.close(2)
            side_dve.close(4)

        def stage_conv_ffn_up(layer):
            y0 = 2 * FF2
            u0 = wts.block // UNIT
            before = layer_norm("ln1", layer)
            with nc.Block() as block:
                @block.tensor
                def _(pe):
                    product(pe, 2 * FF2, KD, of(xs), before)

                weight_programs(block, act=False, before=before)

                def taps(m):
                    ch = layer * 132 + (m % 2) * FF2 + m // 2
                    return [v("ffn_w", ch + 44 * i) for i in range(3)]

                @block.scalar
                def _(act):
                    def gate(j):
                        act.wait_ge(tile_read.sem, tile_read.at(2 * j + 2))
                        S.activation(w[:, y0 + 4 + j % 2, :], w[:, y0 + (2 * j + 1) % 4, :], ACT.Sigmoid
                                     ).then_inc(act_out2.sem, 1)
                        act.wait_ge(dve_out.sem, dve_out.at(j + 1))
                        S.activation(hidden2[:, 0, j, :], w[:, y0 + 2 * j % 4, :], ACT.Copy).then_inc(high_out.sem, 1)

                    wts.round_high(act, S, u0 + SPLIT)
                    before.act(act)
                    for m in range(2 * FF2):
                        wts.round_high(act, S, u0 + m + SPLIT)
                        act.wait_ge(tile_ready.sem, tile_ready.at(m + 1))
                        if m >= 4:
                            act.wait_ge(dve_out2.sem, dve_out2.at((m - 4) // 2 + 1))
                        S.activation(w[:, y0 + m % 4, :], bank(m % 4), ACT.Identity, scale=taps(m)[2],
                                     bias=v("ffn_b", layer * 44 + (m % 2) * FF2 + m // 2)).then_inc(act_out.sem, 1)
                        if m % 2 == 0 and m >= 2:
                            gate(m // 2 - 1)
                    gate(FF2 - 1)

                @block.vector
                def _(dve):
                    def conv(m):
                        y, b = w[:, y0 + m % 4, :], bank(m % 4)
                        dve.wait_ge(act_out.sem, act_out.at(m + 1))
                        dve_chain.link(dve, V.scalar_tensor_tensor(y[:, 1:T], b[:, 0:T - 1], taps(m)[1], y[:, 1:T],
                                                                   ALU.mult, ALU.add))
                        V.scalar_tensor_tensor(y[:, 2:T], b[:, 0:T - 2], taps(m)[0], y[:, 2:T], ALU.mult,
                                               ALU.add).then_inc(tile_read.sem, 1)

                    def join(j):
                        act_gate = w[:, y0 + 4 + j % 2, :]
                        value = w[:, y0 + 2 * j % 4, :]
                        dve.wait_ge(act_out2.sem, act_out2.at(j + 1))
                        dve_chain.link(dve, V.tensor_tensor(act_gate, act_gate, w[:, y0 + (2 * j + 1) % 4, :], ALU.mult))
                        V.tensor_tensor(value, act_gate, value, ALU.mult).then_inc(dve_out.sem, 1)
                        dve.wait_ge(high_out.sem, high_out.at(j + 1))
                        V.tensor_tensor(hidden2[:, 1, j, :], value, hidden2[:, 0, j, :].bitcast(F32),
                                        ALU.subtract).then_inc(dve_out2.sem, 1)

                    before.dve(dve)
                    for m in range(2 * FF2):
                        conv(m)
                        if m % 2 == 0 and m >= 2:
                            join(m // 2 - 1)
                    join(FF2 - 1)
            before.close()
            tile_ready.close(2 * FF2)
            tile_read.close(2 * FF2)
            act_out.close(2 * FF2)
            act_out2.close(FF2)
            dve_out.close(FF2)
            high_out.close(FF2)
            dve_out2.close(FF2)

        ZG, XS, BM, CMM, PL = 0, 4, 8, 10, 12
        ROWS2, SSD_PARTS = 40, 44
        XTK, YS, PO = 16, 20, 24

        def stage_odd_in():
            y0 = 46
            u0 = wts.block // UNIT
            before = layer_norm("ln2", 0)
            dt, tmp, acs, ncs = (w[0:8, ROWS2 + i, :] for i in range(4))
            decay = col[0:8, 12:13]

            def dt_pe(pe, m):
                if m == 1:
                    for k in range(KD):
                        ins = TE.matmul(ps[0:8, 4, :], v("od_dt", 8 * k, 8), xt(k), start=(k == 0), stop=(k == KD - 1))
                    ins.then_inc(side_pe.sem, 1)
                elif m == 8:
                    pe.wait_ge(dve_out.sem, dve_out.at(4))
                    for g in range(4):
                        TE.matmul(bank(4 + g), v("pool_w", g * P, P), w[:, PO + g, :], start=True,
                                  stop=True).then_inc(pe_out.sem, 1)
                elif m == 12:
                    pe.wait_ge(side_dve.sem, side_dve.at(2))
                    pe.wait_ge(dve_out.sem, dve_out.at(8))
                    for i in range(NT):
                        ins = TE.matmul(bank(5, 8 * i, 8), w[0:8, ROWS2, tok(0, i)], c("ident", 0, 8, rows=8),
                                        start=True, stop=True)
                    ins.then_inc(side_pe.sem, 1)

            def dt_act(act, m):
                if m == 4:
                    act_chain.link(act, S.activation(decay, v("a_log", rows=8), ACT.Exp))
                    act.wait_ge(side_dve.sem, side_dve.at(1))
                    act_chain.link(act, S.activation(tmp, tmp, ACT.Exp, scale=-1.0))
                    S.activation(tmp, tmp, ACT.Ln, bias=ones[0:8, 0:1]).then_inc(side_act.sem, 1)

            def dt_dve(dve, m):
                if m == 3:
                    dve.wait_ge(side_pe.sem, side_pe.at(1))
                    dve_chain.link(dve, V.tensor_scalar(acs, ps[0:8, 4, :], v("dt_bias", rows=8), None, ALU.add))
                    dve_chain.link(dve, V.tensor_scalar(tmp, acs, -1.0, None, ALU.mult))
                    V.tensor_tensor(tmp, acs, tmp, ALU.max).then_inc(side_dve.sem, 1)
                elif m == 6:
                    dve.wait_ge(side_act.sem, side_act.at(1))
                    dve_chain.link(dve, V.tensor_scalar(dt, acs, 0.0, None, ALU.max))
                    dve_chain.link(dve, V.tensor_tensor(dt, dt, tmp, ALU.add))
                elif m == 8:
                    dve_chain.link(dve, V.tensor_scalar(tmp, dt, decay, -1.0, ALU.mult, ALU.mult))
                    V.tensor_tensor_scan(acs, ones[0:8, :], tmp, 0.0, ALU.mult, ALU.add).then_inc(side_dve.sem, 1)
                    dve.wait_ge(side_dve.sem, side_dve.at(2))
                    dve_chain.link(dve, V.tensor_scalar(ncs, acs, -1.0, None, ALU.mult))
                    dve_chain.link(dve, V.memset(w[:, SSD_PARTS, :], 0.0))
                elif m in (10, 12):
                    split_rows(dve, w[0:8, ROWS2 + 2 + (m - 10) // 2, :], 8, SSD_PARTS, (m - 10) // 2, ROWS2 + 5,
                               ROWS2 + 1)
                elif m == 15:
                    dve.wait_ge(side_pe.sem, side_pe.at(2))
                    V.tensor_copy(col[:, 16:48], bank(5, 0, 32))

            gated = [m for m in ODD_ORDER if m < 12]

            def pool_mean(dve, g):
                win, u = WINDOWS[g], w[:, PL + g, :]
                a, b = w[:, PO + g, :], w[:, 28 + g, :]
                src, s = u, 1
                while s < win:
                    dst = a if src is not a else b
                    V.tensor_copy(dst[:, 0:s], src[:, 0:s])
                    dve_chain.link(dve, V.tensor_tensor(dst[:, s:T], src[:, s:T], src[:, 0:T - s], ALU.add))
                    src, s = dst, 2 * s
                V.tensor_scalar(src[:, 16:T], src[:, 16:T], 1.0 / win, None, ALU.mult)
                dve_chain.link(dve, V.tensor_tensor(src[:, 0:16], src[:, 0:16], c("inv_count", 16 * g, 16), ALU.mult))
                V.tensor_tensor(a, src, u, ALU.subtract).then_inc(dve_out.sem, 1)

            def pool_out(dve):
                for g in range(4):
                    dve.wait_ge(pe_out.sem, pe_out.at(g + 1))
                    V.tensor_scalar(w[:, PO + g, :], bank(4 + g), v("pool_b", g), v("pool_scale", g), ALU.add,
                                    ALU.mult).then_inc(dve_out.sem, 1)

            with nc.Block() as block:
                @block.tensor
                def _(pe):
                    product(pe, 16, KD, of(xs), before, dt_pe)

                weight_programs(block, act=False, before=before)

                @block.scalar
                def _(act):
                    wts.round_high(act, S, u0 + SPLIT)
                    before.act(act)
                    for n, m in enumerate(ODD_ORDER):
                        wts.round_high(act, S, u0 + n + SPLIT)
                        dt_act(act, n)
                        if m >= 12:
                            continue
                        i = gated.index(m)
                        if m >= 4:
                            act.wait_ge(tile_ready.sem, tile_ready.at(n + 1))
                            S.activation(w[:, m, :], bank(n % 4), ACT.Identity, scale=v("conv_w", 24 + m - 4),
                                         bias=v("conv_b", m - 4)).then_inc(act_out.sem, 1)
                        act.wait_ge(tile_read.sem, tile_read.at(n + 1))
                        S.activation(w[:, y0 + i % 2, :], w[:, m, :], ACT.Sigmoid).then_inc(act_out2.sem, 1)
                    wts.round_high(act, S)

                @block.vector
                def _(dve):
                    before.dve(dve)
                    for n, m in enumerate(ODD_ORDER):
                        y, b = w[:, m, :], bank(n % 4)
                        dve.wait_ge(tile_ready.sem, tile_ready.at(n + 1))
                        if 4 <= m < 12:
                            dve.wait_ge(act_out.sem, act_out.at(m - 3))
                            for i, s in ((2, 1), (1, 2), (0, 3)):
                                ins = V.scalar_tensor_tensor(y[:, s:T], b[:, 0:T - s], v("conv_w", 8 * i + m - 4),
                                                             y[:, s:T], ALU.mult, ALU.add)
                                if i:
                                    dve_chain.link(dve, ins)
                        else:
                            ins = V.tensor_copy(y, b)
                        ins.then_inc(tile_read.sem, 1)
                        if m < 12:
                            i = gated.index(m)
                            dve.wait_ge(act_out2.sem, act_out2.at(i + 1))
                            dve_chain.link(dve, V.tensor_tensor(y, y, w[:, y0 + i % 2, :], ALU.mult))
                        else:
                            dve.wait_ge(tile_read.sem, tile_read.at(n + 1))
                            pool_mean(dve, m - 12)
                        dt_dve(dve, n)
                        if n == 10:
                            pool_out(dve)
            before.close()
            side_pe.close(2)
            side_act.close(1)
            side_dve.close(2)
            tile_ready.close(16)
            tile_read.close(16)
            act_out.close(8)
            act_out2.close(12)
            dve_out.close(8)
            pe_out.close(4)

        def stage_ssd():
            items = [(g, j, hh) for g in range(2) for j in range(NT) for hh in range(4)]
            n_items = len(items)
            e = [w[:, 46, :], w[:, 47, :]]
            m_ = [w[:, 48, :], w[:, 49, :]]
            with nc.Block() as block:
                @block.tensor
                def _(pe):
                    def decay(n):
                        g, j, hh = items[n]
                        a, wd = j * P, T - j * P
                        hd = 4 * g + hh
                        if hh == 0:
                            if n >= 8:
                                pe.wait_ge(dve_out.sem, dve_out.at(n - 4))
                            TE.matmul(bank((n // 4) % 2, 0, wd), w[:, BM + g, a:a + P], w[:, CMM + g, a:T],
                                      start=True, stop=True)
                        if n >= 2:
                            pe.wait_ge(act_out.sem, act_out.at(n - 1))
                        d = bank(2 + n % 2, 0, wd)
                        TE.matmul(d, one_hot(hd, P), row_parts(SSD_PARTS, 0)[:, a:T], start=True, stop=False)
                        TE.matmul(d, row_parts(SSD_PARTS, 1)[:, a:a + P], one_hot(hd, wd), start=False, stop=False)
                        TE.matmul(bank(2 + n % 2, 0, P), ident_h[:, :], diag_st_h[:, :], start=False,
                                  stop=True).then_inc(tile_ready.sem, 1)

                    def values(n):
                        g, j, hh = items[n]
                        hd = 4 * g + hh
                        pe.wait_ge(dve_out.sem, dve_out.at(n + 1))
                        TE.matmul(bank(4 + hd // 2, j * P, T - j * P, half(hd)), w[:, XTK + j, hd * HD:(hd + 1) * HD],
                                  m_[n % 2][:, 0:T - j * P], start=(j == 0), stop=(j == NT - 1)
                                  ).then_inc(pe_out.sem, 1)

                    decay(0)
                    for n in range(n_items):
                        if n + 1 < n_items:
                            decay(n + 1)
                        values(n)

                @block.scalar
                def _(act):
                    for n, (g, j, hh) in enumerate(items):
                        wd = T - j * P
                        act.wait_ge(tile_ready.sem, tile_ready.at(n + 1))
                        if n >= 2:
                            act.wait_ge(dve_out.sem, dve_out.at(n - 1))
                        S.activation(e[n % 2][:, 0:wd], bank(2 + n % 2, 0, wd), ACT.Exp).then_inc(act_out.sem, 1)

                @block.vector
                def _(dve):
                    for n, (g, j, hh) in enumerate(items):
                        wd = T - j * P
                        dve.wait_ge(act_out.sem, act_out.at(n + 1))
                        if n >= 2:
                            dve.wait_ge(pe_out.sem, pe_out.at(n - 1))
                        V.tensor_tensor(m_[n % 2][:, 0:wd], bank((n // 4) % 2, 0, wd), e[n % 2][:, 0:wd],
                                        ALU.mult).then_inc(dve_out.sem, 1)
                    dve.wait_ge(pe_out.sem, pe_out.at(n_items))
                    for t in range(4):
                        y = w[:, YS + t, :]
                        dve_chain.link(dve, V.scalar_tensor_tensor(y, w[:, XS + t, :], v("d_skip", t), bank(4 + t),
                                                                   ALU.mult, ALU.add))
                        dve_chain.link(dve, V.tensor_tensor(y, y, w[:, ZG + t, :], ALU.mult))
            tile_ready.close(n_items)
            pe_out.close(n_items)
            act_out.close(n_items)
            dve_out.close(n_items)

        def stage_last():
            last = layer_norm("ln2", 1, split=False)
            with nc.Block() as block:
                @block.tensor
                def _(pe):
                    last.pe(pe)

                @block.scalar
                def _(act):
                    last.act(act)

                @block.vector
                def _(dve):
                    last.dve(dve)

                @block.sync
                def _(sp):
                    for t in range(KD):
                        sp.wait_ge(norm_act.sem, norm_act.at(t + 2))
                        sp.dma_start(out_t[t * P:(t + 1) * P], x[:, t, :]).then_inc(dma_out.sem, 16)
                    sp.wait_ge(dma_out.sem, dma_out.at(16 * KD))
            last.close()
            dma_out.close(16 * KD)

        steps = [
            ("inputs", stage_inputs),
            ("qkv", stage_qkv),
            ("v_tok", lambda: to_token_major([(Q1 + 8, 28)])),
            ("band", lambda: attention("band", Q1, Q1 + 4, 28, YA, range(32, 42), bias0=20)),
            ("rwkv_in", stage_rwkv_in),
            ("rwkv_chunks", stage_rwkv_chunks),
            ("merge", stage_merge),
            ("w_out", lambda: stage_linear(KD, of(merged_split), "copy", wt(0), sums="squares")),
            ("up_a", lambda: stage_relu2_up(post_mix_pre_ffn())),
            ("down_a", lambda: stage_linear(FF1 // 2, of(hidden1), "copy", wt(36))),
            ("up_b", stage_relu2_up),
            ("down_b", lambda: stage_linear(FF1 // 2, of(hidden1), "add", wt(36), sums="squares")),
            ("even_in", stage_even_in),
            ("ml_tok", lambda: to_token_major([(8, 36), (24, 40)])),
            ("mlstm", lambda: attention("mlstm", 0, 4, 36, HM, (8, 9, 10, 11, 44, 45, 46), parts=ML_PARTS, gate0=12,
                                        f_cols=lambda i, hd: col[:, 16 + 4 * i + hd:17 + 4 * i + hd])),
            ("forget", lambda: attention("forget", 16, 20, 40, HF2, (4, 5, 6, 7, 8, 9, 10, 11), parts=FORGET_PARTS)),
            ("even_out", lambda: stage_linear(
                KD, of(even_split), "residual", sums="both",
                before=split_tiles(lambda t: w[:, t if t < 4 else HF2 + t - 4, :], even_split))),
            ("ffn_up_0", lambda: stage_conv_ffn_up(0)),
            ("ffn_down_0", lambda: stage_linear(FF2, of(hidden2), "residual", sums="both")),
            ("odd_in", stage_odd_in),
            ("x_tok", lambda: to_token_major([(XS, XTK)], scaled=lambda i: col[:, 16 + 8 * i:24 + 8 * i])),
            ("ssd", stage_ssd),
            ("odd_out", lambda: stage_linear(KD, of(odd_split), "residual", sums="both",
                                             before=ssm_norm())),
            ("ffn_up_1", lambda: stage_conv_ffn_up(1)),
            ("ffn_down_1", lambda: stage_linear(FF2, of(hidden2), "residual", sums="both")),
            ("last", stage_last),
        ]
        for _, run in steps:
            run()
        assert wts.block == n_units * UNIT, (wts.block, n_units * UNIT)


def blocks(m):
    k, n = m.shape
    return m.reshape(k // P, P, n // P, P).transpose(2, 0, 1, 3).reshape(-1, P, P)


def weight_stream(a):
    w_in, ev, od = a["w_in"][0], a["ev_w_in_2"][0], a["od_w_in_2"][0]
    gates = blocks(w_in[:, 3328:]).reshape(2, KD, KD, P, P)
    pa, pb = (blocks(a[n][0]).reshape(KD, KH, P, P) for n in ("proj_a", "proj_b"))
    head = blocks(w_in[:, :3328]).reshape(-1, KD, P, P)
    parts = [head[:12].reshape(-1, P, P), head[[12 + m for m in RWKV_ORDER]].reshape(-1, P, P)]
    for kind, m in merge_order():
        parts += [gates[0, m], gates[1, m]] if kind == "gate" else [pa[m], pb[m]]
    up, down, half = a["w_up"][0], a["w_down"][0], FF1 // 2 * P
    parts += [blocks(a["w_out"][0]), blocks(up[:, :half]), blocks(down[:half]), blocks(up[:, half:]),
              blocks(down[half:]), blocks(ev[:, 0:2048]), blocks(ev[:, 2056:3592]), blocks(a["ev_w_out_2"][0])]

    def ffn(layer):
        up = blocks(a["ffn_w_up_2"][layer]).reshape(2, FF2, KD, P, P).transpose(1, 0, 2, 3, 4)
        return [up.reshape(-1, P, P), blocks(a["ffn_w_down_2"][layer])]

    parts += ffn(0)
    odd = np.concatenate([blocks(od[:, 0:1536]), blocks(od[:, 1544:2056])]).reshape(-1, KD, P, P)
    parts += [odd[list(ODD_ORDER)].reshape(-1, P, P), blocks(a["od_w_out_2"][0])]
    parts += ffn(1)
    flat = np.concatenate(parts)
    return np.ascontiguousarray(flat.reshape(-1, UNIT, P, P).transpose(0, 2, 1, 3)).reshape(-1, P, UNIT * P)


def vector_array(a):
    cols, n = columns(VECTORS)
    out = np.zeros((P, n), np.float32)

    def put(name, m, rows=P):
        at, k = cols[name]
        out[0:rows, at:at + k] = m

    def tiled(m):
        return m.reshape(-1, P).T

    for name in ("pre_mix_g", "gate_bias", "shift_mu", "w0", "a0", "k_k", "k_a", "r_k", "ln_x_w", "ln_x_b",
                 "post_mix_g", "pre_ffn_g", "post_ffn_g"):
        put(name, tiled(a[name]))
    b = a["ev_b_in_2"][0]
    put("ev_b", tiled(np.concatenate([b[0:2048], b[2056:3592]])))
    put("ev_bi", b[2048:2052, None], 4)
    put("ev_bf", b[2052:2056, None], 4)
    put("ev_bff", b[3592:3600, None], 8)
    put("ml_norm", tiled(a["ev_ml_norm_2"]))
    put("conv_w", tiled(a["od_conv_w_2"]))
    put("conv_b", tiled(a["od_conv_b_2"]))
    put("dt_bias", a["od_dt_bias_2"][0][:, None], 8)
    put("a_log", a["od_a_log_2"][0][:, None], 8)
    put("d_skip", tiled(np.repeat(a["od_d_skip_2"][0], HD)))
    put("ssm_norm", tiled(a["od_ssm_norm_2"]))
    put("pool_b", tiled(a["od_pool_b_2"]))
    put("pool_scale", tiled(a["od_pool_scale_2"]))
    put("ffn_w", tiled(a["ffn_conv_w_2"]))
    put("ffn_b", tiled(a["ffn_conv_b_2"]))
    for n1 in ("ln1_g", "ln1_b", "ln2_g", "ln2_b"):
        put(n1, tiled(a[n1 + "_2"]))
    put("w2a2", np.concatenate([a["w2"][0], a["a2"][0]]))
    put("g2", a["g2"][0])
    ev, od = a["ev_w_in_2"][0], a["od_w_in_2"][0]

    def narrow(m):
        return m.reshape(KD, P, -1).transpose(1, 0, 2).reshape(P, -1)

    put("ev_gates", narrow(np.concatenate([ev[:, 2048:2056], ev[:, 3592:3600]], axis=1)))
    put("od_dt", narrow(od[:, 1536:1544]))
    put("pool_w", a["od_pool_w_2"][0].transpose(1, 0, 2).reshape(P, -1))
    return out


def constant_array():
    cols, n = columns(CONSTANTS)
    out = np.zeros((P, n), np.float32)
    i = np.arange(P)
    row, colm = i[:, None], i[None, :]

    def put(name, m):
        at, k = cols[name]
        out[:, at:at + k] = m

    put("ident", row == colm)
    put("flip", row + colm == P - 1)
    put("same_head", row // HD == colm // HD)
    levels = []
    for l in range(LEVELS):
        s = 1 << l
        levels.append((row // (2 * s) == colm // (2 * s)) & (row % (2 * s) >= s) & (colm % (2 * s) < s))
    put("levels", np.concatenate(levels, axis=1))
    put("level0_t", levels[0].T)
    put("mask4", np.concatenate([row < colm, row <= colm, row < colm, row <= colm], axis=1))
    put("diag_qk", np.where(colm > row, NEG, 0.0))
    put("diag_st", np.where(colm < row, NEG, 0.0))
    t = np.arange(16)
    put("inv_count", np.concatenate([1.0 / np.minimum(t + 1, win) for win in WINDOWS])[None])
    put("eps", np.array([[RMS_EPS, LN_EPS, GN_EPS]]))
    return out


def kernel(**inputs):
    import concourse.bacc as bacc
    from concourse.bass_utils import run_bass_kernel_spmd

    a = {k: np.asarray(m) for k, m in inputs.items()}
    arrays = {
        "x_t": np.ascontiguousarray(a["x"][0].T),
        "vectors": vector_array(a),
        "constants": constant_array(),
        "rel_rev": np.ascontiguousarray(a["rel_bias"][0][:, ::-1]),
        "stream": weight_stream(a),
    }
    nc = bacc.Bacc("TRN2", target_bir_lowering=False, num_devices=1)
    args = {k: nc.dram_tensor(k, m.shape, mybir.dt.from_np(m.dtype), kind="ExternalInput").ap()
            for k, m in arrays.items()}
    line = nc.dram_tensor("bias_line", (HEADS, DIAG_PAD), F32, kind="Internal").ap()
    out = nc.dram_tensor("out_t", (D, T), F32, kind="ExternalOutput").ap()
    network(nc, **args, bias_line=line, out_t=out)
    r = run_bass_kernel_spmd(nc, [arrays], core_ids=[0])
    return np.ascontiguousarray(r.results[0]["out_t"].T)[None]
```
